# Optimizing a Trainium2 kernel written in Bass

```python
import math
import jax, jax.numpy as jnp
from jax import lax
import numpy as np
import jax
import jax.numpy as jnp

D_MODEL = 1024
BATCH = 1
SEQ = 256
DEPTH = 1

SSD_INNER = D_MODEL
SSD_HEAD_DIM = 64
SSD_HEADS = SSD_INNER // SSD_HEAD_DIM
SSD_GROUPS = 4
SSD_STATE = 128
SSD_CHUNK = 128
SSD_CONV = 4
SSD_BC = SSD_GROUPS * SSD_STATE
SSD_CONV_CH = SSD_INNER + 2 * SSD_BC
DT_MIN = 0.001
DT_MAX = 0.1
ATT_HEAD_DIM = 64
ATT_HEADS = D_MODEL // 128
ATT_INNER = ATT_HEADS * ATT_HEAD_DIM
Q_BLOCK = 128
N_GROUPS = 4
EXPERTS_PER_GROUP = 4
N_EXPERTS = N_GROUPS * EXPERTS_PER_GROUP
TOP_K = 2
EXPERT_FF = D_MODEL // 2
IN_SIZES = (SSD_INNER, SSD_CONV_CH, SSD_HEADS, ATT_INNER, ATT_INNER, ATT_INNER, ATT_HEADS, D_MODEL, D_MODEL)
N_IN = sum(IN_SIZES)
N_MOD = 6
DEEPNORM_ALPHA = (2 * DEPTH) ** 0.25
DEEPNORM_BETA = (8 * DEPTH) ** -0.25
LN_EPS = 1e-5


def layer_norm(x, gain=None, bias=None):
    xf = x.astype(jnp.float32)
    mu = jnp.mean(xf, axis=-1, keepdims=True)
    var = jnp.mean(jnp.square(xf - mu), axis=-1, keepdims=True)
    y = ((xf - mu) * lax.rsqrt(var + LN_EPS)).astype(x.dtype)
    if gain is None:
        return y
    return y * gain + bias

def gated_rms_norm(y, z, w):
    g = (y * jax.nn.silu(z)).astype(jnp.float32)
    g = g * lax.rsqrt(jnp.mean(jnp.square(g), axis=-1, keepdims=True) + LN_EPS)
    return g.astype(y.dtype) * w

def causal_depthwise_conv(u, w, bias):
    k_width, ch = w.shape
    out = lax.conv_general_dilated(
        u, w[:, None, :].astype(u.dtype), window_strides=(1,),
        padding=((k_width - 1, 0),), dimension_numbers=('NWC', 'WIO', 'NWC'),
        feature_group_count=ch)
    return out + bias

def ssd_chunked(xh, dt, a_log, bmat, cmat):
    b, s, h, p = xh.shape
    g, n = bmat.shape[-2:]
    r = h // g
    L = SSD_CHUNK
    nc = s // L
    f32 = jnp.float32
    A = -jnp.exp(a_log.astype(f32))
    a = (dt * A).reshape(b, nc, L, g, r)
    xdt = (xh.astype(f32) * dt[..., None]).reshape(b, nc, L, g, r, p)
    bc = bmat.astype(f32).reshape(b, nc, L, g, n)
    cc = cmat.astype(f32).reshape(b, nc, L, g, n)
    a_cs = jnp.cumsum(a, axis=2)
    causal = jnp.tril(jnp.ones((L, L), dtype=bool))[None, None, :, :, None, None]
    seg = a_cs[:, :, :, None] - a_cs[:, :, None, :]
    decay = jnp.exp(jnp.where(causal, seg, -jnp.inf))
    cb = jnp.einsum('bclgn,bcsgn->bclsg', cc, bc)
    y_diag = jnp.einsum('bclsgr,bcsgrp->bclgrp', cb[..., None] * decay, xdt)
    to_end = jnp.exp(a_cs[:, :, -1:] - a_cs)
    states = jnp.einsum('bclgn,bclgrp->bcgrpn', bc, xdt * to_end[..., None])
    chunk_decay = jnp.exp(a_cs[:, :, -1])

    def carry_state(state, inp):
        st, dec = inp
        return state * dec[..., None, None] + st, state

    _, prev = lax.scan(carry_state, jnp.zeros_like(states[:, 0]),
                       (jnp.moveaxis(states, 1, 0), jnp.moveaxis(chunk_decay, 1, 0)))
    prev = jnp.moveaxis(prev, 0, 1)
    y_off = jnp.einsum('bclgn,bcgrpn->bclgrp', cc, prev) * jnp.exp(a_cs)[..., None]
    return (y_diag + y_off).reshape(b, s, h, p)

def forgetting_attention(q, k, v, log_f):
    b, s, h, d = q.shape
    fcum = jnp.cumsum(log_f.astype(jnp.float32), axis=1).transpose(0, 2, 1)
    scale = d ** -0.5
    q_pos = jnp.arange(Q_BLOCK)
    outs = []
    for i in range(s // Q_BLOCK):
        lo, hi = i * Q_BLOCK, (i + 1) * Q_BLOCK
        logits = jnp.einsum('bqhd,bkhd->bhqk', q[:, lo:hi], k[:, :hi]).astype(jnp.float32) * scale
        logits = logits + fcum[:, :, lo:hi, None] - fcum[:, :, None, :hi]
        causal = jnp.arange(hi)[None, :] <= (lo + q_pos)[:, None]
        logits = jnp.where(causal, logits, -jnp.inf)
        probs = jax.nn.softmax(logits, axis=-1).astype(v.dtype)
        outs.append(jnp.einsum('bhqk,bkhd->bqhd', probs, v[:, :hi]))
    return jnp.concatenate(outs, axis=1)

def hybrid_mixer(h, w_in, conv_w, conv_b, dt_bias, a_log, d_skip, ssd_norm_w, forget_b,
                 w_ssd_o, w_att_o, w_o):
    b, s, _ = h.shape
    split_points = np.cumsum(IN_SIZES)[:-1].tolist()
    proj = h @ w_in
    z, xbc, dt_raw, q, k, v, f_raw, g_ssd, g_att = jnp.split(proj, split_points, axis=-1)
    xbc = jax.nn.silu(causal_depthwise_conv(xbc, conv_w, conv_b))
    xs, bm, cm = jnp.split(xbc, [SSD_INNER, SSD_INNER + SSD_BC], axis=-1)
    dt = jax.nn.softplus((dt_raw + dt_bias).astype(jnp.float32))
    xh = xs.reshape(b, s, SSD_HEADS, SSD_HEAD_DIM)
    y = ssd_chunked(xh, dt, a_log,
                    bm.reshape(b, s, SSD_GROUPS, SSD_STATE),
                    cm.reshape(b, s, SSD_GROUPS, SSD_STATE))
    y = (y + d_skip[:, None] * xh).astype(h.dtype).reshape(b, s, SSD_INNER)
    y_ssd = gated_rms_norm(y, z, ssd_norm_w) @ w_ssd_o
    log_f = jax.nn.log_sigmoid((f_raw + forget_b).astype(jnp.float32))
    o = forgetting_attention(q.reshape(b, s, ATT_HEADS, ATT_HEAD_DIM),
                             k.reshape(b, s, ATT_HEADS, ATT_HEAD_DIM),
                             v.reshape(b, s, ATT_HEADS, ATT_HEAD_DIM), log_f)
    y_att = o.reshape(b, s, ATT_INNER) @ w_att_o
    merged = jax.nn.sigmoid(g_ssd) * y_ssd + jax.nn.sigmoid(g_att) * y_att
    return merged @ w_o

def hierarchical_moe(h, w_rg, b_rg, w_re, b_re, w_gate, w_up, w_down):
    b, s, d = h.shape
    t = h.reshape(-1, d)
    f32 = jnp.float32
    g_prob = jax.nn.softmax((t @ w_rg + b_rg).astype(f32), axis=-1)
    g_p, g_idx = lax.top_k(g_prob, 1)
    onehot_g = jax.nn.one_hot(g_idx[:, 0], N_GROUPS, dtype=f32)
    e_logits = (t @ w_re + b_re).astype(f32).reshape(-1, N_GROUPS, EXPERTS_PER_GROUP)
    e_in = jnp.einsum('tg,tge->te', onehot_g, e_logits)
    top_l, top_i = lax.top_k(e_in, TOP_K)
    w_k = jax.nn.softmax(top_l, axis=-1) * g_p
    w_group = jnp.einsum('tk,tke->te', w_k, jax.nn.one_hot(top_i, EXPERTS_PER_GROUP, dtype=f32))
    gates = (onehot_g[:, :, None] * w_group[:, None, :]).reshape(-1, N_EXPERTS).astype(t.dtype)
    out = jnp.zeros_like(t)
    for e in range(N_EXPERTS):
        hid = jax.nn.silu(t @ w_gate[e]) * (t @ w_up[e])
        out = out + gates[:, e:e + 1] * (hid @ w_down[e])
    return out.reshape(b, s, d)

def first_inputs(seed: int = 0) -> dict:
    key = jax.random.key(seed)
    ks = iter(jax.random.split(key, 32))
    f32 = jnp.float32

    def nrm(shape, scale):
        return jax.random.normal(next(ks), shape, f32) * scale

    offs = np.concatenate([[0], np.cumsum(IN_SIZES)])
    col_scale = np.ones((N_IN,), np.float32)
    col_scale[offs[1]:offs[1] + SSD_INNER] = DEEPNORM_BETA
    col_scale[offs[5]:offs[6]] = DEEPNORM_BETA
    dt0 = jnp.exp(jax.random.uniform(next(ks), (DEPTH, SSD_HEADS), f32)
                  * (math.log(DT_MAX) - math.log(DT_MIN)) + math.log(DT_MIN))
    return {
        'x': nrm((BATCH, SEQ, D_MODEL), 1.0),
        'c': nrm((BATCH, D_MODEL), 1.0),
        'w_mod': nrm((DEPTH, D_MODEL, N_MOD * D_MODEL), 0.5 * D_MODEL ** -0.5),
        'b_mod': nrm((DEPTH, N_MOD * D_MODEL), 0.02),
        'w_in': nrm((DEPTH, D_MODEL, N_IN), D_MODEL ** -0.5) * jnp.asarray(col_scale),
        'conv_w': nrm((DEPTH, SSD_CONV, SSD_CONV_CH), SSD_CONV ** -0.5),
        'conv_b': nrm((DEPTH, SSD_CONV_CH), 0.02),
        'dt_bias': dt0 + jnp.log(-jnp.expm1(-dt0)),
        'a_log': jnp.log(jax.random.uniform(next(ks), (DEPTH, SSD_HEADS), f32, minval=1.0, maxval=16.0)),
        'd_skip': 1.0 + nrm((DEPTH, SSD_HEADS), 0.1),
        'ssd_norm_w': 1.0 + nrm((DEPTH, SSD_INNER), 0.05),
        'forget_b': jax.random.uniform(next(ks), (DEPTH, ATT_HEADS), f32, minval=1.0, maxval=4.0),
        'w_ssd_o': nrm((DEPTH, SSD_INNER, D_MODEL), DEEPNORM_BETA * SSD_INNER ** -0.5),
        'w_att_o': nrm((DEPTH, ATT_INNER, D_MODEL), DEEPNORM_BETA * ATT_INNER ** -0.5),
        'w_o': nrm((DEPTH, D_MODEL, D_MODEL), DEEPNORM_BETA * D_MODEL ** -0.5),
        'ln1_g': 1.0 + nrm((DEPTH, D_MODEL), 0.05),
        'ln1_b': nrm((DEPTH, D_MODEL), 0.02),
        'w_router_group': nrm((DEPTH, D_MODEL, N_GROUPS), D_MODEL ** -0.5),
        'b_router_group': nrm((DEPTH, N_GROUPS), 0.01),
        'w_router_expert': nrm((DEPTH, D_MODEL, N_EXPERTS), D_MODEL ** -0.5),
        'b_router_expert': nrm((DEPTH, N_EXPERTS), 0.01),
        'w_gate': nrm((DEPTH, N_EXPERTS, D_MODEL, EXPERT_FF), D_MODEL ** -0.5),
        'w_up': nrm((DEPTH, N_EXPERTS, D_MODEL, EXPERT_FF), DEEPNORM_BETA * D_MODEL ** -0.5),
        'w_down': nrm((DEPTH, N_EXPERTS, EXPERT_FF, D_MODEL), DEEPNORM_BETA * EXPERT_FF ** -0.5),
        'ln2_g': 1.0 + nrm((DEPTH, D_MODEL), 0.05),
        'ln2_b': nrm((DEPTH, D_MODEL), 0.02),
    }

def first_block(x, c, w_mod, b_mod, w_in, conv_w, conv_b, dt_bias, a_log, d_skip, ssd_norm_w,
              forget_b, w_ssd_o, w_att_o, w_o, ln1_g, ln1_b, w_router_group, b_router_group,
              w_router_expert, b_router_expert, w_gate, w_up, w_down, ln2_g, ln2_b):
    c_act = jax.nn.silu(c)
    for l in range(DEPTH):
        mod = (c_act @ w_mod[l] + b_mod[l])[:, None, :]
        sh1, sc1, gt1, sh2, sc2, gt2 = jnp.split(mod, N_MOD, axis=-1)
        h = layer_norm(x) * (1.0 + sc1) + sh1
        y = hybrid_mixer(h, w_in[l], conv_w[l], conv_b[l], dt_bias[l], a_log[l], d_skip[l],
                         ssd_norm_w[l], forget_b[l], w_ssd_o[l], w_att_o[l], w_o[l])
        x = layer_norm(DEEPNORM_ALPHA * x + (1.0 + gt1) * y, ln1_g[l], ln1_b[l])
        h = layer_norm(x) * (1.0 + sc2) + sh2
        y = hierarchical_moe(h, w_router_group[l], b_router_group[l], w_router_expert[l],
                             b_router_expert[l], w_gate[l], w_up[l], w_down[l])
        x = layer_norm(DEEPNORM_ALPHA * x + (1.0 + gt2) * y, ln2_g[l], ln2_b[l])
    return x


DEPTH_2 = 2

HEAD_DIM = 64
ROPE_THETA = 10000.0
NORM_EPS = 1e-6
QUERY_BLOCK = 128
N_MEM = 256

SWA_HEADS = 8
SWA_KV_HEADS = 2
SWA_WINDOW = 128

NSA_HEADS = 8
NSA_KV_GROUPS = 2
NSA_CMP_BLOCK = 32
NSA_CMP_STRIDE = 16
NSA_SEL_BLOCK = 64
NSA_N_SEL = 16
NSA_WINDOW = 512
NSA_FORCE_BONUS = 1e4

MLA_HEADS = 8
MLA_Q_RANK = 384
MLA_KV_RANK = 256
MLA_NOPE_DIM = 64
MLA_ROPE_DIM = 32
MLA_V_DIM = 64

XATTN_HEADS = 4
XATTN_HEAD_DIM = 128

D_FF = -(-8 * D_MODEL // (3 * 256)) * 256

N_BRANCH = 3
IN_SPLITS = (
    SWA_HEADS * HEAD_DIM, SWA_KV_HEADS * HEAD_DIM, SWA_KV_HEADS * HEAD_DIM,
    NSA_HEADS * HEAD_DIM,
    NSA_KV_GROUPS * HEAD_DIM, NSA_KV_GROUPS * HEAD_DIM,
    NSA_KV_GROUPS * HEAD_DIM, NSA_KV_GROUPS * HEAD_DIM,
    NSA_KV_GROUPS * HEAD_DIM, NSA_KV_GROUPS * HEAD_DIM,
    NSA_HEADS * 3,
    MLA_Q_RANK, MLA_KV_RANK, MLA_ROPE_DIM,
    N_BRANCH * D_MODEL,
)
D_IN = sum(IN_SPLITS)


def rmsnorm(x, g):
    x32 = x.astype(jnp.float32)
    y = x32 * lax.rsqrt(jnp.mean(x32 * x32, axis=-1, keepdims=True) + NORM_EPS)
    return (y * g.astype(jnp.float32)).astype(x.dtype)

def rope(x, pos):
    half = x.shape[-1] // 2
    inv_freq = ROPE_THETA ** (-jnp.arange(half, dtype=jnp.float32) / half)
    ang = pos.astype(jnp.float32)[..., None] * inv_freq
    cos, sin = jnp.cos(ang)[:, :, None, :], jnp.sin(ang)[:, :, None, :]
    x1, x2 = jnp.split(x.astype(jnp.float32), 2, axis=-1)
    return jnp.concatenate([x1 * cos - x2 * sin, x2 * cos + x1 * sin], axis=-1).astype(x.dtype)

def masked_probs(s, mask, sink=None):
    s = jnp.where(mask, s, -jnp.inf)
    m = jnp.max(s, axis=-1, keepdims=True)
    if sink is not None:
        m = jnp.maximum(m, sink)
    m = jnp.where(jnp.isfinite(m), m, 0.0)
    e = jnp.exp(s - m)
    denom = jnp.sum(e, axis=-1, keepdims=True)
    if sink is not None:
        denom = denom + jnp.exp(sink - m)
    return e / jnp.where(denom > 0, denom, 1.0)

def slice_seq(x, start, size):
    return lax.dynamic_slice_in_dim(x, start, size, axis=1)

def pad_front(x, n):
    return jnp.pad(x, ((0, 0), (n, 0), (0, 0), (0, 0)))

def blocked_map(fn, seq_len):
    out = lax.map(fn, jnp.arange(seq_len // QUERY_BLOCK) * QUERY_BLOCK)
    out = jnp.moveaxis(out, 0, 1)
    return out.reshape(out.shape[0], seq_len, *out.shape[3:])

def window_block(q, k_pad, v_pad, qs, window, sink=None):
    B, _, H, d = q.shape
    G = k_pad.shape[2]
    R = H // G
    L = window + QUERY_BLOCK
    qb = slice_seq(q, qs, QUERY_BLOCK).reshape(B, QUERY_BLOCK, G, R, d)
    kb = slice_seq(k_pad, qs, L)
    vb = slice_seq(v_pad, qs, L)
    t = qs + jnp.arange(QUERY_BLOCK)[:, None]
    kpos = qs - window + jnp.arange(L)[None, :]
    mask = (kpos <= t) & (kpos > t - window) & (kpos >= 0)
    s = jnp.einsum('bqgrd,bkgd->bgrqk', qb, kb).astype(jnp.float32) * (d ** -0.5)
    p = masked_probs(s, mask, sink)
    o = jnp.einsum('bgrqk,bkgd->bqgrd', p.astype(vb.dtype), vb)
    return o.reshape(B, QUERY_BLOCK, H, d)

def swa_mixer(q, k, v, pos, sinks):
    B, S, _ = q.shape
    q = rope(q.reshape(B, S, SWA_HEADS, HEAD_DIM), pos)
    k = pad_front(rope(k.reshape(B, S, SWA_KV_HEADS, HEAD_DIM), pos), SWA_WINDOW)
    v = pad_front(v.reshape(B, S, SWA_KV_HEADS, HEAD_DIM), SWA_WINDOW)
    sink = sinks.astype(jnp.float32).reshape(1, SWA_KV_HEADS, SWA_HEADS // SWA_KV_HEADS, 1, 1)
    o = blocked_map(lambda qs: window_block(q, k, v, qs, SWA_WINDOW, sink), S)
    return o.reshape(B, S, SWA_HEADS * HEAD_DIM)

def nsa_compress(k, pe, w1, w2):
    B, S, G, d = k.shape
    n_cmp = (S - NSA_CMP_BLOCK) // NSA_CMP_STRIDE + 1
    idx = np.arange(n_cmp)[:, None] * NSA_CMP_STRIDE + np.arange(NSA_CMP_BLOCK)[None, :]
    blk = k[:, idx] + pe[None, None, :, None, :]
    blk = jnp.swapaxes(blk, 2, 3).reshape(B, n_cmp, G, NSA_CMP_BLOCK * d)
    return jax.nn.silu(blk @ w1) @ w2

def nsa_mixer(q, kc, vc, ks, vs, kw, vw, g_logits, pos, pe_k, pe_v, wk1, wk2, wv1, wv2):
    B, S, _ = q.shape
    H, G, d = NSA_HEADS, NSA_KV_GROUPS, HEAD_DIM
    R = H // G
    shp = (B, S, G, d)
    q = q.reshape(B, S, H, d)
    q_rot = rope(q, pos)
    k_cmp = nsa_compress(kc.reshape(shp), pe_k, wk1, wk2)
    v_cmp = nsa_compress(vc.reshape(shp), pe_v, wv1, wv2)
    n_cmp = k_cmp.shape[1]
    cmp_start = np.arange(n_cmp) * NSA_CMP_STRIDE
    cmp_end = jnp.asarray(cmp_start + NSA_CMP_BLOCK - 1)
    n_slc = S // NSA_SEL_BLOCK
    sel_start = np.arange(n_slc) * NSA_SEL_BLOCK
    cover = (np.minimum(cmp_start[:, None] + NSA_CMP_BLOCK, sel_start[None, :] + NSA_SEL_BLOCK)
             - np.maximum(cmp_start[:, None], sel_start[None, :]))
    cmp_to_sel = jnp.asarray(np.clip(cover, 0, None) / NSA_CMP_STRIDE, dtype=jnp.float32)
    n_sel = min(NSA_N_SEL, n_slc)
    to_blocks = lambda a: jnp.transpose(a.reshape(B, n_slc, NSA_SEL_BLOCK, G, d), (0, 3, 1, 2, 4))
    k_sel_blk = to_blocks(rope(ks.reshape(shp), pos))
    v_sel_blk = to_blocks(vs.reshape(shp))
    k_win = pad_front(rope(kw.reshape(shp), pos), NSA_WINDOW)
    v_win = pad_front(vw.reshape(shp), NSA_WINDOW)
    gate = jax.nn.sigmoid(g_logits.astype(jnp.float32)).reshape(B, S, H, 3)
    gather = jax.vmap(jax.vmap(lambda blocks, ids: blocks[ids]))
    scale = d ** -0.5
    blk_ids = jnp.arange(n_slc)[None, :]
    m_sel = n_sel * NSA_SEL_BLOCK

    def block(qs):
        t = qs + jnp.arange(QUERY_BLOCK)
        qb = slice_seq(q, qs, QUERY_BLOCK).reshape(B, QUERY_BLOCK, G, R, d)
        s = jnp.einsum('bqgrd,bcgd->bgrqc', qb, k_cmp).astype(jnp.float32) * scale
        p_cmp = masked_probs(s, cmp_end[None, :] <= t[:, None])
        o_cmp = jnp.einsum('bgrqc,bcgd->bqgrd', p_cmp.astype(v_cmp.dtype), v_cmp)
        imp = jnp.einsum('bgqc,cj->bgqj', p_cmp.sum(axis=2), cmp_to_sel)
        cur = (t // NSA_SEL_BLOCK)[:, None]
        valid = blk_ids <= cur
        forced = (blk_ids == 0) | (blk_ids == cur) | (blk_ids == cur - 1)
        score = jnp.where(valid, imp + jnp.where(forced, NSA_FORCE_BONUS, 0.0), -jnp.inf)
        top_val, top_idx = lax.top_k(score, n_sel)
        k_g = gather(k_sel_blk, top_idx).reshape(B, G, QUERY_BLOCK, m_sel, d)
        v_g = gather(v_sel_blk, top_idx).reshape(B, G, QUERY_BLOCK, m_sel, d)
        tok = (top_idx[..., None] * NSA_SEL_BLOCK + jnp.arange(NSA_SEL_BLOCK)).reshape(B, G, QUERY_BLOCK, m_sel)
        ok = (tok <= t[:, None]) & jnp.repeat(jnp.isfinite(top_val), NSA_SEL_BLOCK, axis=-1)
        qrb = slice_seq(q_rot, qs, QUERY_BLOCK).reshape(B, QUERY_BLOCK, G, R, d)
        s = jnp.einsum('bqgrd,bgqmd->bgrqm', qrb, k_g).astype(jnp.float32) * scale
        p_sel = masked_probs(s, ok[:, :, None])
        o_sel = jnp.einsum('bgrqm,bgqmd->bqgrd', p_sel.astype(v_g.dtype), v_g)
        o_win = window_block(q_rot, k_win, v_win, qs, NSA_WINDOW)
        g = slice_seq(gate, qs, QUERY_BLOCK).astype(q.dtype)
        return (g[..., 0:1] * o_cmp.reshape(B, QUERY_BLOCK, H, d)
                + g[..., 1:2] * o_sel.reshape(B, QUERY_BLOCK, H, d)
                + g[..., 2:3] * o_win)

    return blocked_map(block, S).reshape(B, S, H * d)

def mla_mixer(q_lat, kv_lat, k_rot, pos, q_norm, w_q_b, kv_norm, w_kv_b):
    B, S, _ = q_lat.shape
    H = MLA_HEADS
    q = (rmsnorm(q_lat, q_norm) @ w_q_b).reshape(B, S, H, MLA_NOPE_DIM + MLA_ROPE_DIM)
    q_nope, q_pe = q[..., :MLA_NOPE_DIM], rope(q[..., MLA_NOPE_DIM:], pos)
    kv = (rmsnorm(kv_lat, kv_norm) @ w_kv_b).reshape(B, S, H, MLA_NOPE_DIM + MLA_V_DIM)
    k_nope, v = kv[..., :MLA_NOPE_DIM], kv[..., MLA_NOPE_DIM:]
    k_pe = rope(k_rot[:, :, None, :], pos)[:, :, 0]
    scale = (MLA_NOPE_DIM + MLA_ROPE_DIM) ** -0.5
    kpos = jnp.arange(S)[None, :]

    def block(qs):
        t = qs + jnp.arange(QUERY_BLOCK)[:, None]
        qn = slice_seq(q_nope, qs, QUERY_BLOCK)
        qp = slice_seq(q_pe, qs, QUERY_BLOCK)
        s = (jnp.einsum('bqhd,bkhd->bhqk', qn, k_nope)
             + jnp.einsum('bqhd,bkd->bhqk', qp, k_pe)).astype(jnp.float32) * scale
        p = masked_probs(s, kpos <= t)
        return jnp.einsum('bhqk,bkhd->bqhd', p.astype(v.dtype), v)

    return blocked_map(block, S).reshape(B, S, H * MLA_V_DIM)

def cross_attn(hx, hm, w_q, w_kv, w_o):
    B, S, _ = hx.shape
    M = hm.shape[1]
    q = (hx @ w_q).reshape(B, S, XATTN_HEADS, XATTN_HEAD_DIM)
    kv = (hm @ w_kv).reshape(B, M, 2, XATTN_HEADS, XATTN_HEAD_DIM)
    k, v = kv[:, :, 0], kv[:, :, 1]
    s = jnp.einsum('bshd,bmhd->bhsm', q, k).astype(jnp.float32) * (XATTN_HEAD_DIM ** -0.5)
    p = jax.nn.softmax(s, axis=-1)
    o = jnp.einsum('bhsm,bmhd->bshd', p.astype(v.dtype), v)
    return o.reshape(B, S, XATTN_HEADS * XATTN_HEAD_DIM) @ w_o

def second_inputs(seed: int = 0) -> dict:
    key = jax.random.key(seed)
    ks = iter(jax.random.split(key, 32))
    f32 = jnp.float32
    L = DEPTH_2

    def dense(shape, fan_in):
        return jax.random.normal(next(ks), shape, f32) * fan_in ** -0.5

    def gain(shape):
        return 1.0 + 0.1 * jax.random.normal(next(ks), shape, f32)

    x = jax.random.normal(next(ks), (BATCH, SEQ, D_MODEL), f32)
    mem = jax.random.normal(next(ks), (BATCH, N_MEM, D_MODEL), f32)
    positions = (jnp.arange(SEQ, dtype=jnp.int32)[None, :]
                 + jax.random.randint(next(ks), (BATCH, 1), 0, 4096, dtype=jnp.int32))
    cmp_in = NSA_CMP_BLOCK * HEAD_DIM
    return {
        'x': x,
        'mem': mem,
        'positions': positions,
        'norm_mix': gain((L, D_MODEL)),
        'w_in': dense((L, D_MODEL, D_IN), D_MODEL),
        'swa_sinks': jax.random.normal(next(ks), (L, SWA_HEADS), f32),
        'nsa_pe_k': 0.1 * jax.random.normal(next(ks), (L, NSA_CMP_BLOCK, HEAD_DIM), f32),
        'nsa_pe_v': 0.1 * jax.random.normal(next(ks), (L, NSA_CMP_BLOCK, HEAD_DIM), f32),
        'nsa_wk1': dense((L, cmp_in, HEAD_DIM), cmp_in),
        'nsa_wk2': dense((L, HEAD_DIM, HEAD_DIM), HEAD_DIM),
        'nsa_wv1': dense((L, cmp_in, HEAD_DIM), cmp_in),
        'nsa_wv2': dense((L, HEAD_DIM, HEAD_DIM), HEAD_DIM),
        'mla_q_norm': gain((L, MLA_Q_RANK)),
        'mla_w_q_b': dense((L, MLA_Q_RANK, MLA_HEADS * (MLA_NOPE_DIM + MLA_ROPE_DIM)), MLA_Q_RANK),
        'mla_kv_norm': gain((L, MLA_KV_RANK)),
        'mla_w_kv_b': dense((L, MLA_KV_RANK, MLA_HEADS * (MLA_NOPE_DIM + MLA_V_DIM)), MLA_KV_RANK),
        'w_br_a': dense((L, SWA_HEADS * HEAD_DIM, D_MODEL), SWA_HEADS * HEAD_DIM),
        'w_br_b': dense((L, NSA_HEADS * HEAD_DIM, D_MODEL), NSA_HEADS * HEAD_DIM),
        'w_br_c': dense((L, MLA_HEADS * MLA_V_DIM, D_MODEL), MLA_HEADS * MLA_V_DIM),
        'w_out': dense((L, D_MODEL, D_MODEL), D_MODEL),
        'norm_xattn': gain((L, D_MODEL)),
        'norm_mem': gain((L, D_MODEL)),
        'w_xq': dense((L, D_MODEL, XATTN_HEADS * XATTN_HEAD_DIM), D_MODEL),
        'w_xkv': dense((L, D_MODEL, 2 * XATTN_HEADS * XATTN_HEAD_DIM), D_MODEL),
        'w_xo': dense((L, XATTN_HEADS * XATTN_HEAD_DIM, D_MODEL), XATTN_HEADS * XATTN_HEAD_DIM),
        'norm_ffn': gain((L, D_MODEL)),
        'w_gate_up': dense((L, D_MODEL, 2 * D_FF), D_MODEL),
        'w_down': dense((L, D_FF, D_MODEL), D_FF),
        'norm_final': gain((D_MODEL,)),
    }

def second_block(x, mem, positions, norm_mix, w_in, swa_sinks, nsa_pe_k, nsa_pe_v, nsa_wk1, nsa_wk2,
              nsa_wv1, nsa_wv2, mla_q_norm, mla_w_q_b, mla_kv_norm, mla_w_kv_b, w_br_a, w_br_b,
              w_br_c, w_out, norm_xattn, norm_mem, w_xq, w_xkv, w_xo, norm_ffn, w_gate_up, w_down,
              norm_final):
    B, S, D = x.shape
    offsets = np.cumsum(IN_SPLITS)[:-1].tolist()
    for l in range(DEPTH_2):
        h = rmsnorm(x, norm_mix[l])
        (a_q, a_k, a_v, b_q, b_kc, b_vc, b_ks, b_vs, b_kw, b_vw, b_g,
         c_qa, c_kv, c_kr, g_br) = jnp.split(h @ w_in[l], offsets, axis=-1)
        o_a = swa_mixer(a_q, a_k, a_v, positions, swa_sinks[l])
        o_b = nsa_mixer(b_q, b_kc, b_vc, b_ks, b_vs, b_kw, b_vw, b_g, positions,
                        nsa_pe_k[l], nsa_pe_v[l], nsa_wk1[l], nsa_wk2[l], nsa_wv1[l], nsa_wv2[l])
        o_c = mla_mixer(c_qa, c_kv, c_kr, positions, mla_q_norm[l], mla_w_q_b[l],
                        mla_kv_norm[l], mla_w_kv_b[l])
        g = jax.nn.sigmoid(g_br.astype(jnp.float32)).reshape(B, S, N_BRANCH, D).astype(x.dtype)
        merged = (g[:, :, 0] * (o_a @ w_br_a[l])
                  + g[:, :, 1] * (o_b @ w_br_b[l])
                  + g[:, :, 2] * (o_c @ w_br_c[l]))
        x = x + merged @ w_out[l]
        x = x + cross_attn(rmsnorm(x, norm_xattn[l]), rmsnorm(mem, norm_mem[l]),
                           w_xq[l], w_xkv[l], w_xo[l])
        h = rmsnorm(x, norm_ffn[l])
        gate_h, up_h = jnp.split(h @ w_gate_up[l], 2, axis=-1)
        x = x + (jax.nn.silu(gate_h) * up_h) @ w_down[l]
    return rmsnorm(x, norm_final)


def setup_inputs(seed=0):
    out = dict(first_inputs(seed))
    for name, value in second_inputs(seed + 1).items():
        if name != "x":
            out[name + "_2"] = value
    return out


def reference(
    x, c, w_mod, b_mod, w_in, conv_w, conv_b, dt_bias, a_log, d_skip, ssd_norm_w, forget_b,
    w_ssd_o, w_att_o, w_o, ln1_g, ln1_b, w_router_group, b_router_group, w_router_expert,
    b_router_expert, w_gate, w_up, w_down, ln2_g, ln2_b, mem_2, positions_2, norm_mix_2, w_in_2,
    swa_sinks_2, nsa_pe_k_2, nsa_pe_v_2, nsa_wk1_2, nsa_wk2_2, nsa_wv1_2, nsa_wv2_2,
    mla_q_norm_2, mla_w_q_b_2, mla_kv_norm_2, mla_w_kv_b_2, w_br_a_2, w_br_b_2, w_br_c_2,
    w_out_2, norm_xattn_2, norm_mem_2, w_xq_2, w_xkv_2, w_xo_2, norm_ffn_2, w_gate_up_2,
    w_down_2, norm_final_2,
):
    x = first_block(
        x, c, w_mod, b_mod, w_in, conv_w, conv_b, dt_bias, a_log, d_skip, ssd_norm_w, forget_b,
        w_ssd_o, w_att_o, w_o, ln1_g, ln1_b, w_router_group, b_router_group, w_router_expert,
        b_router_expert, w_gate, w_up, w_down, ln2_g, ln2_b,
    )
    return second_block(
        x, mem_2, positions_2, norm_mix_2, w_in_2, swa_sinks_2, nsa_pe_k_2, nsa_pe_v_2,
        nsa_wk1_2, nsa_wk2_2, nsa_wv1_2, nsa_wv2_2, mla_q_norm_2, mla_w_q_b_2, mla_kv_norm_2,
        mla_w_kv_b_2, w_br_a_2, w_br_b_2, w_br_c_2, w_out_2, norm_xattn_2, norm_mem_2, w_xq_2,
        w_xkv_2, w_xo_2, norm_ffn_2, w_gate_up_2, w_down_2, norm_final_2,
    )


_drawn_inputs = setup_inputs


def setup_inputs(seed=0):
    import zlib

    import numpy as np

    out = dict(_drawn_inputs(seed))
    spreads = {}
    factors = {'b_mod': 3.553,
     'conv_b': 5.441,
     'd_skip': 3.688,
     'ssd_norm_w': 4.55,
     'b_router_group': 6.046,
     'b_router_expert': 8.0,
     'swa_sinks_2': 3.651,
     'nsa_pe_k_2': 8.0,
     'mla_q_norm_2': 3.851,
     'norm_xattn_2': 3.464}
    for name, (base, spread) in spreads.items():
        noise = np.random.default_rng([zlib.crc32(name.encode()), seed]).standard_normal(out[name].shape)
        drawn = base * np.exp(spread * noise) if base else spread * noise
        out[name] = jnp.asarray(drawn.astype(out[name].dtype))
    for name, factor in factors.items():
        out[name] = (out[name] * factor).astype(out[name].dtype)
    return out
```

```python
from contextlib import ExitStack

import numpy as np

import concourse.bass as bass
from concourse import mybir

F32 = mybir.dt.float32
I32 = mybir.dt.int32
ALU = mybir.AluOpType
ACT = mybir.ActivationFunctionType
AX_X = mybir.AxisListType.X

P = 128
SEQ = 256
TB = SEQ // P
D = 1024
KD = D // P
HALF = 512
LN_EPS = 1e-5
RMS_EPS = 1e-6
MASKED = 1e30

SSD_HEADS, SSD_P, SSD_GROUPS, SSD_N = 16, 64, 4, 128
SSD_R = SSD_HEADS // SSD_GROUPS
CONV_TILES = (D + 2 * SSD_GROUPS * SSD_N) // P
CONV_K = 4
FOX_HEADS = 8
OFF_Z, OFF_XBC, OFF_DT, OFF_Q, OFF_K, OFF_V, OFF_F, OFF_GS, OFF_GA = (
    int(v) for v in np.cumsum([0, D, CONV_TILES * P, SSD_HEADS, 512, 512, 512, FOX_HEADS, D]))
N_GROUPS, PER_GROUP = 4, 4
N_EXPERTS = N_GROUPS * PER_GROUP
FF = D // 2
KF = FF // P
SLOT_TOKENS = P // 2
PAIRS = N_EXPERTS // 2
ROUNDS = SEQ // SLOT_TOKENS
PICKS = ROUNDS * N_EXPERTS + 2
ALPHA = float(2.0 ** 0.25)

LAYERS = 2
HEADS, HD = 8, 64
CMP_BLOCK, CMP_STRIDE = 32, 16
N_CMP = (SEQ - CMP_BLOCK) // CMP_STRIDE + 1
CMP = N_CMP + 1
MLA_Q, MLA_KV, MLA_QK, MLA_ROPE = 384, 256, 96, 32
XH, XD = 4, 128
D_FF = 2816
KFF = D_FF // P
(C_AQ, C_AK, C_AV, C_BQ, C_KC, C_VC, C_KS, C_VS, C_KW, C_VW, C_BG, C_QA, C_KV, C_KR, C_G) = (
    int(v) for v in np.cumsum([0, 512, 128, 128, 512, 128, 128, 128, 128, 128, 128, 24, MLA_Q, MLA_KV, MLA_ROPE]))
assert SEQ // 64 <= 16 and SEQ <= 512

IN_AT = [C_AQ, C_AK, C_BQ, C_KC, C_KW, (C_KW + C_G) // 2, C_G]

SLOTS = 3
SLOT = KD * HALF

G_MIX, G_XATTN, G_MEM, G_FFN, G_QN, G_KVN, G_PEK, G_PEV, G_END = (
    int(v) for v in np.cumsum([0, KD, KD, KD, KD, MLA_Q // P, MLA_KV // P, 16, 16]))


class Bank:

    def __init__(self, ap, full, free, given=0):
        self.ap, self.full, self.free = ap, full, free
        self.start, self.per, self.uses, self.total = {}, {}, {}, given

    def begin(self, part, per_round):
        self.part, self.start[part], self.per[part], self.uses[part] = part, self.total, per_round, []

    def turn(self, name, rnd=0):
        uses = self.uses[self.part]
        assert name not in uses, name
        uses.append(name)
        return self.start[self.part] + rnd * self.per[self.part] + len(uses) - 1

    def end(self, rounds):
        n = len(self.uses[self.part])
        assert rounds == 1 or n == self.per[self.part], (self.part, n, self.per[self.part])
        self.total += rounds * n

    def nth(self, part, name, rnd=0):
        return self.start[part] + rnd * self.per[part] + self.uses[part].index(name) + 1


class Steps:

    def __init__(self, eng, sem):
        self.eng, self.sem, self.base, self.n, self.rnd, self.per = eng, sem, 0, 0, 0, 0

    def begin(self, rnd, per):
        self.n, self.rnd, self.per = 0, rnd, per

    def done(self, ins):
        ins.then_inc(self.sem, 1)
        self.n += 1

    def settle(self):
        self.eng.wait_ge(self.sem, self.base + self.rnd * self.per + self.n)

    def end(self, rounds=1):
        assert rounds == 1 or self.n == self.per, (self.n, self.per)
        self.base += rounds * self.n
        self.n, self.rnd, self.per = 0, 0, 0


class Named:

    def __init__(self, sem, **parts):
        self.sem, self.parts, self.start, total = sem, {}, {}, 0
        for part, (rounds, names) in parts.items():
            self.parts[part], self.start[part] = names, total
            total += rounds * len(names)
        self.total = total

    def at(self, part, name, rnd=0):
        names = self.parts[part]
        return self.start[part] + rnd * len(names) + names.index(name) + 1


MOD_CHUNKS = [f"mod{i}" for i in range(6 * D // HALF)]
FIRST_CHUNKS = (MOD_CHUNKS + ["dtf"] + [f"xbc{i}" for i in range(4)] + ["q", "k", "v", "z0", "z1", "ga0", "ga1",
                "gs0", "gs1", "att", "so0", "so1", "o0", "o1"])
PAIR_CHUNKS = ["gate0", "up0", "gate1", "up1", "down0", "down1"]
GATE_CHUNKS = [f"g{i}" for i in range(6)]
LAYER_CHUNKS = ([f"in{i}" for i in range(6)] + ["g0", "qb", "kvb", "g1", "g2", "g3", "g4", "cmp", "g5"]
                + ["bra", "brb", "brc", "out0", "out1", "memk", "memv", "xq", "xo"]
                + [f"gu{i}" for i in range(KFF // 2)] + [f"fd{i}" for i in range(6)])

FOX_STEPS = [("fox", pp, qb) for pp in range(2) for qb in range(TB)]
SWA_STEPS = [("swa", pp, qb) for pp in range(2) for qb in range(TB)]
CMP_STEPS = [("cmp", 0, qb) for qb in range(TB)]
SEL_STEPS = [("sel", pp, qb) for pp in range(2) for qb in range(TB)]
WIN_STEPS = [("win", pp, qb) for pp in range(2) for qb in range(TB)]
MLA_STEPS = [("mla", pp, qb) for pp in range(2) for qb in range(TB)]
X_STEPS = [("x", 0, qb) for qb in range(TB)]
LAYER_STEPS = SWA_STEPS + CMP_STEPS + SEL_STEPS + WIN_STEPS + MLA_STEPS + X_STEPS
FILLERS = {("swa", 0, 0): "g1", ("swa", 0, 1): "g2", ("swa", 1, 0): "g3", ("swa", 1, 1): "g4", ("sel", 0, 0): "g5"}


def step_tag(step):
    return f"{step[0]}{step[1]}{step[2]}"


def keys_of(step):
    return SEQ if step[2] == 1 or step[0] == "x" else P


ROUND = float(1.5 * 2 ** 23)
TURN = (6.28125, float(np.float32(2 * np.pi - 6.28125) // 2 ** -21 * 2 ** -21))
TURN = (*TURN, float(np.float32(2 * np.pi - TURN[0] - TURN[1])))
PI_IN = 3.1415925

ARENA = 31100


PIECES = {"in0": 2 * KD, "in2": 2 * KD, "dtf": 2, "cmp": 2, **{f"gu{i}": 2 for i in range(KFF // 2)}}
PARTS = {"first": (1, FIRST_CHUNKS), "layer": (LAYERS, LAYER_CHUNKS + ["unused"])}
assert len(PARTS["layer"][1]) % SLOTS == 0 and len(PAIR_CHUNKS) == 2 * SLOTS


def place_chunks():
    place, at, landed = {}, 0, [0] * SLOTS
    for part, (rounds, names) in PARTS.items():
        per = [0] * SLOTS
        for j, name in enumerate(names):
            per[(at + j) % SLOTS] += 16 * PIECES.get(name, 1) * (name != "unused")
        seen = [0] * SLOTS
        for j, name in enumerate(names):
            s = (at + j) % SLOTS
            seen[s] += 16 * PIECES.get(name, 1) * (name != "unused")
            place[part, name] = (s, landed[s] + seen[s], per[s])
        landed = [a + rounds * b for a, b in zip(landed, per)]
        at += rounds * len(names)
    return place


PLACE = place_chunks()

LAYER_USES = {"G0": 40, "G1": 40, "S": 21, "P": 21, "O": 44, "X": 28}
LAYER_DVE_STEPS = 132


def two_blocks(nc, t, out):
    with ExitStack() as ctx, nc.allow_non_contiguous_dma(reason="small vectors turned onto partitions"):
        def sb(name, shape, dt=F32):
            return ctx.enter_context(nc.sbuf_tensor(name, shape, dt))

        def sem(name):
            return ctx.enter_context(nc.semaphore(name))

        ring = sb("ring", [P, SLOTS, SLOT])
        x_rows = sb("x_rows", [P, TB, D])
        h_rows = sb("h_rows", [P, TB, D])
        h_t = sb("h_t", [P, KD, SEQ])
        ident = sb("ident", [P, P])
        tri = sb("tri", [P, SEQ])
        causal = sb("causal", [P, SEQ])
        windowed = sb("windowed", [P, SEQ])
        cmp_mask = sb("cmp_mask", [P, TB, CMP])
        head_of = sb("head_of", [P, HEADS])
        half_power = sb("half_power", [P, TB])
        inv_freq = sb("inv_freq", [P, HD // 2])
        pos_i = sb("pos_i", [P, TB], I32)
        pos_f = sb("pos_f", [P, TB])
        angle = sb("angle", [P, 4, TB, HD // 2])
        rope_c = sb("rope_c", [P, TB, HD])
        rope_s = sb("rope_s", [P, TB, HD])
        stage = sb("stage", [P, P])
        c_col = sb("c_col", [P, KD])
        c_act = sb("c_act", [P, KD])
        conv_col = sb("conv_col", [P, CONV_TILES * (CONV_K + 1) + KD])
        bias24 = sb("bias24", [P, SSD_HEADS + FOX_HEADS])
        a_log_b = sb("a_log_b", [P, SSD_HEADS])
        d_skip_b = sb("d_skip_b", [P, SSD_HEADS])
        sp = sb("sp", [P, 6, TB, SSD_HEADS + FOX_HEADS])
        dt_a = sb("dt_a", [P, 5, TB, SSD_HEADS])
        route_w = sb("route_w", [P, KD, N_GROUPS + N_EXPERTS])
        route_b = sb("route_b", [P, N_GROUPS + N_EXPERTS])
        rt = sb("rt", [P, TB, N_GROUPS + N_EXPERTS])
        rt_s = sb("rt_s", [P, 24, TB, PER_GROUP])
        rt_m = sb("rt_m", [P, TB, N_EXPERTS])
        back = sb("back", [P, PER_GROUP])
        gates = sb("gates", [P, TB, N_EXPERTS])
        rounds_f = sb("rounds_f", [P, 4])
        rounds_i = sb("rounds_i", [1, 2], I32)
        bn = sb("bn", [P, TB, 2, 6])
        mean_var = sb("mean_var", [P, TB, 2])
        square_sum = sb("square_sum", [P, TB])
        var_in = sb("var_in", [P, TB])
        rstd = sb("rstd", [P, TB])
        g_col = sb("g_col", [P, G_END])
        neg_max = sb("neg_max", [P, 2, HEADS])
        den = sb("den", [P, 2, HEADS])
        rden = sb("rden", [P, 2, HEADS])
        sink_neg = sb("sink_neg", [P, HEADS])
        sink_e = sb("sink_e", [P, 2, HEADS])
        branch_g = sb("branch_g", [P, TB, HEADS * 3])
        w2 = sb("w2", [HD, 2, HD])
        w2_k = sb("w2_k", [HD, 2, HD])
        w2_v = sb("w2_v", [HD, HD])
        cmp_h = sb("cmp_h", [HD, 4, 2, CMP])
        cmp_hv = sb("cmp_hv", [HD, 2, HEADS // 2, CMP])
        cmp_k = sb("cmp_k", [P, 2 * CMP])
        arena = sb("arena", [P, ARENA])

        def view(at, *shape):
            n = int(np.prod(shape))
            assert at + n <= ARENA, (at, shape)
            v = arena[:, at:at + n]
            if len(shape) == 2:
                v = v.rearrange("p (a b) -> p a b", b=shape[1])
            elif len(shape) == 3:
                v = v.rearrange("p (a b c) -> p a b c", b=shape[1], c=shape[2])
            return v

        at = 0
        mod = view(at, 6, D)
        xs = view(at, TB, SSD_HEADS, SSD_P)
        at += 6 * D
        b_mod = view(at, 1, 6 * D)
        conv = view(at, CONV_TILES, SEQ)
        ssd_y = view(at + CONV_TILES * SEQ, TB, D)
        pick = view(at, TB, P)
        pick_g = view(at + SEQ, TB, P)
        pick_t = view(at + 2 * SEQ, 1, SEQ)
        taken_t = view(at + D, KD, P)
        pair_y = view(at + 2 * D, 1, D)
        expert_t = view(at + 3 * D, 4, KF * SLOT_TOKENS)
        hid_t = view(at + 4 * D, 2, KF, SLOT_TOKENS)
        place = view(at + 4 * D + 512, TB, PICKS)
        gate_of = view(at + 4 * D + 768, TB, PICKS)
        slot_row = view(at + 5 * D, 1, SLOT_TOKENS)
        picked = view(at + 5 * D + 64, TB, N_EXPERTS)
        load_of = view(at + 5 * D + 128, 1, N_EXPERTS)
        at += 6 * D
        PAD = SEQ + CONV_K - 1
        xbc_pad = view(at, CONV_TILES, PAD)
        conv_tanh = view(at, CONV_TILES, SEQ)
        decay = view(at, TB * SSD_GROUPS, SSD_R, P)
        ln_rows = view(at, 4, D)
        at += CONV_TILES * PAD
        z_silu = view(at, TB, D)
        y_turned = view(at, KD, SEQ)
        resid = view(at, TB, D)
        at += TB * D
        gate_ssd = view(at, TB, D)
        at += TB * D
        gate_att = view(at, TB, D)
        at += TB * D
        q_t, k_t, v_rows = view(at, 4, SEQ), view(at + 1024, 4, SEQ), view(at + 2048, TB, HALF)
        x_end, cb, states = view(at, SSD_HEADS, SSD_P), view(at + 1024, TB * SSD_GROUPS, P), view(at + 2048, SSD_GROUPS, SSD_R * SSD_P)
        at += 3072
        fox_o, fox_ot = view(at, TB, HALF), view(at + 1024, KF, SEQ)
        b_rows = view(at + 1024, SSD_GROUPS, SSD_N)
        at += 2048
        S_AT = at
        scores = view(at, 2, 4, SEQ)
        probs_t = view(at + 2048, 4, 2, P)
        at += 3072
        xdt = h_rows[:, :, :].rearrange("p t (h d) -> p t h d", d=SSD_P)

        PW = C_G
        at = 0
        proj = view(at, TB, PW)
        mem_rows = view(0, TB, D)
        mem_t = view(2 * D, KD, SEQ)
        at += TB * PW
        gate_t = view(at, TB, 3 * D)
        ff_t = view(at, KFF, SEQ)
        at += TB * 3 * D
        rot = view(at, 1, 2816)
        swa_r = rot[:, 0, 0:1280].rearrange("p (t n) -> p t n", t=TB)
        nsa_q = rot[:, 0, 1280:2304].rearrange("p (t n) -> p t n", t=TB)
        nsa_k = rot[:, 0, 2304:2816].rearrange("p (t n) -> p t n", t=TB)
        mem_v = rot[:, 0, 0:1024].rearrange("p (t n) -> p t n", t=TB)
        x_gain = rot[:, 0, 0:D]
        at += 2816
        qt = view(at, 8, SEQ)
        merged = view(at, TB, D)
        at += 2048
        kt = view(at, 8, SEQ)
        kc_t = arena[:, at + 512:at + 512 + 4 * 272].rearrange("p (v g n) -> p v g n", v=2, g=2)
        at += 2048
        o_a, o_b, o_c = (view(at + 1024 * i, TB, HALF) for i in range(3))
        lat_t = view(at + 1024, 5, SEQ)
        at += 3072
        o_t = view(at, KF, SEQ)
        at += 1024
        lat = view(at, TB, MLA_Q + MLA_KV)
        at += TB * (MLA_Q + MLA_KV)
        mla_q = view(at, TB, HEADS * MLA_QK)
        at += TB * HEADS * MLA_QK
        mla_k = view(at, TB, HEADS * MLA_QK)
        at += TB * HEADS * MLA_QK
        cmp_v = view(at, HEADS, HD)
        at += HEADS * HD
        assert at <= S_AT, (at, S_AT)
        rope_tmp = view(S_AT, 1, 2048)
        kc_twice = view(S_AT + 2048, TB, HALF)
        cmp_blk = arena[:, S_AT:S_AT + 1024].rearrange("p (v j n) -> p v j n", v=2, j=16)
        ff_tmp = view(S_AT, 4, HALF)
        at = S_AT + 3072
        o_tmp = view(at, 4, HD)
        at += 256
        kv_rows = h_rows
        assert at <= ARENA, at

        def bank(name, first, n):
            ap = ctx.enter_context(nc.psum_tensor(f"ps_{name}", [P, n * HALF], F32))
            return Bank(ap, sem(f"{name}_full"), sem(f"{name}_free"))

        G0, G1 = bank("g0", 0, 1), bank("g1", 1, 1)
        S, PT = bank("s", 2, 2), bank("p", 4, 2)
        O, X = bank("o", 6, 1), bank("x", 7, 1)
        G, BANKS = (G0, G1), {"G0": G0, "G1": G1, "S": S, "P": PT, "O": O, "X": X}
        M0, M1, MO, MX = (Bank(b.ap, sem(f"expert_{n}_full"), sem(f"expert_{n}_free"), given=1)
                          for n, b in (("g0", G0), ("g1", G1), ("o", O), ("x", X)))
        EXPERT_BANKS = (M0, M1, MO, MX)

        landed = [sem(f"landed{s}") for s in range(SLOTS)]
        in_x, in_small, in_ln, in_stage, in_route = (sem(n) for n in ("in_x", "in_small", "in_ln", "in_stage", "in_route"))
        in_c, in_vec = sem("in_c"), sem("in_vec")
        consts = sem("consts")
        stored = sem("stored")
        c_tanh, c_ready = sem("c_tanh"), sem("c_ready")
        sp_exp, sp_ln, sp_abs, sp_one = sem("sp_exp"), sem("sp_ln"), sem("sp_abs"), sem("sp_one")
        conv_done, conv_tanhed = sem("conv_done"), sem("conv_tanhed")
        angle_ready, sines_ready = sem("angle_ready"), sem("sines_ready")
        sums_exp, forget_ready = sem("sums_exp"), sem("forget_ready")
        seg_exp, seg_cut, decay_ready = sem("seg_exp"), sem("seg_cut"), sem("decay_ready")
        conv_ready, xdt_ready = sem("conv_ready"), sem("xdt_ready")
        route_in, route_out = sem("route_in"), sem("route_out")
        gate_tanhed, ff_used = sem("gate_tanhed"), sem("ff_used")
        picked_ready, rounds_ready, sums_cleared = sem("picked_ready"), sem("rounds_ready"), sem("sums_cleared")
        expert_landed = [sem(f"expert_landed{s}") for s in range(SLOTS)]
        expert_used = sem("expert_used")
        pick_ready, pick_g_ready = sem("pick_ready"), sem("pick_g_ready")
        expert_tanhed, expert_steps = sem("expert_tanhed"), sem("expert_steps")
        z_tanhed = sem("z_tanhed")
        norms = ["mix", "qn", "kvn", "mem", "xattn", "ffn"]
        x_ready = Named(sem("x_ready"), mid=(1, ["x"]), layer=(LAYERS, ["ffn"]))
        squares = Named(sem("squares"), first=(1, ["gy"]), layer=(LAYERS, norms), last=(1, ["out"]))
        var_ready = Named(sem("var_ready"), first=(1, ["h", "gy", "ln1", "h2"]), mid=(1, ["ln2"]), layer=(LAYERS, norms), last=(1, ["out"]))
        rstd_ready = Named(sem("rstd_ready"), first=(1, ["h", "gy", "ln1", "h2"]), mid=(1, ["ln2"]), layer=(LAYERS, norms), last=(1, ["out"]))
        gy_ready = sem("gy_ready")
        rows = Named(sem("rows_ready"), first=(1, ["h", "gy", "mg", "h2"]),
                     layer=(LAYERS, ["mix", "swa", "nsa", "twice", "lat", "mk", "blk", "hcv", "ob", "merged", "mem", "xattn", "ffn"]))
        masked = Named(sem("scores_masked"), first=(1, [step_tag(s) for s in FOX_STEPS]), layer=(LAYERS, [step_tag(s) for s in LAYER_STEPS]))
        probs = Named(sem("probs_ready"), first=(1, [step_tag(s) for s in FOX_STEPS]), layer=(LAYERS, [step_tag(s) for s in LAYER_STEPS]))
        in_layer, in_mem = sem("in_layer"), sem("in_mem")
        bg_tanhed, cmp_tanhed = sem("bg_tanhed"), sem("cmp_tanhed")
        cmp_exp = sem("cmp_exp")
        last_rows, out_ready = sem("last_rows"), sem("out_ready")
        dve_steps, act_steps, pool_steps = sem("vector_steps"), sem("scalar_steps"), sem("gpsimd_steps")

        used = {}

        def chunk(eng, part, name, rnd=0):
            slot, count, per = PLACE[part, name]
            eng.wait_ge(landed[slot], count + rnd * per)
            return ring[:, slot, :]

        def keys(w, k, n):
            return w[:, 0:k * n].rearrange("p (k n) -> p k n", n=n)

        block = ctx.enter_context(nc.Block())

        @block.tensor
        def _(pe):
            def claim(b, name, rnd=0):
                v = b.turn(name, rnd)
                if not (isinstance(v, int) and v == 0):
                    pe.wait_ge(b.free, v)

            def begin(part):
                per = LAYER_USES if part == "layer" else {}
                for n, b in BANKS.items():
                    b.begin(part, per.get(n, 0))

            def end(rounds=1):
                for n, b in BANKS.items():
                    b.end(rounds)

            def turned(part, tag, n, rnd=0):
                for r in range(max(0, n - 2), n):
                    b = (X, O)[r % 2]
                    pe.wait_ge(b.free, b.nth(part, f"{tag}{r}", rnd))

            def turn_rows(tag, pieces, rnd=0, size=P):
                for r in range(0, len(pieces), 2):
                    b = (X, O)[r // 2 % 2]
                    claim(b, f"{tag}{r // 2}", rnd)
                    for i, piece in enumerate(pieces[r:r + 2]):
                        for tb in range(TB):
                            ins = pe.transpose(b.ap[0:size, i * SEQ + tb * P:i * SEQ + (tb + 1) * P], piece(tb), ident[:, :])
                    ins.then_inc(b.full, 1)

            def product_rows(part, name, tag, lhs, w, nk, lo, n, rnd=0, last=True):
                for tb in range(TB):
                    claim(G[tb], tag, rnd)
                    for k in range(nk):
                        ins = pe.matmul(G[tb].ap[:, 0:n], lhs[:, k, tb * P:(tb + 1) * P], w[:, k, lo:lo + n],
                                        start=k == 0, stop=k == nk - 1)
                    ins.then_inc(G[tb].full, 1)
                if last:
                    used[part, name] = (G1, tag)

            def product_turned(part, name, tag, rhs, w, nk, rnd=0):
                for f in range(4):
                    b = G[f // 2]
                    if f % 2 == 0:
                        claim(b, tag, rnd)
                    for k in range(nk):
                        ins = pe.matmul(b.ap[:, (f % 2) * SEQ:(f % 2 + 1) * SEQ], w[:, k, f * P:(f + 1) * P], rhs[:, k, :],
                                        start=k == 0, stop=k == nk - 1)
                    if f % 2:
                        ins.then_inc(b.full, 1)
                used[part, name] = (G1, tag)

            def product_wide(part, name, lhs, rnd=0):
                w = keys(chunk(pe, part, name, rnd), KF, D)
                for half in range(2):
                    product_rows(part, name, f"{name}{half}", lhs, w, KF, half * HALF, HALF, rnd, last=half == 1)

            def score_step(part, step, q, kk, rnd=0):
                kind, pp, qb = step
                nk = keys_of(step)
                claim(S, step_tag(step), rnd)
                s4 = S.ap[:, :].rearrange("p (i n) -> p i n", n=SEQ)
                for i in range(4):
                    half, pr = divmod(i, 2)
                    if kind in ("mla", "x"):
                        head, lo, n = 4 * pp + i, 0, MLA_QK if kind == "mla" else XD
                        ins = pe.matmul(s4[:, i, 0:nk], q[0:n, head, qb * P:(qb + 1) * P], kk[0:n, head, 0:nk], start=True, stop=True)
                        continue
                    lo, pair = HD * half, 2 * pp + pr
                    kpair = pair if kind == "fox" else 0
                    ins = pe.matmul(s4[:, i, 0:nk], q[lo:lo + HD, pair, qb * P:(qb + 1) * P], kk[lo:lo + HD, kpair, 0:nk],
                                    start=True, stop=kind != "fox")
                    if kind == "fox":
                        forget = lambda b: sp[:, 5, b, SSD_HEADS + 2 * pair + half:SSD_HEADS + 2 * pair + half + 1].broadcast_to([P, P])
                        ins = pe.matmul(s4[:, i, 0:nk], forget(0), tri[:, 0:nk], start=False, stop=qb == 0)
                        if qb == 1:
                            ins = pe.matmul(s4[:, i, P:SEQ], forget(1), tri[:, 0:P], start=False, stop=True)
                ins.then_inc(S.full, 1)

            def output_step(part, step, v, rnd=0, width=HD):
                tag, kbs = step_tag(step), keys_of(step) // P
                p4 = PT.ap[:, :].rearrange("p (i b n) -> p i b n", i=4, b=2)
                pe.wait_ge(probs.sem, probs.at(part, tag, rnd))
                claim(PT, tag, rnd)
                n = masked.parts[part].index(tag)
                for i in range(4):
                    for b in range(kbs):
                        ins = pe.transpose(p4[:, i, b, :], scores[:, n % 2, i, b * P:(b + 1) * P], ident[:, :])
                ins.then_inc(PT.full, 1)
                claim(O, tag, rnd)
                pe.wait_ge(PT.free, PT.nth(part, tag, rnd))
                for i in range(4):
                    for b in range(kbs):
                        ins = pe.matmul(O.ap[:, i * width:(i + 1) * width], probs_t[:, i, b, :], v(i, b),
                                        start=b == 0, stop=b == kbs - 1)
                ins.then_inc(O.full, 1)

            def attention(part, steps, q, kk, v, rnd=0, width=HD, filler=None):
                score_step(part, steps[0], q, kk, rnd)
                for n, step in enumerate(steps):
                    if n + 1 < len(steps):
                        score_step(part, steps[n + 1], q, kk, rnd)
                    if filler and step in FILLERS:
                        filler(FILLERS[step])
                    output_step(part, step, lambda i, b, s=step: v(s, i, b), rnd, width)

            begin("first")
            pe.wait_ge(consts, 1)
            pe.wait_ge(in_stage, 16 * 3)
            claim(X, "conv_col")
            n = CONV_TILES * (CONV_K + 1) + KD
            pe.transpose(X.ap[:, 0:n], stage[0:n, :], ident[0:n, 0:n]).then_inc(X.full, 1)

            pe.wait_ge(c_ready, 1)
            pe.wait_ge(in_small, 16)
            for i, name in enumerate(MOD_CHUNKS):
                w = keys(chunk(pe, "first", name), KD, HALF)
                b = G[i % 2]
                claim(b, name)
                for k in range(KD):
                    pe.matmul(b.ap[:, :], c_act[:, k:k + 1].broadcast_to([P, P]), w[:, k, :], start=k == 0, stop=False)
                pe.matmul(b.ap[:, :], tri[0:1, P:SEQ], b_mod[0:1, 0, i * HALF:(i + 1) * HALF], start=False, stop=True)\
                    .then_inc(b.full, 1)
                used["first", name] = (b, name)

            pe.wait_ge(rows.sem, rows.at("first", "h"))
            turn_rows("h", [lambda tb, k=k: h_rows[:, tb, k * P:(k + 1) * P] for k in range(KD)])
            turned("first", "h", 4)

            w = chunk(pe, "first", "dtf")[:, 0:KD * 24].rearrange("p (k n) -> p k n", n=24)
            product_rows("first", "dtf", "dtf", h_t, w, KD, 0, 24)
            for name in ["xbc0", "xbc1", "xbc2", "xbc3", "q", "k"]:
                product_turned("first", name, name, h_t, keys(chunk(pe, "first", name), KD, HALF), KD)
            for name in ["v", "z0", "z1", "ga0", "ga1", "gs0", "gs1"]:
                product_rows("first", name, name, h_t, keys(chunk(pe, "first", name), KD, HALF), KD, 0, HALF)

            for b in G:
                pe.wait_ge(b.free, b.nth("first", "v"))
            pe.wait_ge(forget_ready, 1)
            attention("first", FOX_STEPS, q_t, k_t, lambda s, i, b: v_rows[
                :, b, (2 * (2 * s[1] + i % 2) + i // 2) * HD:(2 * (2 * s[1] + i % 2) + i // 2 + 1) * HD])
            pe.wait_ge(O.free, O.nth("first", step_tag(FOX_STEPS[-1])))
            turn_rows("fox", [lambda tb, k=k: fox_o[:, tb, k * P:(k + 1) * P] for k in range(KF)])
            turned("first", "fox", 2)
            product_wide("first", "att", fox_ot)

            claim(X, "sums")
            a_in = dt_a[:, 1, :, :].rearrange("p t h -> p (t h)")
            pe.matmul(X.ap[:, 0:32], tri[:, 0:P], a_in, start=True, stop=True)
            pe.matmul(X.ap[:, 32:64], tri[:, P:SEQ], a_in, start=True, stop=True).then_inc(X.full, 1)
            pe.wait_ge(conv_ready, 4)
            claim(O, "b_rows")
            for g in range(SSD_GROUPS):
                ins = pe.transpose(O.ap[:, g * P:(g + 1) * P], conv[:, 8 + g, 0:P], ident[:, :])
            ins.then_inc(O.full, 1)
            for r in range(4):
                tb, half = divmod(r, 2)
                b = (X, O)[r % 2]
                claim(b, f"xs{r}")
                for i in range(4):
                    ins = pe.transpose(b.ap[:, i * P:(i + 1) * P], conv[:, 4 * half + i, tb * P:(tb + 1) * P], ident[:, :])
                ins.then_inc(b.full, 1)
            claim(S, "cb")
            for c in range(TB):
                for g in range(SSD_GROUPS):
                    ins = pe.matmul(S.ap[:, (c * SSD_GROUPS + g) * P:(c * SSD_GROUPS + g + 1) * P], conv[:, 8 + g, c * P:(c + 1) * P],
                                    conv[:, 12 + g, c * P:(c + 1) * P], start=True, stop=True)
            ins.then_inc(S.full, 1)
            for c in range(TB):
                for g in range(SSD_GROUPS):
                    b = G[g % 2]
                    claim(b, f"seg{c}{g}")
                    for r in range(SSD_R):
                        h = g * SSD_R + r
                        ins = pe.matmul(b.ap[:, r * P:(r + 1) * P], dt_a[:, 1, c, h:h + 1].broadcast_to([P, P]), tri[:, 0:P],
                                        start=True, stop=True)
                    ins.then_inc(b.full, 1)
            pe.wait_ge(xdt_ready, 1)
            pe.wait_ge(O.free, O.nth("first", "b_rows"))
            claim(S, "states")
            for g in range(SSD_GROUPS):
                ins = pe.matmul(S.ap[:, g * SEQ:(g + 1) * SEQ], b_rows[:, g, :],
                                x_end[:, g * SSD_R:(g + 1) * SSD_R, :].rearrange("p h d -> p (h d)"), start=True, stop=True)
            ins.then_inc(S.full, 1)
            for c in range(TB):
                claim(PT, f"yd{c}")
                for g in range(SSD_GROUPS):
                    pe.wait_ge(decay_ready, c * SSD_GROUPS + g + 1)
                    for r in range(SSD_R):
                        h = g * SSD_R + r
                        ins = pe.matmul(PT.ap[:, h * SSD_P:(h + 1) * SSD_P], decay[:, c * SSD_GROUPS + g, r, :], xdt[:, c, h, :],
                                        start=True, stop=True)
                ins.then_inc(PT.full, 1)
            pe.wait_ge(S.free, S.nth("first", "states"))
            claim(S, "yo")
            for g in range(SSD_GROUPS):
                ins = pe.matmul(S.ap[:, g * SEQ:(g + 1) * SEQ], conv[:, 12 + g, P:SEQ], states[:, g, :], start=True, stop=True)
            ins.then_inc(S.full, 1)
            pe.wait_ge(rows.sem, rows.at("first", "gy"))
            turn_rows("gy", [lambda tb, k=k: ssd_y[:, tb, k * P:(k + 1) * P] for k in range(KD)])
            turned("first", "gy", 4)
            for name in ["so0", "so1"]:
                product_rows("first", name, name, y_turned, keys(chunk(pe, "first", name), KD, HALF), KD, 0, HALF)

            pe.wait_ge(rows.sem, rows.at("first", "mg"))
            turn_rows("mg", [lambda tb, k=k: gate_att[:, tb, k * P:(k + 1) * P] for k in range(KD)])
            turned("first", "mg", 4)
            for name in ["o0", "o1"]:
                product_rows("first", name, name, h_t, keys(chunk(pe, "first", name), KD, HALF), KD, 0, HALF)

            pe.wait_ge(rows.sem, rows.at("first", "h2"))
            turn_rows("h2", [lambda tb, k=k: h_rows[:, tb, k * P:(k + 1) * P] for k in range(KD)])
            turned("first", "h2", 4)
            pe.wait_ge(in_route, 32)
            product_rows("first", "route", "route", h_t, route_w, KD, 0, N_GROUPS + N_EXPERTS)

            pe.wait_ge(picked_ready, 1)
            claim(X, "places")
            upto, ones = tri[:, 0:P], tri[:, P:SEQ]
            pe.matmul(X.ap[:, 0:16], upto, picked[:, 0, :], start=True, stop=True)
            pe.matmul(X.ap[:, 16:32], ones, picked[:, 0, :], start=True, stop=False)
            pe.matmul(X.ap[:, 16:32], upto, picked[:, 1, :], start=False, stop=True)
            pe.matmul(X.ap[:, 32:48], ones, picked[:, 0, :], start=True, stop=False)
            pe.matmul(X.ap[:, 32:48], ones, picked[:, 1, :], start=False, stop=True)
            pe.matmul(X.ap[:, 48:48 + SLOT_TOKENS], ones, tri[:, 0:SLOT_TOKENS], start=True, stop=True).then_inc(X.full, 1)
            end()

            def gather(q, name="taken"):
                pe.wait_ge(pick_ready, q + 1)
                for j, b in enumerate((MO, MX)):
                    claim(b, name, q - 1)
                    for i in range(4):
                        k = 4 * j + i
                        for tb in range(TB):
                            ins = pe.matmul(b.ap[:, i * P:(i + 1) * P], h_rows[:, tb, k * P:(k + 1) * P], pick[:, tb, :],
                                            start=tb == 0, stop=tb == TB - 1)
                    ins.then_inc(b.full, 1)

            def scatter(start=False, stop=False):
                for tb, b in enumerate((S, PT)):
                    for half in range(2):
                        ins = pe.matmul(b.ap[:, half * HALF:(half + 1) * HALF], pick_t[:, 0, tb * P:(tb + 1) * P],
                                        pair_y[:, 0, half * HALF:(half + 1) * HALF], start=start, stop=stop)
                    if stop:
                        ins.then_inc(b.full, 1)

            begin("mid")
            pe.wait_ge(sums_cleared, 1)
            claim(S, "sums")
            claim(PT, "sums")
            scatter(start=True)
            for b in EXPERT_BANKS:
                b.begin("start", 0)
            pe.wait_ge(rounds_ready, 1)
            n_pairs = pe.value_load(rounds_i[0:1, 1:2], min_val=PAIRS, max_val=PAIRS * ROUNDS)
            gather(0, "taken")
            for b in EXPERT_BANKS:
                b.end(1)
            for b, n in ((M0, 2), (M1, 1), (MO, 2), (MX, 2)):
                b.begin("moe", n)
            for b in (MO, MX):
                pe.wait_ge(b.free, b.nth("start", "taken"))
            with pe.Fori(0, n_pairs) as q:
                def weights(j):
                    pe.wait_ge(expert_landed[j % SLOTS], q * 32 + 16 * (j // SLOTS + 1))
                    return ring[:, j % SLOTS, :]

                for b in (MO, MX):
                    pe.wait_ge(b.free, q * 2 + 1)
                for e, b in enumerate((M0, M1)):
                    claim(b, f"hidden{e}", q)
                    for kind in range(2):
                        w = keys(weights(2 * e + kind), KD, HALF)
                        for f in range(KF):
                            at_f = (kind * KF + f) * SLOT_TOKENS
                            for k in range(KD):
                                ins = pe.matmul(b.ap[:, at_f:at_f + SLOT_TOKENS], w[:, k, f * P:(f + 1) * P],
                                                taken_t[:, k, e * SLOT_TOKENS:(e + 1) * SLOT_TOKENS], start=k == 0, stop=k == KD - 1)
                        ins.then_inc(expert_used if kind == 0 else b.full, 1)
                    if e == 0:
                        for y in (MO, MX):
                            pe.wait_ge(y.free, q * 2 + 2)
                        pe.wait_ge(M0.free, q * 2 + 1)
                        scatter()
                claim(M0, "turned", q)
                pe.wait_ge(pick_g_ready, q + 1)
                for tb in range(TB):
                    ins = pe.transpose(M0.ap[:, tb * P:(tb + 1) * P], pick_g[:, tb, :], ident[:, :])
                ins.then_inc(M0.full, 1)
                gather(q + 1)
                for e, b in enumerate((M0, M1)):
                    wd = keys(weights(4 + e), KF, D)
                    pe.wait_ge(b.free, b.nth("moe", f"hidden{e}", q))
                    lanes = slice(e * SLOT_TOKENS, (e + 1) * SLOT_TOKENS)
                    for half, y in enumerate((MO, MX)):
                        if e == 0:
                            claim(y, "out", q)
                        for k in range(KF):
                            ins = pe.matmul(y.ap[lanes, :], hid_t[:, e, k, :], wd[:, k, half * HALF:(half + 1) * HALF],
                                            start=k == 0, stop=k == KF - 1)
                        if e == 1:
                            ins.then_inc(y.full, 1)
                    if e == 0:
                        ins.then_inc(expert_used, 1)
            for y in (MO, MX):
                pe.wait_ge(y.free, n_pairs * 2 + 2)
            pe.wait_ge(M0.free, n_pairs * 2 + 1)
            scatter(stop=True)
            end()

            begin("layer")
            with pe.Fori(0, LAYERS) as l:
                claim(X, "g_col", l)
                pe.wait_ge(in_layer, 16 * 11 + l * (16 * 11))
                pe.transpose(X.ap[:, 0:G_END], stage[0:G_END, :], ident[0:G_END, 0:G_END]).then_inc(X.full, 1)
                pe.wait_ge(rows.sem, rows.at("layer", "mix", l))
                turn_rows("mix", [lambda tb, k=k: h_rows[:, tb, k * P:(k + 1) * P] for k in range(KD)], l)
                turned("layer", "mix", 4, l)
                for i in range(6):
                    n = IN_AT[i + 1] - IN_AT[i]
                    product_rows("layer", f"in{i}", f"in{i}", h_t, keys(chunk(pe, "layer", f"in{i}", l), KD, n), KD, 0, n, l)

                def gate_product(name):
                    product_rows("layer", name, name, h_t, keys(chunk(pe, "layer", name, l), KD, HALF), KD, 0, HALF, l)

                gate_product("g0")

                pe.wait_ge(rows.sem, rows.at("layer", "lat", l))
                turn_rows("lat", [lambda tb, k=k: lat[:, tb, k * P:(k + 1) * P] for k in range(5)], l)
                turned("layer", "lat", 3, l)
                n = HEADS * MLA_QK
                w = chunk(pe, "layer", "qb", l)[:, 0:3 * n].rearrange("p (k n) -> p k n", n=n)
                product_rows("layer", "qb", "qb0", lat_t, w, 3, 0, HALF, l, last=False)
                product_rows("layer", "qb", "qb1", lat_t, w, 3, HALF, n - HALF, l)
                w = keys(chunk(pe, "layer", "kvb", l), 2, D)
                product_rows("layer", "kvb", "kvb0", lat_t[:, 3:5, :], w, 2, 0, HALF, l, last=False)
                product_rows("layer", "kvb", "kvb1", lat_t[:, 3:5, :], w, 2, HALF, HALF, l)

                def pair(src, lo, i):
                    return lambda tb: src[:, tb, lo + i * P:lo + (i + 1) * P]

                pe.wait_ge(rows.sem, rows.at("layer", "twice", l))
                turn_rows("nsc", [pair(kc_twice, 0, i) for i in range(4)], l)
                pe.wait_ge(rows.sem, rows.at("layer", "swa", l))
                turn_rows("swa", [pair(swa_r, 0, i) for i in range(4)] + [lambda tb: swa_r[:, tb, 512:640]], l)
                turned("layer", "swa", 3, l)
                attention("layer", SWA_STEPS, qt, kt, lambda s, i, b: proj[:, b, C_AV + HD * (i // 2):C_AV + HD * (i // 2 + 1)], l,
                          filler=gate_product)

                pe.wait_ge(rows.sem, rows.at("layer", "nsa", l))
                turn_rows("nsr", [pair(proj, C_BQ, i) for i in range(4)], l)
                turn_rows("nsq", [pair(nsa_q, 0, i) for i in range(4)]
                          + [lambda tb: nsa_k[:, tb, 0:P], lambda tb: nsa_k[:, tb, P:2 * P]], l)
                w = ring[:, PLACE["layer", "cmp"][0], 0:2 * 16 * HD].rearrange("p (v j n) -> p v j n", v=2, j=16)
                chunk(pe, "layer", "cmp", l)
                pe.wait_ge(rows.sem, rows.at("layer", "blk", l))
                claim(X, "cmph", l)
                for v in range(2):
                    for j in range(16):
                        ins = pe.matmul(X.ap[0:HD, v * 2 * CMP:(v + 1) * 2 * CMP], w[:, v, j, :], cmp_blk[:, v, j, :], start=j == 0, stop=j == 15)
                ins.then_inc(X.full, 1)
                used["layer", "cmp"] = (X, "cmph")
                pe.wait_ge(rows.sem, rows.at("layer", "hcv", l))
                claim(O, "cmpkv", l)
                pe.matmul(O.ap[:, 0:2 * CMP], w2_k[:, :, :].rearrange("p a b -> p (a b)"),
                          cmp_h[:, 2, :, :].rearrange("p g n -> p (g n)"), start=True, stop=True)
                pe.matmul(O.ap[:, 64:64 + HD], cmp_hv[:, :, :, :].rearrange("p g h n -> p (g h n)"), w2_v[:, :], start=True, stop=True)\
                    .then_inc(O.full, 1)
                pe.wait_ge(O.free, O.nth("layer", "cmpkv", l))
                turned("layer", "nsr", 2, l)
                for qb in range(TB):
                    tag = f"cmp0{qb}"
                    claim(S, tag, l)
                    for h in range(HEADS):
                        f, pr = divmod(h, 4)
                        ins = pe.matmul(S.ap[:, f * HALF + pr * CMP:f * HALF + (pr + 1) * CMP], qt[f * HD:(f + 1) * HD, pr, qb * P:(qb + 1) * P],
                                        cmp_k[f * HD:(f + 1) * HD, f * CMP:(f + 1) * CMP], start=True, stop=True)
                    ins.then_inc(S.full, 1)
                for qb in range(TB):
                    tag = f"cmp0{qb}"
                    n = masked.parts["layer"].index(tag)
                    pe.wait_ge(probs.sem, probs.at("layer", tag, l))
                    claim(PT, tag, l)
                    pe.transpose(PT.ap[:, 0:P], scores[:, n % 2, 0, 0:P], ident[:, :]).then_inc(PT.full, 1)
                    claim(O, tag, l)
                    pe.wait_ge(PT.free, PT.nth("layer", tag, l))
                    pe.matmul(O.ap[:, :], probs_t[:, 0, 0, :], cmp_v[:, :, :].rearrange("p h d -> p (h d)"), start=True, stop=True)\
                        .then_inc(O.full, 1)
                turned("layer", "nsq", 3, l)
                attention("layer", SEL_STEPS, qt[:, 4:8, :], kt[:, 0:1, :],
                          lambda s, i, b: proj[:, b, C_VS + HD * (i // 2):C_VS + HD * (i // 2 + 1)], l, filler=gate_product)
                attention("layer", WIN_STEPS, qt[:, 4:8, :], kt[:, 1:2, :],
                          lambda s, i, b: proj[:, b, C_VW + HD * (i // 2):C_VW + HD * (i // 2 + 1)], l)

                pe.wait_ge(rows.sem, rows.at("layer", "mk", l))
                turn_rows("mq", [lambda tb, h=h: mla_q[:, tb, h * MLA_QK:(h + 1) * MLA_QK] for h in range(HEADS)], l, MLA_QK)
                turn_rows("mk", [lambda tb, h=h: mla_k[:, tb, h * MLA_QK:(h + 1) * MLA_QK] for h in range(HEADS)], l, MLA_QK)
                turned("layer", "mk", 4, l)
                attention("layer", MLA_STEPS, qt, kt, lambda s, i, b: kv_rows[:, b, (4 * s[1] + i) * P + HD:(4 * s[1] + i + 1) * P], l)

                for name, src in (("a", o_a), ("b", o_b), ("c", o_c)):
                    if name == "b":
                        pe.wait_ge(rows.sem, rows.at("layer", "ob", l))
                    else:
                        pe.wait_ge(O.free, O.nth("layer", step_tag((SWA_STEPS if name == "a" else MLA_STEPS)[-1]), l))
                    turn_rows(f"o{name}", [lambda tb, k=k, s=src: s[:, tb, k * P:(k + 1) * P] for k in range(KF)], l)
                    turned("layer", f"o{name}", 2, l)
                    product_wide("layer", f"br{name}", o_t, l)
                pe.wait_ge(rows.sem, rows.at("layer", "merged", l))
                turn_rows("mg", [lambda tb, k=k: merged[:, tb, k * P:(k + 1) * P] for k in range(KD)], l)
                turned("layer", "mg", 4, l)
                for name in ["out0", "out1"]:
                    product_rows("layer", name, name, h_t, keys(chunk(pe, "layer", name, l), KD, HALF), KD, 0, HALF, l)

                pe.wait_ge(rows.sem, rows.at("layer", "mem", l))
                turn_rows("mem", [lambda tb, k=k: mem_rows[:, tb, k * P:(k + 1) * P] for k in range(KD)], l)
                turned("layer", "mem", 4, l)
                product_turned("layer", "memk", "memk", mem_t, keys(chunk(pe, "layer", "memk", l), KD, HALF), KD, l)
                product_rows("layer", "memv", "memv", mem_t, keys(chunk(pe, "layer", "memv", l), KD, HALF), KD, 0, HALF, l)
                pe.wait_ge(rows.sem, rows.at("layer", "xattn", l))
                turn_rows("hx", [lambda tb, k=k: h_rows[:, tb, k * P:(k + 1) * P] for k in range(KD)], l)
                turned("layer", "hx", 4, l)
                product_turned("layer", "xq", "xq", h_t, keys(chunk(pe, "layer", "xq", l), KD, HALF), KD, l)
                for b in G:
                    pe.wait_ge(b.free, b.nth("layer", "xq", l))
                attention("layer", X_STEPS, qt, kt, lambda s, i, b: mem_v[:, b, i * XD:(i + 1) * XD], l, XD)
                pe.wait_ge(O.free, O.nth("layer", step_tag(X_STEPS[-1]), l))
                turn_rows("ox", [lambda tb, k=k: o_a[:, tb, k * P:(k + 1) * P] for k in range(KF)], l)
                turned("layer", "ox", 2, l)
                product_wide("layer", "xo", o_t, l)

                pe.wait_ge(rows.sem, rows.at("layer", "ffn", l))
                turn_rows("hf", [lambda tb, k=k: h_rows[:, tb, k * P:(k + 1) * P] for k in range(KD)], l)
                turned("layer", "hf", 4, l)
                for c in range(KFF // 2):
                    product_turned("layer", f"gu{c}", f"gu{c}", h_t, keys(chunk(pe, "layer", f"gu{c}", l), KD, HALF), KD, l)
                claim(S, "ffd", l)
                claim(PT, "ffd", l)
                for c in range(6):
                    w = keys(chunk(pe, "layer", f"fd{c}", l), KF, D)
                    for k in range(4 * c, min(4 * c + 4, KFF)):
                        if k % 2 == 0:
                            pe.wait_ge(G1.free, G1.nth("layer", f"gu{k // 2}", l))
                        for tb, b in enumerate((S, PT)):
                            for half in range(2):
                                ins = pe.matmul(b.ap[:, half * HALF:(half + 1) * HALF], ff_t[:, k, tb * P:(tb + 1) * P],
                                                w[:, k - 4 * c, half * HALF:(half + 1) * HALF], start=k == 0, stop=k == KFF - 1)
                            if k == KFF - 1:
                                ins.then_inc(b.full, 1)
                    if c < 5:
                        ins.then_inc(ff_used, 1)
                        used["layer", f"fd{c}"] = (ff_used, lambda rnd, c=c: 5 * rnd + c + 1)
                used["layer", "fd5"] = (PT, "ffd")
            end(LAYERS)

        @block.sync
        def _(sync):
            last = [None] * SLOTS

            def sources(part, name, rnd):
                def cols(w, lo, n):
                    return w.rearrange("(k p) n -> p k n", p=P)[:, :, lo:lo + n]
                if part == "first":
                    if name.startswith("mod"):
                        return [t["w_mod"][0].rearrange("(p k) n -> p k n", p=P)[:, :, int(name[3:]) * HALF:(int(name[3:]) + 1) * HALF]]
                    if name == "dtf":
                        return [cols(t["w_in"][0], OFF_DT, SSD_HEADS), cols(t["w_in"][0], OFF_F, FOX_HEADS)]
                    if name == "att":
                        return [cols(t["w_att_o"][0], 0, D)]
                    i = int(name[-1]) if name[-1].isdigit() else 0
                    w, off = {"xbc": ("w_in", OFF_XBC), "q": ("w_in", OFF_Q), "k": ("w_in", OFF_K), "v": ("w_in", OFF_V), "z": ("w_in", OFF_Z),
                              "ga": ("w_in", OFF_GA), "gs": ("w_in", OFF_GS), "so": ("w_ssd_o", 0), "o": ("w_o", 0)}[name.rstrip("0123456789")]
                    return [cols(t[w][0], off + i * HALF, HALF)]
                i = int(name[-1]) if name[-1].isdigit() else 0
                if name.startswith("in"):
                    return [cols(t["w_in_2"][rnd], IN_AT[i], IN_AT[i + 1] - IN_AT[i])]
                if name.startswith("gu"):
                    i = int(name[2:])
                    return [cols(t["w_gate_up_2"][rnd], i * SEQ, SEQ), cols(t["w_gate_up_2"][rnd], D_FF + i * SEQ, SEQ)]
                if name.startswith("g"):
                    return [cols(t["w_in_2"][rnd], C_G + i * HALF, HALF)]
                if name == "cmp":
                    return [t[w][rnd].rearrange("(j p) n -> p j n", p=P) for w in ("nsa_wk1_2", "nsa_wv1_2")]
                if name.startswith("fd"):
                    return [cols(t["w_down_2"][rnd][i * HALF:min((i + 1) * HALF, D_FF), :], 0, D)]
                w, lo, n = {"qb": ("mla_w_q_b_2", 0, HEADS * MLA_QK), "kvb": ("mla_w_kv_b_2", 0, D), "bra": ("w_br_a_2", 0, D),
                            "brb": ("w_br_b_2", 0, D), "brc": ("w_br_c_2", 0, D), "out": ("w_out_2", i * HALF, HALF),
                            "memk": ("w_xkv_2", 0, HALF), "memv": ("w_xkv_2", HALF, HALF), "xq": ("w_xq_2", 0, HALF),
                            "xo": ("w_xo_2", 0, D)}[name.rstrip("0123456789")]
                return [cols(t[w][rnd], lo, n)]

            PAIRED = ("in0", "in2")

            def load(part, name, rnd=0):
                slot, before = PLACE[part, name][0], last[PLACE[part, name][0]]
                if before:
                    where, use = used[before[0], before[1]]
                    if isinstance(where, Bank):
                        sync.wait_ge(where.full, where.nth(before[0], use, before[2]))
                    else:
                        sync.wait_ge(where, use(before[2]))
                pieces = sources(part, name, rnd)
                if name == "cmp":
                    dst = ring[:, slot, 0:2 * 16 * HD].rearrange("p (v j n) -> p v j n", v=2, j=16)
                    dsts = [dst[:, 0], dst[:, 1]]
                elif part == "layer" and name in PAIRED:
                    dst = ring[:, slot, :].rearrange("p (k r f d) -> p k f r d", k=KD, f=2, d=HD)
                    src = pieces[0].rearrange("p k (f r d) -> p k f r d", f=2, d=HD)
                    dsts, pieces = ([v[:, k, f] for k in range(KD) for f in range(2)] for v in (dst, src))
                else:
                    n = sum(s.shape[2] for s in pieces)
                    dst = ring[:, slot, 0:pieces[0].shape[1] * n].rearrange("p (k n) -> p k n", n=n)
                    at_n = np.cumsum([0] + [s.shape[2] for s in pieces])
                    dsts = [dst[:, :, int(at_n[j]):int(at_n[j + 1])] for j in range(len(pieces))]
                for d, s in zip(dsts, pieces):
                    sync.dma_start(d, s).then_inc(landed[slot], 16)
                last[slot] = (part, name, rnd)

            for name in FIRST_CHUNKS:
                load("first", name)
            for name, use, rnd in last:
                where, what = used[name, use]
                sync.wait_ge(where.full, where.nth(name, what, rnd))

            done_with = {"gate0": (expert_used, lambda q: q * 3 + 2), "up0": (M0.full, lambda q: M0.nth("moe", "hidden0", q)),
                         "gate1": (expert_used, lambda q: q * 3 + 3), "up1": (M1.full, lambda q: M1.nth("moe", "hidden1", q)),
                         "down0": (expert_used, lambda q: q * 3 + 4), "down1": (MX.full, lambda q: MX.nth("moe", "out", q))}

            def load_pair(p, q):
                for j, name in enumerate(PAIR_CHUNKS):
                    where, count = done_with[PAIR_CHUNKS[(j + SLOTS) % (2 * SLOTS)]]
                    sync.wait_ge(where, count(q if j >= SLOTS else q - 1))
                    w = t[f"w_{name[:-1]}"][0, p * 2 + int(name[-1])].rearrange("(k p) n -> p k n", p=P)
                    dst = ring[:, j % SLOTS, :].rearrange("p (k n) -> p k n", n=w.shape[2])
                    sync.dma_start(dst, w).then_inc(expert_landed[j % SLOTS], 16)

            with sync.Fori(0, PAIRS) as p:
                load_pair(p, p)
            sync.wait_ge(rounds_ready, 1)
            n_rounds = sync.value_load(rounds_i[0:1, 0:1], min_val=1, max_val=ROUNDS)
            with sync.If(n_rounds > 1):
                with sync.Fori(1, n_rounds) as again:
                    with sync.Fori(0, PAIRS) as p:
                        load_pair(p, again * PAIRS + p)
            for s in range(SLOTS):
                where, count = done_with[PAIR_CHUNKS[SLOTS + s]]
                used["moe", f"slot{s}"] = (where, lambda rnd, count=count: count(n_rounds * PAIRS - 1))
                last[s] = ("moe", f"slot{s}", 0)
            for rnd in range(LAYERS):
                for name in LAYER_CHUNKS:
                    load("layer", name, rnd)
            sync.wait_ge(out_ready, 1)
            sync.dma_start(out[0].rearrange("(b p) n -> p b n", p=P), h_rows[:, :, :]).then_inc(stored, 16)
            sync.wait_ge(stored, 16)

        @block.gpsimd
        def _(pool):
            st = Steps(pool, pool_steps)
            st.done(pool.memset(ident[:, :], 0.0))
            st.done(pool.memset(tri[:, :], 1.0))
            st.done(pool.memset(causal[:, :], 0.0))
            st.done(pool.memset(cmp_mask[:, :, :], 0.0))
            st.done(pool.memset(head_of[:, :], 1.0))
            st.done(pool.memset(half_power[:, :], -0.5))
            st.done(pool.memset(xbc_pad[:, :, 0:CONV_K - 1], 0.0))
            st.settle()
            for i in range(HD // 2):
                st.done(pool.memset(inv_freq[:, i:i + 1], float(np.float32(10000.0) ** np.float32(-i / (HD // 2)))))
            for i in range(PER_GROUP):
                st.done(pool.memset(back[:, i:i + 1], float(PER_GROUP - i)))
            st.done(pool.affine_select(out=ident[:, :], in_=ident[:, :], compare_op=ALU.not_equal, fill=1.0, base=0,
                                       pattern=[[-1, P]], channel_multiplier=1))
            st.done(pool.affine_select(out=tri[:, :], in_=tri[:, :], compare_op=ALU.is_ge, fill=0.0, base=0,
                                       pattern=[[1, SEQ]], channel_multiplier=-1))
            st.done(pool.affine_select(out=causal[:, :], in_=causal[:, :], compare_op=ALU.is_ge, fill=MASKED, base=P,
                                       pattern=[[-1, SEQ]], channel_multiplier=1))
            st.done(pool.affine_select(out=cmp_mask[:, :, :], in_=cmp_mask[:, :, :], compare_op=ALU.is_ge, fill=MASKED,
                                       base=1 - CMP_BLOCK, pattern=[[P, TB], [-CMP_STRIDE, CMP]], channel_multiplier=1))
            st.done(pool.affine_select(out=head_of[:, :], in_=head_of[:, :], compare_op=ALU.is_ge, fill=0.0, base=0,
                                       pattern=[[-CMP, HEADS]], channel_multiplier=1))
            st.settle()
            st.done(pool.affine_select(out=windowed[:, :], in_=causal[:, :], compare_op=ALU.is_ge, fill=MASKED, base=-1,
                                       pattern=[[1, SEQ]], channel_multiplier=-1))
            st.done(pool.affine_select(out=head_of[:, :], in_=head_of[:, :], compare_op=ALU.is_ge, fill=0.0, base=CMP - 1,
                                       pattern=[[CMP, HEADS]], channel_multiplier=-1))
            st.settle()
            pool.sem_inc(consts, 1)

            def root(part, name, rnd=0):
                pool.wait_ge(var_ready.sem, var_ready.at(part, name, rnd))
                pool.tensor_tensor(rstd[:, :], var_in[:, :], half_power[:, :], ALU.pow).then_inc(rstd_ready.sem, 1)

            root("first", "h")
            for i in range(TB * SSD_GROUPS):
                b = G[i % SSD_GROUPS % 2]
                pool.wait_ge(b.free, b.nth("first", f"seg{i // SSD_GROUPS}{i % SSD_GROUPS}"))
                pool.affine_select(out=decay[:, i], in_=decay[:, i], compare_op=ALU.is_ge, fill=-MASKED, base=0,
                                   pattern=[[0, SSD_R], [1, P]], channel_multiplier=-1).then_inc(seg_cut, 1)
            for name in ["gy", "ln1", "h2"]:
                root("first", name)
            root("mid", "ln2")
            with pool.Fori(0, LAYERS) as l:
                for name in var_ready.parts["layer"]:
                    root("layer", name, l)
            root("last", "out")

        @block.scalar
        def _(act):
            st = Steps(act, act_steps)
            act.dma_start(c_col[:, :], t["c"].rearrange("a (p k) -> p (a k)", p=P)).then_inc(in_c, 16)
            act.dma_start(stage[0:64, :], t["conv_w"][0].rearrange("j (t p) -> (j t) p", p=P)).then_inc(in_stage, 16)
            act.dma_start(stage[64:80, :], t["conv_b"][0].rearrange("(t p) -> t p", p=P)).then_inc(in_stage, 16)
            act.dma_start(stage[80:88, :], t["ssd_norm_w"][0].rearrange("(t p) -> t p", p=P)).then_inc(in_stage, 16)
            act.dma_start(b_mod[0:1, :, :].rearrange("p a n -> p (a n)"), t["b_mod"]).then_inc(in_small, 16)
            act.dma_start(x_rows[:, :, :], t["x"][0].rearrange("(b p) n -> p b n", p=P)).then_inc(in_x, 16)
            for dst, src in ((bias24[:, 0:SSD_HEADS], "dt_bias"), (bias24[:, SSD_HEADS:], "forget_b"), (a_log_b[:, :], "a_log"),
                             (d_skip_b[:, :], "d_skip"), (route_b[:, 0:N_GROUPS], "b_router_group"), (route_b[:, N_GROUPS:], "b_router_expert")):
                act.dma_start(dst, t[src].broadcast_to([P, dst.shape[1]])).then_inc(in_vec, 16)
            act.dma_start(pos_i[:, :], t["positions_2"].rearrange("a (b p) -> p (a b)", p=P)).then_inc(in_vec, 16)
            act.dma_start(route_w[:, :, 0:N_GROUPS], t["w_router_group"][0].rearrange("(k p) n -> p k n", p=P)).then_inc(in_route, 16)
            act.dma_start(route_w[:, :, N_GROUPS:], t["w_router_expert"][0].rearrange("(k p) n -> p k n", p=P)).then_inc(in_route, 16)

            def copy_turned(part, tag, n, dst, rnd=0, size=P):
                for r in range(n):
                    b = (X, O)[r % 2]
                    d = dst(r)
                    act.wait_ge(b.full, b.nth(part, f"{tag}{r}", rnd))
                    act.activation(d, b.ap[0:size, 0:d.shape[1] * SEQ].rearrange("p (k n) -> p k n", n=SEQ), ACT.Copy).then_inc(b.free, 1)

            def take(part, name, dst, func=ACT.Copy, scale=1.0, rnd=0):
                for i, b in enumerate(G):
                    d = dst(i)
                    act.wait_ge(b.full, b.nth(part, name, rnd))
                    src = b.ap[:, 0:d.free_size()]
                    if len(d.shape) == 3:
                        src = src.rearrange("p (a n) -> p a n", n=d.shape[2])
                    act.activation(d, src, func, scale=scale).then_inc(b.free, 1)

            def square_rows(part, name, src, junk, rnd=0):
                act.activation(junk(0), src(0), ACT.Square, accum_out=square_sum[:, 0:1])
                act.activation(junk(1), src(1), ACT.Square, accum_out=square_sum[:, 1:2]).then_inc(squares.sem, 1)

            def softmax_step(part, step, rnd=0, filler=None):
                tag, nk = step_tag(step), keys_of(step)
                n = masked.parts[part].index(tag)
                act.wait_ge(masked.sem, masked.at(part, tag, rnd))
                if step[0] == "swa":
                    act.activation(sink_e[:, n % 2, 4:8], sink_e[:, n % 2, 0:4], ACT.Exp)
                for i in range(4):
                    s = scores[:, n % 2, i, 0:nk]
                    ins = act.activation(s, s, ACT.Exp, bias=neg_max[:, n % 2, i:i + 1], scale=-1.0, accum_out=den[:, n % 2, i:i + 1])
                ins.then_inc(probs.sem, 1)
                if filler:
                    filler()
                kb = nk // P
                act.wait_ge(PT.full, PT.nth(part, tag, rnd))
                act.activation(probs_t[:, :, 0:kb, :], PT.ap[:, :].rearrange("p (i b n) -> p i b n", i=4, b=2)[:, :, 0:kb, :], ACT.Copy)\
                    .then_inc(PT.free, 1)

            act.wait_ge(in_c, 16)
            act.activation(c_act[:, :], c_col[:, :], ACT.Tanh, scale=0.5).then_inc(c_tanh, 1)
            act.wait_ge(angle_ready, 1)
            act.activation(angle[:, 0:2], angle[:, 0:2], ACT.Sin).then_inc(sines_ready, 1)
            copy_turned("first", "h", 4, lambda r: h_t[:, 2 * r:2 * r + 2, :])

            def conv_gate(c):
                act.wait_ge(conv_done, c + 1)
                act.activation(conv_tanh[:, 4 * c:4 * c + 4, :], conv[:, 4 * c:4 * c + 4, :], ACT.Tanh).then_inc(conv_tanhed, 1)

            for i in range(4):
                take("first", f"xbc{i}", lambda j, i=i: xbc_pad[:, 4 * i + 2 * j:4 * i + 2 * j + 2, CONV_K - 1:])
                if i == 0:
                    act.wait_ge(sp_abs, 1)
                    act.activation(a_log_b[:, :], a_log_b[:, :], ACT.Exp)
                    act.activation(sp[:, 1], sp[:, 1], ACT.Exp, scale=-1.0).then_inc(sp_exp, 1)
                    act.wait_ge(sp_one, 1)
                    act.activation(sp[:, 3], sp[:, 2], ACT.Ln).then_inc(sp_ln, 1)
                else:
                    conv_gate(i - 1)
            take("first", "q", lambda j: q_t[:, 2 * j:2 * j + 2, :])
            conv_gate(3)
            take("first", "k", lambda j: k_t[:, 2 * j:2 * j + 2, :])
            take("first", "v", lambda j: v_rows[:, j, :])
            for i in range(2):
                for tb, b in enumerate(G):
                    act.wait_ge(b.full, b.nth("first", f"z{i}"))
                    act.activation(z_silu[:, tb, i * HALF:(i + 1) * HALF], b.ap[:, :], ACT.Tanh, scale=0.5).then_inc(z_tanhed, 1)
            for name, dst in (("ga", gate_att), ("gs", gate_ssd)):
                for i in range(2):
                    take("first", f"{name}{i}", lambda tb, d=dst, i=i: d[:, tb, i * HALF:(i + 1) * HALF], ACT.Tanh, 0.5)
            for step in FOX_STEPS:
                softmax_step("first", step)
            copy_turned("first", "fox", 2, lambda r: fox_ot[:, 2 * r:2 * r + 2, :])
            act.wait_ge(X.free, X.nth("first", "sums"))
            act.activation(dt_a[:, 3], dt_a[:, 2], ACT.Exp)
            act.activation(dt_a[:, 4], dt_a[:, 4], ACT.Exp).then_inc(sums_exp, 1)
            act.wait_ge(O.full, O.nth("first", "b_rows"))
            act.activation(b_rows[:, :, :], O.ap[:, :].rearrange("p (g n) -> p g n", n=SSD_N), ACT.Copy).then_inc(O.free, 1)
            for i in range(TB * SSD_GROUPS):
                act.wait_ge(seg_cut, i + 1)
                act.activation(decay[:, i], decay[:, i], ACT.Exp).then_inc(seg_exp, 1)
            act.wait_ge(S.full, S.nth("first", "states"))
            act.activation(states[:, :, :], S.ap[:, :].rearrange("p (g n) -> p g n", n=SSD_R * SSD_P), ACT.Copy).then_inc(S.free, 1)
            act.wait_ge(gy_ready, 1)
            square_rows("first", "gy", lambda tb: ssd_y[:, tb, :], lambda tb: z_silu[:, tb, :])
            copy_turned("first", "mg", 4, lambda r: h_t[:, 2 * r:2 * r + 2, :])
            for i, name in enumerate(["ln1_g", "ln1_b", "ln2_g", "ln2_b"]):
                act.dma_start(ln_rows[:, i, :], t[name].broadcast_to([P, D])).then_inc(in_ln, 16)
            copy_turned("first", "h2", 4, lambda r: h_t[:, 2 * r:2 * r + 2, :])
            act.wait_ge(route_in, 1)
            act.activation(rt_s[:, 1], rt_s[:, 0], ACT.Exp).then_inc(route_out, 1)
            act.wait_ge(route_in, 2)
            act.activation(rt_s[:, 12, :, 1:2], rt_s[:, 12, :, 0:1], ACT.Exp).then_inc(route_out, 1)

            def take_tokens(at_q):
                for j, b in enumerate((MO, MX)):
                    act.wait_ge(b.full, at_q)
                    act.activation(taken_t[:, 4 * j:4 * j + 4, :], b.ap[:, :].rearrange("p (k n) -> p k n", n=P), ACT.Copy).then_inc(b.free, 1)

            act.wait_ge(rounds_ready, 1)
            n_pairs = act.value_load(rounds_i[0:1, 1:2], min_val=PAIRS, max_val=PAIRS * ROUNDS)
            take_tokens(MO.nth("start", "taken"))
            with act.Fori(0, n_pairs) as q:
                for e, b in enumerate((M0, M1)):
                    act.wait_ge(b.full, b.nth("moe", f"hidden{e}", q))
                    act.activation(expert_t[:, e, :], b.ap[:, 0:KF * SLOT_TOKENS], ACT.Tanh, scale=0.5).then_inc(expert_tanhed, 1)
                act.wait_ge(M0.full, M0.nth("moe", "turned", q))
                act.activation(pick_t[:, 0, :], M0.ap[:, 0:SEQ], ACT.Copy).then_inc(M0.free, 1)
                take_tokens(MO.nth("moe", "taken", q))
                for half, b in enumerate((MO, MX)):
                    act.wait_ge(b.full, b.nth("moe", "out", q))
                    act.activation(pair_y[:, 0, half * HALF:(half + 1) * HALF], b.ap[:, :], ACT.Copy).then_inc(b.free, 1)

            with act.Fori(0, LAYERS) as l:
                for lo, name, n in ((G_MIX, "norm_mix_2", KD), (G_XATTN, "norm_xattn_2", KD), (G_MEM, "norm_mem_2", KD), (G_FFN, "norm_ffn_2", KD),
                                    (G_QN, "mla_q_norm_2", 3), (G_KVN, "mla_kv_norm_2", 2)):
                    act.dma_start(stage[lo:lo + n, :], t[name][l].rearrange("(t p) -> t p", p=P)).then_inc(in_layer, 16)
                for lo, name in ((G_PEK, "nsa_pe_k_2"), (G_PEV, "nsa_pe_v_2")):
                    act.dma_start(stage[lo:lo + 16, :], t[name][l].rearrange("(j a) d -> j (a d)", a=2)).then_inc(in_layer, 16)
                act.dma_start(sink_neg[:, :], t["swa_sinks_2"][l].rearrange("(a n) -> a n", a=1).broadcast_to([P, HEADS])).then_inc(in_layer, 16)
                act.dma_start(w2[:, 0, :], t["nsa_wk2_2"][l]).then_inc(in_layer, 16)
                act.dma_start(w2[:, 1, :], t["nsa_wv2_2"][l]).then_inc(in_layer, 16)
                act.wait_ge(x_ready.sem, x_ready.start["layer"] + l)
                square_rows("layer", "mix", lambda tb: x_rows[:, tb, :], lambda tb: h_rows[:, tb, :], l)
                for i in range(6):
                    take("layer", f"in{i}", lambda tb, a=IN_AT[i], b=IN_AT[i + 1]: proj[:, tb, a:b], rnd=l)
                for b in G:
                    act.wait_ge(b.free, b.nth("layer", "in5", l))
                square_rows("layer", "qn", lambda tb: proj[:, tb, C_QA:C_KV], lambda tb: lat[:, tb, 0:MLA_Q], l)
                act.wait_ge(var_ready.sem, var_ready.at("layer", "qn", l))
                square_rows("layer", "kvn", lambda tb: proj[:, tb, C_KV:C_KR], lambda tb: lat[:, tb, MLA_Q:], l)
                act.activation(branch_g[:, :, :], proj[:, :, C_BG:C_QA], ACT.Tanh, scale=0.5).then_inc(bg_tanhed, 1)

                def take_gate(name):
                    i = int(name[1:])
                    take("layer", name, lambda tb: gate_t[:, tb, i * HALF:(i + 1) * HALF], ACT.Tanh, 0.5, l)

                take_gate("g0")
                take("layer", "qb0", lambda tb: mla_q[:, tb, 0:HALF], rnd=l)
                take("layer", "qb1", lambda tb: mla_q[:, tb, HALF:], rnd=l)
                take("layer", "kvb0", lambda tb: kv_rows[:, tb, 0:HALF], rnd=l)
                take("layer", "kvb1", lambda tb: kv_rows[:, tb, HALF:], rnd=l)

                def steps(which):
                    for step in which:
                        name = FILLERS.get(step)
                        softmax_step("layer", step, l, (lambda: take_gate(name)) if name else None)

                copy_turned("layer", "nsc", 2, lambda r: kc_t[:, r, :, 0:SEQ], l)
                copy_turned("layer", "swa", 3, lambda r: qt[:, 2 * r:2 * r + 2, :] if r < 2 else kt[:, 0:1, :], l)
                steps(SWA_STEPS)
                copy_turned("layer", "nsr", 2, lambda r: qt[:, 2 * r:2 * r + 2, :], l)
                copy_turned("layer", "nsq", 3, lambda r: qt[:, 4 + 2 * r:6 + 2 * r, :] if r < 2 else kt[:, 0:2, :], l)
                act.wait_ge(X.full, X.nth("layer", "cmph", l))
                act.activation(cmp_h[:, 0:2].rearrange("p v g n -> p (v g n)"), X.ap[0:HD, 0:4 * CMP], ACT.Tanh, scale=0.5).then_inc(cmp_tanhed, 1)
                for qb in range(TB):
                    tag = f"cmp0{qb}"
                    n = masked.parts["layer"].index(tag)
                    act.wait_ge(masked.sem, masked.at("layer", tag, l))
                    act.activation(scores[:, n % 2, 0, 0:P], scores[:, n % 2, 0, 0:P], ACT.Exp, scale=-1.0).then_inc(cmp_exp, 1)
                for qb in range(TB):
                    act.wait_ge(PT.full, PT.nth("layer", f"cmp0{qb}", l))
                    act.activation(probs_t[:, 0, 0, :], PT.ap[:, 0:P], ACT.Copy).then_inc(PT.free, 1)
                steps(SEL_STEPS + WIN_STEPS)
                copy_turned("layer", "mq", 4, lambda r: qt[0:MLA_QK, 2 * r:2 * r + 2, :], l, MLA_QK)
                copy_turned("layer", "mk", 4, lambda r: kt[0:MLA_QK, 2 * r:2 * r + 2, :], l, MLA_QK)
                steps(MLA_STEPS)
                act.wait_ge(O.full, O.nth("layer", step_tag(MLA_STEPS[-1]), l))
                act.dma_start(mem_rows[:, :, :], t["mem_2"][0].rearrange("(b p) n -> p b n", p=P)).then_inc(in_mem, 16)
                for name in "abc":
                    copy_turned("layer", f"o{name}", 2, lambda r: o_t[:, 2 * r:2 * r + 2, :], l)
                copy_turned("layer", "mg", 4, lambda r: h_t[:, 2 * r:2 * r + 2, :], l)
                act.wait_ge(in_mem, 16 + l * 16)
                square_rows("layer", "mem", lambda tb: mem_rows[:, tb, :], lambda tb: mem_t[:, :, :].rearrange("p k n -> p (k n)")[:, tb * D:(tb + 1) * D], l)
                take("layer", "memk", lambda j: kt[:, 2 * j:2 * j + 2, :], rnd=l)
                take("layer", "memv", lambda tb: mem_v[:, tb, :], rnd=l)
                for b in G:
                    act.wait_ge(b.free, b.nth("layer", "out1", l))
                square_rows("layer", "xattn", lambda tb: x_rows[:, tb, :], lambda tb: h_rows[:, tb, :], l)
                take("layer", "xq", lambda j: qt[:, 2 * j:2 * j + 2, :], rnd=l)
                steps(X_STEPS)
                copy_turned("layer", "ox", 2, lambda r: o_t[:, 2 * r:2 * r + 2, :], l)
                for b in G:
                    act.wait_ge(b.free, b.nth("layer", "xo1", l))
                square_rows("layer", "ffn", lambda tb: x_rows[:, tb, :], lambda tb: h_rows[:, tb, :], l)
                for c in range(KFF // 2):
                    act.wait_ge(G0.full, G0.nth("layer", f"gu{c}", l))
                    act.activation(ff_tmp[:, c % 2, :], G0.ap[:, :], ACT.Tanh, scale=0.5).then_inc(gate_tanhed, 1)
            act.wait_ge(x_ready.sem, x_ready.total)
            square_rows("last", "out", lambda tb: x_rows[:, tb, :], lambda tb: h_rows[:, tb, :])
            act.dma_start(x_gain[:, :], t["norm_final_2"].rearrange("(a n) -> a n", a=1).broadcast_to([P, D])).then_inc(in_ln, 16)

        @block.vector
        def _(dve):
            st = Steps(dve, dve_steps)

            def over(v, n):
                return v.unsqueeze(2).broadcast_to([v.shape[0], v.shape[1], n])

            def across(v, n):
                return v.unsqueeze(1).broadcast_to([v.shape[0], n, v.shape[1]])

            def gain_turned(part, tag, tiles, dst, gains, rnd=0):
                for r in range((tiles + 1) // 2):
                    b, n = (X, O)[r % 2], min(2, tiles - 2 * r)
                    dve.wait_ge(b.full, b.nth(part, f"{tag}{r}", rnd))
                    dve.tensor_tensor(dst[:, 2 * r:2 * r + n, :], b.ap[:, 0:n * SEQ].rearrange("p (k n) -> p k n", n=SEQ),
                                      over(gains[:, 2 * r:2 * r + n], SEQ), ALU.mult).then_inc(b.free, 1)

            def rms_rows(part, name, n, eps, src, dst, rnd=0):
                dve.wait_ge(squares.sem, squares.at(part, name, rnd))
                dve.tensor_scalar(var_in[:, :], square_sum[:, :], 1.0 / n, eps, ALU.mult, ALU.add).then_inc(var_ready.sem, 1)
                dve.wait_ge(rstd_ready.sem, rstd_ready.at(part, name, rnd))
                for tb in range(TB):
                    ins = dve.tensor_scalar(dst(tb), src(tb), rstd[:, tb:tb + 1], None, ALU.mult)
                return ins

            def layer_norm(part, name, src, dst):
                for tb in range(TB):
                    for half in range(2):
                        st.done(dve.bn_stats(bn[:, tb, half, :], src[:, tb, half * HALF:(half + 1) * HALF]))
                st.settle()
                for tb in range(TB):
                    st.done(dve.bn_aggr(mean_var[:, tb, :], bn[:, tb, :, :].rearrange("p a b -> p (a b)")))
                st.settle()
                dve.tensor_scalar(var_in[:, :], mean_var[:, :, 1], LN_EPS, None, ALU.add).then_inc(var_ready.sem, 1)

            def layer_norm_end(part, name, src, dst):
                dve.wait_ge(rstd_ready.sem, rstd_ready.at(part, name))
                for tb in range(TB):
                    st.done(dve.tensor_scalar(dst[:, tb, :], src[:, tb, :], mean_var[:, tb, 0:1], rstd[:, tb:tb + 1], ALU.subtract, ALU.mult))
                st.settle()

            def scale_shift(v, scale, shift):
                st.done(dve.tensor_tensor(v, v, across(scale, TB), ALU.mult))
                st.settle()
                return dve.tensor_tensor(v, v, across(shift, TB), ALU.add)

            def mask_step(part, step, rnd=0):
                kind, pp, qb = step
                tag, nk = step_tag(step), keys_of(step)
                n = masked.parts[part].index(tag)
                scale = {"mla": MLA_QK, "x": XD}.get(kind, HD) ** -0.5
                s4 = S.ap[:, :].rearrange("p (i n) -> p i n", n=SEQ)[:, :, 0:nk]
                dst = scores[:, n % 2, :, 0:nk]
                low = neg_max[:, n % 2, 0:4]
                dve.wait_ge(S.full, S.nth(part, tag, rnd))
                if kind == "x":
                    ins = dve.tensor_scalar(dst, s4, -scale, None, ALU.mult)
                else:
                    m = causal[:, P:SEQ] if qb == 0 else windowed[:, :] if kind == "swa" else causal[:, :]
                    ins = dve.scalar_tensor_tensor(dst, s4, -scale, across(m, 4), ALU.mult, ALU.add)
                ins.then_inc(S.free, 1)
                dve.wait_ge(S.free, S.nth(part, tag, rnd))
                ins = dve.tensor_reduce(low, dst, AX_X, ALU.min)
                if kind == "swa":
                    st.done(ins)
                    st.settle()
                    sink = sink_neg[:, :].rearrange("p (f a r) -> p f a r", f=2, a=2)[:, :, pp, :]
                    low4 = low.rearrange("p (f r) -> p f r", f=2)
                    st.done(dve.tensor_tensor(low4, low4, sink, ALU.min))
                    st.settle()
                    ins = dve.tensor_tensor(sink_e[:, n % 2, 0:4].rearrange("p (f r) -> p f r", f=2), low4, sink, ALU.subtract)
                ins.then_inc(masked.sem, 1)

            def finish_step(part, step, dst, rnd=0, gate=None, width=HD):
                tag = step_tag(step)
                n = masked.parts[part].index(tag)
                total, inv = den[:, n % 2, 0:4], rden[:, n % 2, 0:4]
                dve.wait_ge(probs.sem, probs.at(part, tag, rnd))
                if step[0] == "swa":
                    st.done(dve.tensor_tensor(total, total, sink_e[:, n % 2, 4:8], ALU.add))
                    st.settle()
                st.done(dve.reciprocal(inv, total))
                st.settle()
                if gate is not None:
                    inv4 = inv.rearrange("p (f r) -> p f r", f=2)
                    st.done(dve.tensor_tensor(inv4, inv4, gate, ALU.mult))
                    st.settle()
                dve.wait_ge(O.full, O.nth(part, tag, rnd))
                o4 = O.ap[:, 0:4 * width].rearrange("p (i d) -> p i d", d=width)
                if gate is None:
                    if len(dst.shape) == 4:
                        o4 = o4.rearrange("p (f r) d -> p f r d", f=2)
                        w = over(inv, width).rearrange("p (f r) d -> p f r d", f=2)
                    else:
                        w = over(inv, width)
                    dve.tensor_tensor(dst, o4, w, ALU.mult).then_inc(O.free, 1)
                    return None
                dve.tensor_tensor(o_tmp[:, :, :], o4, over(inv, width), ALU.mult).then_inc(O.free, 1)
                dve.wait_ge(O.free, O.nth(part, tag, rnd))
                return dve.tensor_tensor(dst, dst, o_tmp[:, :, :].rearrange("p (f r) d -> p f r d", f=2), ALU.add)

            def attention(part, steps, dst, rnd=0, gate=None, width=HD, end=None):
                mask_step(part, steps[0], rnd)
                for n, step in enumerate(steps):
                    if n + 1 < len(steps):
                        mask_step(part, steps[n + 1], rnd)
                    ins = finish_step(part, step, dst(step), rnd, gate(step) if gate else None, width)
                    if ins is not None:
                        if end and n == len(steps) - 1:
                            ins.then_inc(end, 1)
                        else:
                            st.done(ins)
                            st.settle()

            def crossed(o):
                return lambda s: o[:, s[2], :].rearrange("p (f a r d) -> p f a r d", f=2, a=2, d=HD)[:, :, s[1], :, :]

            dve.wait_ge(c_tanh, 1)
            st.done(dve.scalar_tensor_tensor(c_act[:, :], c_act[:, :], 1.0, c_col[:, :], ALU.add, ALU.mult))
            st.settle()
            dve.tensor_scalar(c_act[:, :], c_act[:, :], 0.5, None, ALU.mult).then_inc(c_ready, 1)

            dve.wait_ge(consts, 1)
            dve.wait_ge(in_vec, 16 * 7)
            st.done(dve.tensor_copy(pos_f[:, :], pos_i[:, :]))
            st.settle()
            for tb in range(TB):
                st.done(dve.tensor_scalar(angle[:, 2, tb, :], inv_freq[:, :], pos_f[:, tb:tb + 1], None, ALU.mult))
            st.settle()
            for f, (shift, add) in enumerate(((0.0, 0.0), (0.25, float(np.pi / 2)))):
                turns, ang, r = angle[:, 3], angle[:, 2], angle[:, f]
                st.done(dve.tensor_scalar(turns, ang, float(1 / (2 * np.pi)), shift, ALU.mult, ALU.add))
                st.settle()
                st.done(dve.tensor_scalar(turns, turns, ROUND, None, ALU.add))
                st.settle()
                st.done(dve.tensor_scalar(turns, turns, -ROUND, None, ALU.add))
                st.settle()
                for j, part in enumerate(TURN):
                    st.done(dve.scalar_tensor_tensor(r, turns, -part, ang if j == 0 else r, ALU.mult, ALU.add))
                    st.settle()
                st.done(dve.tensor_scalar(r, r, add, None, ALU.add))
                st.settle()
                ins = dve.tensor_scalar(r, r, -PI_IN, PI_IN, ALU.max, ALU.min)
                if f == 0:
                    st.done(ins)
                else:
                    ins.then_inc(angle_ready, 1)
            dve.wait_ge(in_x, 16)
            layer_norm("first", "h", x_rows, h_rows)
            dve.wait_ge(sines_ready, 1)
            hh = HD // 2
            st.done(dve.tensor_copy(rope_c[:, :, 0:hh], angle[:, 1]))
            st.done(dve.tensor_copy(rope_c[:, :, hh:], angle[:, 1]))
            st.done(dve.tensor_scalar(rope_s[:, :, 0:hh], angle[:, 0], -1.0, None, ALU.mult))
            st.done(dve.tensor_copy(rope_s[:, :, hh:], angle[:, 0]))

            dve.wait_ge(X.full, X.nth("first", "conv_col"))
            nc_ = CONV_TILES * (CONV_K + 1)
            st.done(dve.tensor_scalar(conv_col[:, 0:nc_], X.ap[:, 0:nc_], 0.5, None, ALU.mult))
            dve.tensor_copy(conv_col[:, nc_:], X.ap[:, nc_:nc_ + KD]).then_inc(X.free, 1)
            for i, name in enumerate(MOD_CHUNKS):
                b = G[i % 2]
                dve.wait_ge(b.full, b.nth("first", name))
                plus = 0.0 if i // 2 in (0, 3) else 1.0
                dve.tensor_scalar(mod[:, i // 2, i % 2 * HALF:(i % 2 + 1) * HALF], b.ap[:, :], plus, None, ALU.add).then_inc(b.free, 1)
                if i == 3:
                    for b in G:
                        dve.wait_ge(b.free, b.nth("first", MOD_CHUNKS[2 + G.index(b)]))
                    layer_norm_end("first", "h", x_rows, h_rows)
                    scale_shift(h_rows[:, :, :], mod[:, 1, :], mod[:, 0, :]).then_inc(rows.sem, 1)

            for tb, b in enumerate(G):
                dve.wait_ge(b.full, b.nth("first", "dtf"))
                dve.tensor_tensor(sp[:, 0, tb, :], b.ap[:, 0:24], bias24[:, :], ALU.add).then_inc(b.free, 1)
            for b in G:
                dve.wait_ge(b.free, b.nth("first", "dtf"))
            st.done(dve.tensor_scalar(sp[:, 0, :, SSD_HEADS:], sp[:, 0, :, SSD_HEADS:], -1.0, None, ALU.mult))
            st.settle()
            dve.scalar_tensor_tensor(sp[:, 1], sp[:, 0], -1.0, sp[:, 0], ALU.mult, ALU.max).then_inc(sp_abs, 1)
            dve.wait_ge(sp_exp, 1)
            dve.tensor_scalar(sp[:, 2], sp[:, 1], 1.0, None, ALU.add).then_inc(sp_one, 1)
            dve.wait_ge(sp_one, 1)
            st.done(dve.tensor_scalar(sp[:, 4], sp[:, 2], -1.0, None, ALU.add))
            st.settle()
            st.done(dve.tensor_scalar(sp[:, 5], sp[:, 4], 0.0, None, ALU.is_equal))
            st.settle()
            st.done(dve.tensor_tensor(sp[:, 4], sp[:, 4], sp[:, 5], ALU.add))
            st.settle()
            st.done(dve.reciprocal(sp[:, 4], sp[:, 4]))
            st.done(dve.tensor_tensor(sp[:, 5], sp[:, 5], sp[:, 1], ALU.mult))
            st.settle()
            st.done(dve.tensor_tensor(sp[:, 4], sp[:, 4], sp[:, 1], ALU.mult))
            st.settle()
            dve.wait_ge(sp_ln, 1)
            st.done(dve.tensor_tensor(sp[:, 3], sp[:, 3], sp[:, 4], ALU.mult))
            st.settle()
            st.done(dve.tensor_tensor(sp[:, 3], sp[:, 3], sp[:, 5], ALU.add))
            st.settle()
            st.done(dve.scalar_tensor_tensor(sp[:, 5], sp[:, 0], 0.0, sp[:, 3], ALU.max, ALU.add))
            st.settle()
            st.done(dve.tensor_copy(dt_a[:, 0], sp[:, 5, :, 0:SSD_HEADS]))
            st.done(dve.tensor_scalar(sp[:, 5, :, SSD_HEADS:], sp[:, 5, :, SSD_HEADS:], HD ** 0.5, None, ALU.mult))
            st.settle()
            dve.scalar_tensor_tensor(dt_a[:, 1], dt_a[:, 0], -1.0, across(a_log_b[:, :], TB), ALU.mult, ALU.mult).then_inc(forget_ready, 1)

            def conv_gate(c):
                dve.wait_ge(conv_tanhed, c + 1)
                u = conv[:, 4 * c:4 * c + 4, :]
                dve.scalar_tensor_tensor(u, conv_tanh[:, 4 * c:4 * c + 4, :], 1.0, u, ALU.add, ALU.mult).then_inc(conv_ready, 1)

            for c in range(4):
                for b in G:
                    dve.wait_ge(b.free, b.nth("first", f"xbc{c}"))
                for j in range(CONV_K):
                    for tile in range(4 * c, 4 * c + 4):
                        tap = xbc_pad[:, tile, j:j + SEQ]
                        w = conv_col[:, j * CONV_TILES + tile:j * CONV_TILES + tile + 1]
                        if j == 0:
                            bias = conv_col[:, CONV_K * CONV_TILES + tile:CONV_K * CONV_TILES + tile + 1]
                            ins = dve.tensor_scalar(conv[:, tile, :], tap, w, bias, ALU.mult, ALU.add)
                        else:
                            ins = dve.scalar_tensor_tensor(conv[:, tile, :], tap, w, conv[:, tile, :], ALU.mult, ALU.add)
                        if j < CONV_K - 1 or tile < 4 * c + 3:
                            st.done(ins)
                    if j < CONV_K - 1:
                        st.settle()
                ins.then_inc(conv_done, 1)
                if c:
                    conv_gate(c - 1)
            conv_gate(3)
            for i in range(2):
                for tb, b in enumerate(G):
                    z = z_silu[:, tb, i * HALF:(i + 1) * HALF]
                    dve.wait_ge(z_tanhed, 2 * i + tb + 1)
                    dve.scalar_tensor_tensor(z, z, 1.0, b.ap[:, :], ALU.add, ALU.mult).then_inc(b.free, 1)

            attention("first", FOX_STEPS, lambda s: fox_o[:, s[2], s[1] * SEQ:(s[1] + 1) * SEQ].rearrange("p (r f d) -> p f r d", f=2, d=HD))
            for half in range(2):
                for tb, b in enumerate(G):
                    d = gate_att[:, tb, half * HALF:(half + 1) * HALF]
                    dve.wait_ge(b.full, b.nth("first", f"att{half}"))
                    dve.scalar_tensor_tensor(d, d, 1.0, b.ap[:, :], ALU.add, ALU.mult).then_inc(b.free, 1)

            dve.wait_ge(X.full, X.nth("first", "sums"))
            st.done(dve.tensor_copy(dt_a[:, 2], X.ap[:, 0:32].rearrange("p (t h) -> p t h", t=TB)))
            st.settle()
            dve.tensor_tensor(dt_a[:, 4], X.ap[:, 32:64].rearrange("p (t h) -> p t h", t=TB), dt_a[:, 2], ALU.subtract).then_inc(X.free, 1)
            for r in range(4):
                tb, half = divmod(r, 2)
                b = (X, O)[r % 2]
                hs = slice(8 * half, 8 * half + 8)
                src = b.ap[:, :].rearrange("p (h d) -> p h d", d=SSD_P)
                dve.wait_ge(b.full, b.nth("first", f"xs{r}"))
                st.done(dve.tensor_copy(xs[:, tb, hs, :], src))
                dve.tensor_tensor(xdt[:, tb, hs, :], src, over(dt_a[:, 0, tb, hs], SSD_P), ALU.mult).then_inc(b.free, 1)
            dve.wait_ge(sums_exp, 1)
            for b, r in ((X, 2), (O, 3)):
                dve.wait_ge(b.free, b.nth("first", f"xs{r}"))
            dve.tensor_tensor(x_end[:, :, :], xdt[:, 0], over(dt_a[:, 4, 0, :], SSD_P), ALU.mult).then_inc(xdt_ready, 1)
            dve.wait_ge(S.full, S.nth("first", "cb"))
            dve.tensor_copy(cb[:, :, :], S.ap[:, :].rearrange("p (c n) -> p c n", n=P)).then_inc(S.free, 1)
            for i in range(TB * SSD_GROUPS):
                c, g = divmod(i, SSD_GROUPS)
                b = G[g % 2]
                dve.wait_ge(b.full, b.nth("first", f"seg{c}{g}"))
                dve.tensor_tensor(decay[:, i], b.ap[:, :].rearrange("p (r n) -> p r n", n=P),
                                  over(dt_a[:, 2, c, g * SSD_R:(g + 1) * SSD_R], P), ALU.subtract).then_inc(b.free, 1)
            for tb in range(TB):
                st.done(dve.tensor_tensor(ssd_y[:, tb, :].rearrange("p (h d) -> p h d", d=SSD_P), xs[:, tb], over(d_skip_b[:, :], SSD_P), ALU.mult))
            dve.wait_ge(S.free, S.nth("first", "cb"))
            for i in range(TB * SSD_GROUPS):
                dve.wait_ge(seg_exp, i + 1)
                dve.tensor_tensor(decay[:, i], decay[:, i], across(cb[:, i, :], SSD_R), ALU.mult).then_inc(decay_ready, 1)
            st.settle()
            for c in range(TB):
                dve.wait_ge(PT.full, PT.nth("first", f"yd{c}"))
                dve.tensor_tensor(ssd_y[:, c, :], PT.ap[:, :], ssd_y[:, c, :], ALU.add).then_inc(PT.free, 1)
            dve.wait_ge(S.full, S.nth("first", "yo"))
            dve.tensor_tensor(xs[:, 0], S.ap[:, :].rearrange("p (h d) -> p h d", d=SSD_P), over(dt_a[:, 3, 1, :], SSD_P), ALU.mult).then_inc(S.free, 1)
            dve.wait_ge(S.free, S.nth("first", "yo"))
            dve.wait_ge(PT.free, PT.nth("first", "yd1"))
            st.done(dve.tensor_tensor(ssd_y[:, 1, :], ssd_y[:, 1, :], xs[:, 0].rearrange("p h d -> p (h d)"), ALU.add))
            st.settle()
            dve.scalar_tensor_tensor(ssd_y[:, :, :], ssd_y[:, :, :], 0.5, z_silu[:, :, :], ALU.mult, ALU.mult).then_inc(gy_ready, 1)
            rms_rows("first", "gy", D, LN_EPS, lambda tb: ssd_y[:, tb, :], lambda tb: ssd_y[:, tb, :]).then_inc(rows.sem, 1)
            gain_turned("first", "gy", KD, y_turned, conv_col[:, nc_:])
            for i in range(2):
                for tb, b in enumerate(G):
                    cols = slice(i * HALF, (i + 1) * HALF)
                    dve.wait_ge(b.full, b.nth("first", f"so{i}"))
                    dve.scalar_tensor_tensor(gate_ssd[:, tb, cols], gate_ssd[:, tb, cols], 1.0, b.ap[:, :], ALU.add, ALU.mult).then_inc(b.free, 1)
            for b in G:
                dve.wait_ge(b.free, b.nth("first", "so1"))
            dve.tensor_tensor(gate_att[:, :, :], gate_att[:, :, :], gate_ssd[:, :, :], ALU.add).then_inc(rows.sem, 1)

            def residual_norm(part, name, gain, shift):
                st.done(dve.scalar_tensor_tensor(resid[:, :, :], x_rows[:, :, :], ALPHA, resid[:, :, :], ALU.mult, ALU.add))
                st.settle()
                layer_norm(part, name, resid, x_rows)
                layer_norm_end(part, name, resid, x_rows)
                return scale_shift(x_rows[:, :, :], gain, shift)

            for i in range(2):
                for tb, b in enumerate(G):
                    cols = slice(i * HALF, (i + 1) * HALF)
                    dve.wait_ge(b.full, b.nth("first", f"o{i}"))
                    dve.scalar_tensor_tensor(resid[:, tb, cols], b.ap[:, :], 0.5, mod[:, 2, cols], ALU.mult, ALU.mult).then_inc(b.free, 1)
            for b in G:
                dve.wait_ge(b.free, b.nth("first", "o1"))
            dve.wait_ge(in_ln, 16 * 4)
            st.done(residual_norm("first", "ln1", ln_rows[:, 0, :], ln_rows[:, 1, :]))
            st.settle()
            layer_norm("first", "h2", x_rows, h_rows)
            layer_norm_end("first", "h2", x_rows, h_rows)
            scale_shift(h_rows[:, :, :], mod[:, 4, :], mod[:, 3, :]).then_inc(rows.sem, 1)

            for tb, b in enumerate(G):
                dve.wait_ge(b.full, b.nth("first", "route"))
                dve.tensor_tensor(rt[:, tb, :], b.ap[:, 0:N_GROUPS + N_EXPERTS], route_b[:, :], ALU.add).then_inc(b.free, 1)
            for b in G:
                dve.wait_ge(b.free, b.nth("first", "route"))

            def small(i):
                return rt_s[:, i]

            def one(i):
                return rt_s[:, i, :, 0]

            def do(ins):
                st.done(ins)
                st.settle()

            def first_best(v, top, hot):
                do(dve.tensor_reduce(one(top), v, AX_X, ALU.max))
                do(dve.tensor_tensor(small(5), v, over(one(top), PER_GROUP), ALU.is_equal))
                do(dve.tensor_tensor(small(5), small(5), across(back[:, :], TB), ALU.mult))
                do(dve.tensor_reduce(one(6), small(5), AX_X, ALU.max))
                do(dve.tensor_tensor(small(hot), small(5), over(one(6), PER_GROUP), ALU.is_equal))

            first_best(rt[:, :, 0:N_GROUPS], 2, 8)
            dve.tensor_tensor(small(0), rt[:, :, 0:N_GROUPS], over(one(2), N_GROUPS), ALU.subtract).then_inc(route_in, 1)
            for tb in range(TB):
                st.done(dve.tensor_tensor(rt_m[:, tb, :].rearrange("p (g e) -> p g e", g=N_GROUPS),
                                          rt[:, tb, N_GROUPS:].rearrange("p (g e) -> p g e", g=N_GROUPS), over(rt_s[:, 8, tb, :], PER_GROUP), ALU.mult))
            st.settle()
            for tb in range(TB):
                st.done(dve.tensor_reduce(rt_s[:, 9, tb, :], rt_m[:, tb, :].rearrange("p (g e) -> p e g", g=N_GROUPS), AX_X, ALU.add))
            st.settle()
            first_best(small(9), 10, 13)
            do(dve.scalar_tensor_tensor(small(14), small(13), -MASKED, small(9), ALU.mult, ALU.add))
            first_best(small(14), 11, 15)
            dve.tensor_tensor(one(12), one(11), one(10), ALU.subtract).then_inc(route_in, 1)
            do(dve.tensor_tensor(small(20), small(13), small(15), ALU.add))
            for tb in range(TB):
                st.done(dve.tensor_tensor(picked[:, tb, :].rearrange("p (g e) -> p g e", g=N_GROUPS), over(rt_s[:, 8, tb, :], PER_GROUP),
                                          across(rt_s[:, 20, tb, :], N_GROUPS), ALU.mult))
            st.settle()
            dve.sem_inc(picked_ready, 1)
            dve.wait_ge(route_out, 2)
            do(dve.tensor_reduce(one(3), small(1), AX_X, ALU.add))
            do(dve.tensor_scalar(one(16), rt_s[:, 12, :, 1], 1.0, None, ALU.add))
            do(dve.tensor_tensor(one(16), one(16), one(3), ALU.mult))
            do(dve.reciprocal(one(16), one(16)))
            do(dve.tensor_scalar(one(16), one(16), 0.5, None, ALU.mult))
            do(dve.tensor_tensor(one(17), one(16), rt_s[:, 12, :, 1], ALU.mult))
            do(dve.tensor_tensor(small(18), small(13), over(one(16), PER_GROUP), ALU.mult))
            do(dve.tensor_tensor(small(19), small(15), over(one(17), PER_GROUP), ALU.mult))
            do(dve.tensor_tensor(small(18), small(18), small(19), ALU.add))
            for tb in range(TB):
                st.done(dve.tensor_tensor(gates[:, tb, :].rearrange("p (g e) -> p g e", g=N_GROUPS), over(rt_s[:, 8, tb, :], PER_GROUP),
                                          across(rt_s[:, 18, tb, :], N_GROUPS), ALU.mult))
            st.done(dve.memset(pick_t[:, 0, :], 0.0))
            st.done(dve.memset(pair_y[:, 0, :], 0.0))
            st.done(dve.memset(place[:, :, PICKS - 2:], 0.0))
            st.done(dve.memset(gate_of[:, :, PICKS - 2:], 0.0))
            st.settle()
            for i in range(ROUNDS):
                st.done(dve.tensor_copy(gate_of[:, :, i * N_EXPERTS:(i + 1) * N_EXPERTS], gates[:, :, :]))
            st.settle()
            dve.sem_inc(sums_cleared, 1)

            dve.wait_ge(X.full, X.nth("first", "places"))
            st.done(dve.tensor_copy(load_of[:, 0, :], X.ap[:, 32:48]))
            st.done(dve.tensor_copy(slot_row[:, 0, :], X.ap[:, 48:48 + SLOT_TOKENS]))
            do(dve.tensor_tensor(place[:, :, 0:N_EXPERTS], X.ap[:, 0:32].rearrange("p (t e) -> p t e", t=TB), picked[:, :, :], ALU.mult))
            dve.sem_inc(X.free, 1)
            for i in range(1, ROUNDS):
                st.done(dve.tensor_scalar(place[:, :, i * N_EXPERTS:(i + 1) * N_EXPERTS], place[:, :, 0:N_EXPERTS],
                                          -float(i * SLOT_TOKENS), None, ALU.add))
            do(dve.tensor_reduce(rounds_f[:, 0:1], load_of[:, 0, :], AX_X, ALU.max))
            do(dve.tensor_scalar(rounds_f[:, 1:2], rounds_f[:, 0:1], float(SLOT_TOKENS) + 0.5, 1.0, ALU.is_ge, ALU.add))
            for i in range(2, ROUNDS):
                do(dve.scalar_tensor_tensor(rounds_f[:, 1:2], rounds_f[:, 0:1], float(i * SLOT_TOKENS) + 0.5, rounds_f[:, 1:2], ALU.is_ge, ALU.add))
            do(dve.tensor_scalar(rounds_f[:, 2:3], rounds_f[:, 1:2], float(PAIRS), None, ALU.mult))
            do(dve.tensor_copy(rounds_i[:, :], rounds_f[0:1, 1:3]))
            for b in EXPERT_BANKS:
                dve.sem_inc(b.full, 1)
                dve.sem_inc(b.free, 1)
            dve.sem_inc(expert_used, 1)
            dve.sem_inc(rounds_ready, 1)

            def pick_slots(q, dst, gate):
                for j in range(2):
                    for tb in range(TB):
                        c = bass.ds(q * 2 + j, 1)
                        d = dst[:, tb, j * SLOT_TOKENS:(j + 1) * SLOT_TOKENS]
                        if gate:
                            ins = dve.tensor_scalar(d, slot_row[:, 0, :], place[:, tb, c], gate_of[:, tb, c], ALU.is_equal, ALU.mult)
                        else:
                            ins = dve.tensor_scalar(d, slot_row[:, 0, :], place[:, tb, c], None, ALU.is_equal)
                return ins

            n_pairs = dve.value_load(rounds_i[0:1, 1:2], min_val=PAIRS, max_val=PAIRS * ROUNDS)
            pick_slots(0, pick, False).then_inc(pick_ready, 1)
            pick_slots(0, pick_g, True).then_inc(pick_g_ready, 1)
            dve.wait_ge(MX.full, MX.nth("start", "taken"))
            es = Steps(dve, expert_steps)
            with dve.Fori(0, n_pairs) as q:
                es.begin(q, 2)
                dve.wait_ge(MX.full, q * 2 + 1)
                pick_slots(q + 1, pick, False).then_inc(pick_ready, 1)
                for e, b in enumerate((M0, M1)):
                    n = KF * SLOT_TOKENS
                    dve.wait_ge(expert_tanhed, q * 2 + e + 1)
                    es.done(dve.scalar_tensor_tensor(expert_t[:, 2 + e, :], expert_t[:, e, :], 1.0, b.ap[:, 0:n], ALU.add, ALU.mult))
                    es.settle()
                    dve.tensor_tensor(hid_t[:, e, :, :].rearrange("p k n -> p (k n)"), expert_t[:, 2 + e, :], b.ap[:, n:2 * n], ALU.mult)\
                        .then_inc(b.free, 1)
                dve.wait_ge(M0.full, M0.nth("moe", "turned", q))
                pick_slots(q + 1, pick_g, True).then_inc(pick_g_ready, 1)

            for tb, b in enumerate((S, PT)):
                dve.wait_ge(b.full, b.nth("mid", "sums"))
                dve.tensor_tensor(resid[:, tb, :], b.ap[:, :], mod[:, 5, :], ALU.mult).then_inc(b.free, 1)
            for b in (S, PT):
                dve.wait_ge(b.free, b.nth("mid", "sums"))
            residual_norm("mid", "ln2", ln_rows[:, 2, :], ln_rows[:, 3, :]).then_inc(x_ready.sem, 1)
            dve.wait_ge(x_ready.sem, 1)
            st.end()

            with dve.Fori(0, LAYERS) as l:
                st.begin(l, LAYER_DVE_STEPS)
                dve.wait_ge(in_layer, 16 * 11 + l * (16 * 11))
                st.done(dve.tensor_scalar(sink_neg[:, :], sink_neg[:, :], -1.0, None, ALU.mult))
                for i in range(2):
                    st.done(dve.tensor_scalar(w2_k[:, i, :], w2[:, 0, :], 0.5, None, ALU.mult))
                st.done(dve.tensor_scalar(w2_v[:, :], w2[:, 1, :], 0.5, None, ALU.mult))
                for v in range(2):
                    st.done(dve.memset(kc_t[:, v, :, SEQ:], 0.0))
                dve.wait_ge(X.full, X.nth("layer", "g_col", l))
                dve.tensor_copy(g_col[:, :], X.ap[:, 0:G_END]).then_inc(X.free, 1)
                rms_rows("layer", "mix", D, RMS_EPS, lambda tb: x_rows[:, tb, :], lambda tb: h_rows[:, tb, :], l).then_inc(rows.sem, 1)
                dve.wait_ge(X.free, X.nth("layer", "g_col", l))
                gain_turned("layer", "mix", KD, h_t, g_col[:, G_MIX:], l)

                def rope(pieces, half, cos, sin):
                    at_t, made = 0, []
                    for dst, src, tb in pieces:
                        nh = src.shape[1]
                        tmp = rope_tmp[:, 0, at_t:at_t + nh * 2 * half].rearrange("p (h d) -> p h d", h=nh)
                        at_t += nh * 2 * half
                        st.done(dve.tensor_tensor(tmp[:, :, 0:half], src[:, :, half:], across(sin(tb, 0), nh), ALU.mult))
                        st.done(dve.tensor_tensor(tmp[:, :, half:], src[:, :, 0:half], across(sin(tb, 1), nh), ALU.mult))
                        made.append(tmp)
                    st.settle()
                    for dst, src, tb in pieces:
                        for i in range(2):
                            part = slice(i * half, (i + 1) * half)
                            st.done(dve.tensor_tensor(dst[:, :, part], src[:, :, part], across(cos(tb), src.shape[1]), ALU.mult))
                    st.settle()
                    for (dst, src, tb), tmp in zip(pieces, made):
                        ins = dve.tensor_tensor(dst, dst, tmp, ALU.add)
                    return ins

                cos64, sin64 = (lambda tb: rope_c[:, tb, 0:hh]), (lambda tb, i: rope_s[:, tb, i * hh:(i + 1) * hh])
                by_head = lambda v: v.rearrange("p (h d) -> p h d", d=HD)
                for b in G:
                    dve.wait_ge(b.free, b.nth("layer", "in1", l))
                rope([(by_head(swa_r[:, tb, :]), by_head(proj[:, tb, 0:C_AV]), tb) for tb in range(TB)], hh, cos64, sin64).then_inc(rows.sem, 1)
                for b in G:
                    dve.wait_ge(b.free, b.nth("layer", "in4", l))
                dve.wait_ge(rows.sem, rows.at("layer", "swa", l))
                rope([(by_head(nsa_q[:, tb, :]), by_head(proj[:, tb, C_BQ:C_KC]), tb) for tb in range(TB)]
                     + [(by_head(nsa_k[:, tb, 0:P]), by_head(proj[:, tb, C_KS:C_VS]), tb) for tb in range(TB)]
                     + [(by_head(nsa_k[:, tb, P:]), by_head(proj[:, tb, C_KW:C_VW]), tb) for tb in range(TB)], hh, cos64, sin64).then_inc(rows.sem, 1)

                for tb in range(TB):
                    ins = dve.tensor_copy(kc_twice[:, tb, :].rearrange("p (v a d) -> p v a d", a=2, d=HD),
                                          by_head(proj[:, tb, C_KC:C_KS]).unsqueeze(2).broadcast_to([P, 4, 2, HD]))
                ins.then_inc(rows.sem, 1)

                st.done(rms_rows("layer", "qn", MLA_Q, RMS_EPS, lambda tb: proj[:, tb, C_QA:C_KV], lambda tb: lat[:, tb, 0:MLA_Q], l))
                rms_rows("layer", "kvn", MLA_KV, RMS_EPS, lambda tb: proj[:, tb, C_KV:C_KR], lambda tb: lat[:, tb, MLA_Q:], l).then_inc(rows.sem, 1)
                dve.wait_ge(bg_tanhed, l + 1)
                st.done(dve.tensor_scalar(branch_g[:, :, :], branch_g[:, :, :], 1.0, 0.5, ALU.add, ALU.mult))
                gain_turned("layer", "lat", 5, lat_t, g_col[:, G_QN:G_PEK], l)

                for b in G:
                    dve.wait_ge(b.free, b.nth("layer", "kvb1", l))
                dve.wait_ge(rows.sem, rows.at("layer", "nsa", l))
                hr = MLA_ROPE // 2
                cos32, sin32 = (lambda tb: rope_c[:, tb, 0:hh:2]), (lambda tb, i: rope_s[:, tb, i * hh:(i + 1) * hh:2])
                heads96 = lambda v: v.rearrange("p (h d) -> p h d", d=MLA_QK)
                q_pe = lambda tb: heads96(mla_q[:, tb, :])[:, :, HD:]
                k_pe = lambda tb: proj[:, tb, C_KR:C_G].unsqueeze(1)
                st.done(rope([(q_pe(tb), q_pe(tb), tb) for tb in range(TB)] + [(k_pe(tb), k_pe(tb), tb) for tb in range(TB)], hr, cos32, sin32))
                st.settle()
                for tb in range(TB):
                    k = heads96(mla_k[:, tb, :])
                    st.done(dve.tensor_copy(k[:, :, 0:HD], kv_rows[:, tb, :].rearrange("p (h d) -> p h d", d=P)[:, :, 0:HD]))
                    ins = dve.tensor_copy(k[:, :, HD:], across(proj[:, tb, C_KR:C_G], HEADS))
                    if tb == 0:
                        st.done(ins)
                ins.then_inc(rows.sem, 1)

                attention("layer", SWA_STEPS, crossed(o_a), l)

                for b, r in ((X, 0), (O, 1)):
                    dve.wait_ge(b.free, b.nth("layer", f"nsc{r}", l))
                st.settle()
                for v in range(2):
                    for half in range(2):
                        lanes = slice(HD * half, HD * half + HD)
                        for hi in range(2):
                            src = kc_t[lanes, v, :, 16 * hi:16 * hi + SEQ].rearrange("p g (n j a) -> p j g n a", j=8, a=2)[:, :, :, :, half]
                            pos = g_col[lanes, G_PEK + 16 * v + 8 * hi:G_PEK + 16 * v + 8 * hi + 8]
                            ins = dve.tensor_tensor(cmp_blk[lanes, v, 8 * hi:8 * hi + 8, :].rearrange("p j (g n) -> p j g n", g=2), src,
                                                    pos.unsqueeze(2).unsqueeze(3).broadcast_to([HD, 8, 2, CMP]), ALU.add)
                            if (v, half, hi) != (1, 1, 1):
                                st.done(ins)
                ins.then_inc(rows.sem, 1)
                dve.wait_ge(cmp_tanhed, l + 1)
                dve.scalar_tensor_tensor(cmp_h[:, 2:4].rearrange("p v g n -> p (v g n)"), cmp_h[:, 0:2].rearrange("p v g n -> p (v g n)"), 1.0,
                                         X.ap[0:HD, 0:4 * CMP], ALU.add, ALU.mult).then_inc(X.free, 1)
                dve.wait_ge(X.free, X.nth("layer", "cmph", l))
                dve.tensor_copy(cmp_hv[:, :, :, :], cmp_h[:, 3].unsqueeze(2).broadcast_to([HD, 2, HEADS // 2, CMP])).then_inc(rows.sem, 1)
                dve.wait_ge(O.full, O.nth("layer", "cmpkv", l))
                st.done(dve.tensor_copy(cmp_k[:, :], O.ap[:, 0:2 * CMP]))
                dve.tensor_tensor(cmp_v[:, :, :], across(O.ap[:, 64:64 + HD], HEADS), over(head_of[:, :], HD), ALU.mult).then_inc(O.free, 1)

                for qb in range(TB):
                    tag = f"cmp0{qb}"
                    n = masked.parts["layer"].index(tag)
                    s8 = scores[:, n % 2, 0, 0:P].rearrange("p (h n) -> p h n", n=CMP)
                    dve.wait_ge(S.full, S.nth("layer", tag, l))
                    for f in range(2):
                        ins = dve.scalar_tensor_tensor(s8[:, 4 * f:4 * f + 4, :], S.ap[:, f * HALF:f * HALF + 4 * CMP].rearrange("p (h n) -> p h n", n=CMP),
                                                       -HD ** -0.5, across(cmp_mask[:, qb, :], 4), ALU.mult, ALU.add)
                        if f == 0:
                            st.done(ins)
                    ins.then_inc(S.free, 1)
                    st.settle()
                    dve.wait_ge(S.free, S.nth("layer", tag, l))
                    st.done(dve.tensor_reduce(neg_max[:, n % 2, :], s8, AX_X, ALU.min))
                    st.settle()
                    st.done(dve.tensor_scalar(neg_max[:, n % 2, :], neg_max[:, n % 2, :], MASKED / 10, None, ALU.min))
                    st.settle()
                    dve.tensor_tensor(s8, s8, over(neg_max[:, n % 2, :], CMP), ALU.subtract).then_inc(masked.sem, 1)
                for qb in range(TB):
                    n = masked.parts["layer"].index(f"cmp0{qb}")
                    s8 = scores[:, n % 2, 0, 0:P].rearrange("p (h n) -> p h n", n=CMP)
                    dve.wait_ge(cmp_exp, TB * l + qb + 1)
                    st.done(dve.tensor_reduce(den[:, n % 2, :], s8, AX_X, ALU.add))
                    st.settle()
                    st.done(dve.tensor_scalar(den[:, n % 2, :], den[:, n % 2, :], 0.5, None, ALU.max))
                    st.settle()
                    st.done(dve.reciprocal(rden[:, n % 2, :], den[:, n % 2, :]))
                    st.settle()
                    dve.tensor_tensor(s8, s8, over(rden[:, n % 2, :], CMP), ALU.mult).then_inc(probs.sem, 1)
                for qb in range(TB):
                    dve.wait_ge(O.full, O.nth("layer", f"cmp0{qb}", l))
                    g0 = branch_g[:, qb, :].rearrange("p (h b) -> p h b", b=3)[:, :, 0]
                    dve.tensor_tensor(o_b[:, qb, :].rearrange("p (h d) -> p h d", d=HD), O.ap[:, :].rearrange("p (h d) -> p h d", d=HD),
                                      over(g0, HD), ALU.mult).then_inc(O.free, 1)
                dve.wait_ge(O.free, O.nth("layer", "cmp01", l))

                def branch(i):
                    return lambda s: branch_g[:, s[2], :].rearrange("p (f a r b) -> p f a r b", f=2, a=2, b=3)[:, :, s[1], :, i]

                attention("layer", SEL_STEPS, crossed(o_b), l, branch(1))
                attention("layer", WIN_STEPS, crossed(o_b), l, branch(2), end=rows.sem)
                attention("layer", MLA_STEPS, lambda s: o_c[:, s[2], s[1] * SEQ:(s[1] + 1) * SEQ].rearrange("p (i d) -> p i d", d=HD), l)

                for j, name in enumerate("abc"):
                    for half in range(2):
                        for tb, b in enumerate(G):
                            m = merged[:, tb, half * HALF:(half + 1) * HALF]
                            g = gate_t[:, tb, j * D + half * HALF:j * D + (half + 1) * HALF]
                            dve.wait_ge(b.full, b.nth("layer", f"br{name}{half}", l))
                            dve.scalar_tensor_tensor(m if j == 0 else g, g, 1.0, b.ap[:, :], ALU.add, ALU.mult).then_inc(b.free, 1)
                            if j:
                                dve.wait_ge(b.free, b.nth("layer", f"br{name}{half}", l))
                                ins = dve.tensor_tensor(m, m, g, ALU.add)
                                if (j, half, tb) != (2, 1, 1):
                                    st.done(ins)
                    if j == 1:
                        st.settle()
                ins.then_inc(rows.sem, 1)

                rms_rows("layer", "mem", D, RMS_EPS, lambda tb: mem_rows[:, tb, :], lambda tb: mem_rows[:, tb, :], l).then_inc(rows.sem, 1)
                for i in range(2):
                    for tb, b in enumerate(G):
                        x = x_rows[:, tb, i * HALF:(i + 1) * HALF]
                        dve.wait_ge(b.full, b.nth("layer", f"out{i}", l))
                        dve.scalar_tensor_tensor(x, b.ap[:, :], 0.5, x, ALU.mult, ALU.add).then_inc(b.free, 1)
                gain_turned("layer", "mem", KD, mem_t, g_col[:, G_MEM:], l)
                rms_rows("layer", "xattn", D, RMS_EPS, lambda tb: x_rows[:, tb, :], lambda tb: h_rows[:, tb, :], l).then_inc(rows.sem, 1)
                gain_turned("layer", "hx", KD, h_t, g_col[:, G_XATTN:], l)
                attention("layer", X_STEPS, lambda s: o_a[:, s[2], :].rearrange("p (i d) -> p i d", d=XD), l, None, XD)
                for half in range(2):
                    for tb, b in enumerate(G):
                        x = x_rows[:, tb, half * HALF:(half + 1) * HALF]
                        dve.wait_ge(b.full, b.nth("layer", f"xo{half}", l))
                        dve.tensor_tensor(x, b.ap[:, :], x, ALU.add).then_inc(b.free, 1)

                rms_rows("layer", "ffn", D, RMS_EPS, lambda tb: x_rows[:, tb, :], lambda tb: h_rows[:, tb, :], l).then_inc(rows.sem, 1)
                gain_turned("layer", "hf", KD, h_t, g_col[:, G_FFN:], l)
                for c in range(KFF // 2):
                    dve.wait_ge(gate_tanhed, l * (KFF // 2) + c + 1)
                    dve.scalar_tensor_tensor(ff_tmp[:, 2 + c % 2, :], ff_tmp[:, c % 2, :], 1.0, G0.ap[:, :], ALU.add, ALU.mult).then_inc(G0.free, 1)
                    dve.wait_ge(G1.full, G1.nth("layer", f"gu{c}", l))
                    dve.wait_ge(G0.free, G0.nth("layer", f"gu{c}", l))
                    dve.tensor_tensor(ff_t[:, 2 * c:2 * c + 2, :].rearrange("p k n -> p (k n)"), ff_tmp[:, 2 + c % 2, :], G1.ap[:, :], ALU.mult)\
                        .then_inc(G1.free, 1)
                for tb, b in enumerate((S, PT)):
                    x = x_rows[:, tb, :]
                    dve.wait_ge(b.full, b.nth("layer", "ffd", l))
                    dve.scalar_tensor_tensor(x, b.ap[:, :], 0.5, x, ALU.mult, ALU.add).then_inc(b.free, 1)
                for b in (S, PT):
                    dve.wait_ge(b.free, b.nth("layer", "ffd", l))
                dve.sem_inc(x_ready.sem, 1)
                st.settle()
            st.end(LAYERS)

            rms_rows("last", "out", D, RMS_EPS, lambda tb: x_rows[:, tb, :], lambda tb: h_rows[:, tb, :]).then_inc(last_rows, 1)
            dve.wait_ge(last_rows, 1)
            dve.wait_ge(in_ln, 16 * 5)
            dve.tensor_tensor(h_rows[:, :, :], h_rows[:, :, :], across(x_gain, TB), ALU.mult).then_inc(out_ready, 1)


_INS = [
    "x", "c", "w_mod", "b_mod", "w_in", "conv_w", "conv_b", "dt_bias", "a_log", "d_skip", "ssd_norm_w", "forget_b",
    "w_ssd_o", "w_att_o", "w_o", "ln1_g", "ln1_b", "w_router_group", "b_router_group", "w_router_expert",
    "b_router_expert", "w_gate", "w_up", "w_down", "ln2_g", "ln2_b", "mem_2", "positions_2", "norm_mix_2", "w_in_2",
    "swa_sinks_2", "nsa_pe_k_2", "nsa_pe_v_2", "nsa_wk1_2", "nsa_wk2_2", "nsa_wv1_2", "nsa_wv2_2",
    "mla_q_norm_2", "mla_w_q_b_2", "mla_kv_norm_2", "mla_w_kv_b_2", "w_br_a_2", "w_br_b_2", "w_br_c_2",
    "w_out_2", "norm_xattn_2", "norm_mem_2", "w_xq_2", "w_xkv_2", "w_xo_2", "norm_ffn_2", "w_gate_up_2",
    "w_down_2", "norm_final_2",
]


def kernel(**inputs):
    import numpy as _np
    import concourse.bacc as _bacc
    from concourse import mybir as _mybir
    from concourse.bass_utils import run_bass_kernel_spmd as _run

    nc = _bacc.Bacc("TRN2", target_bir_lowering=False, num_devices=1)
    arrays, views = {}, {}
    for name in _INS:
        a = _np.ascontiguousarray(inputs[name])
        arrays[f"in_{name}_dram"] = a
        views[name] = nc.dram_tensor(f"in_{name}_dram", a.shape, _mybir.dt.from_np(a.dtype), kind="ExternalInput").ap()
    out = nc.dram_tensor("out_0_dram", (1, SEQ, D), F32, kind="ExternalOutput").ap()
    two_blocks(nc, views, out)
    r = _run(nc, [arrays], core_ids=[0])
    return r.results[0]["out_0_dram"]
```

```python
from contextlib import ExitStack

import numpy as np

import concourse.bass as bass
from concourse import mybir

F32 = mybir.dt.float32
F32R = mybir.dt.float32r
I32 = mybir.dt.int32
ALU = mybir.AluOpType
ACT = mybir.ActivationFunctionType
AX_X = mybir.AxisListType.X

P = 128
SEQ = 256
TB = SEQ // P
D = 1024
KD = D // P
HALF = 512
LN_EPS = 1e-5
RMS_EPS = 1e-6
MASKED = 1e30

SSD_HEADS, SSD_P, SSD_GROUPS, SSD_N = 16, 64, 4, 128
SSD_R = SSD_HEADS // SSD_GROUPS
CONV_TILES = (D + 2 * SSD_GROUPS * SSD_N) // P
CONV_K = 4
FOX_HEADS = 8
OFF_Z, OFF_XBC, OFF_DT, OFF_Q, OFF_K, OFF_V, OFF_F, OFF_GS, OFF_GA = (
    int(v) for v in np.cumsum([0, D, CONV_TILES * P, SSD_HEADS, 512, 512, 512, FOX_HEADS, D]))
N_GROUPS, PER_GROUP = 4, 4
N_EXPERTS = N_GROUPS * PER_GROUP
FF = D // 2
KF = FF // P
SLOT_TOKENS = P // 2
PAIRS = N_EXPERTS // 2
ROUNDS = SEQ // SLOT_TOKENS
PICKS = ROUNDS * N_EXPERTS + 2
ALPHA = float(2.0 ** 0.25)

LAYERS = 2
HEADS, HD = 8, 64
CMP_BLOCK, CMP_STRIDE = 32, 16
N_CMP = (SEQ - CMP_BLOCK) // CMP_STRIDE + 1
CMP = N_CMP + 1
MLA_Q, MLA_KV, MLA_QK, MLA_ROPE = 384, 256, 96, 32
XH, XD = 4, 128
D_FF = 2816
KFF = D_FF // P
(C_AQ, C_AK, C_AV, C_BQ, C_KC, C_VC, C_KS, C_VS, C_KW, C_VW, C_BG, C_QA, C_KV, C_KR, C_G) = (
    int(v) for v in np.cumsum([0, 512, 128, 128, 512, 128, 128, 128, 128, 128, 128, 24, MLA_Q, MLA_KV, MLA_ROPE]))
assert SEQ // 64 <= 16 and SEQ <= 512

IN_AT = [C_AQ, C_AK, C_BQ, C_KC, C_KW, (C_KW + C_G) // 2, C_G]

IN_ORDER = [1, 0, 2, 3, 4, 5]

SLOTS = 3
SLOT = KD * HALF

G_MIX, G_XATTN, G_MEM, G_FFN, G_QN, G_KVN, G_PEK, G_PEV, G_END = (
    int(v) for v in np.cumsum([0, KD, KD, KD, KD, MLA_Q // P, MLA_KV // P, 16, 16]))


class Bank:

    def __init__(self, ap, full, free, given=0):
        self.ap, self.full, self.free, self.given = ap, full, free, given
        self.start, self.per, self.uses, self.total = {}, {}, {}, given

    def begin(self, part, per_round):
        self.part, self.start[part], self.per[part], self.uses[part] = part, self.total, per_round, []

    def turn(self, name, rnd=0):
        uses = self.uses[self.part]
        assert name not in uses, name
        uses.append(name)
        return self.start[self.part] + rnd * self.per[self.part] + len(uses) - 1

    def end(self, rounds):
        n = len(self.uses[self.part])
        assert rounds == 1 or n == self.per[self.part], (self.part, n, self.per[self.part])
        self.total += rounds * n

    def nth(self, part, name, rnd=0):
        return self.start[part] + rnd * self.per[part] + self.uses[part].index(name) + 1


class Steps:

    def __init__(self, eng, sem):
        self.eng, self.sem, self.base, self.n, self.rnd, self.per = eng, sem, 0, 0, 0, 0

    def begin(self, rnd, per):
        self.n, self.rnd, self.per = 0, rnd, per

    def done(self, ins):
        ins.then_inc(self.sem, 1)
        self.n += 1

    def settle(self):
        self.eng.wait_ge(self.sem, self.base + self.rnd * self.per + self.n)

    def end(self, rounds=1):
        assert rounds == 1 or self.n == self.per, (self.n, self.per)
        self.base += rounds * self.n
        self.n, self.rnd, self.per = 0, 0, 0


class Named:

    def __init__(self, sem, **parts):
        self.sem, self.parts, self.start, total = sem, {}, {}, 0
        for part, (rounds, names) in parts.items():
            self.parts[part], self.start[part] = names, total
            total += rounds * len(names)
        self.total = total

    def at(self, part, name, rnd=0):
        names = self.parts[part]
        return self.start[part] + rnd * len(names) + names.index(name) + 1


MOD_CHUNKS = [f"mod{i}" for i in range(6 * D // HALF)]
MOD_FIRST = [MOD_CHUNKS[i] for i in (0, 2, 1, 3)]
MOD_SUMMED = [0, 2, 8, 9, 10, 11]
FIRST_CHUNKS = (MOD_FIRST + ["dtf"] + [f"xbc{i}" for i in range(4)] + ["q", "k", "v", "z0", "z1", "ga0", "ga1", "mod8", "gs0", "mod9", "att", "gs1",
                "mod4", "so0", "so1", "mod10", "mod5", "o0", "o1", "mod11", "mod6", "mod7"])
PAIR_CHUNKS = ["gate0", "up0", "gate1", "up1", "down0", "down1"]
GATE_CHUNKS = [f"g{i}" for i in range(6)]
LAYER_CHUNKS = ([f"in{i}" for i in IN_ORDER] + ["g0", "qb", "kvb", "g1", "g2", "cmp", "g3", "g4", "g5"]
                + ["bra", "brb", "brc", "memk", "out0", "out1", "memv", "xq", "xo"]
                + [f"gu{i}" for i in range(KFF // 2)] + [f"fd{i}" for i in range(6)])

FOX_STEPS = [("fox", pp, qb) for pp in range(2) for qb in range(TB)]
SWA_STEPS = [("swa", pp, qb) for pp in range(2) for qb in range(TB)]
CMP_STEPS = [("cmp", 0, qb) for qb in range(TB)]
SEL_STEPS = [("sel", pp, qb) for pp in range(2) for qb in range(TB)]
WIN_STEPS = [("win", pp, qb) for pp in range(2) for qb in range(TB)]
MLA_STEPS = [("mla", pp, qb) for pp in range(2) for qb in range(TB)]
X_STEPS = [("x", 0, qb) for qb in range(TB)]
LAYER_STEPS = SWA_STEPS + CMP_STEPS + SEL_STEPS + WIN_STEPS + MLA_STEPS + X_STEPS
FILLERS = {("fox", 0, 0): ("gs0", 0), ("fox", 0, 1): ("gs0", 1), ("swa", 0, 0): "g1", ("sel", 0, 0): "g5"}


FIRST_SPLIT = [f"xbc{i}" for i in range(4)] + ["q", "k", "v", "z0", "z1", "ga0", "ga1"]
SPLIT = [f"in{i}" for i in IN_ORDER] + ["bra", "brb", "brc", "memk", "out0", "out1", "memv", "xq", "xo"] + [f"gu{i}" for i in range(KFF // 2)] + [f"fd{i}" for i in range(6)]
SPLIT_X = [f"{tag}{i}" for tag, n in (("mix", 4), ("oa", 2), ("ob", 2), ("oc", 2), ("mem", 4), ("mg", 4), ("hx", 4), ("ox", 2), ("hf", 4)) for i in range(n)]


def chunk_size(name):
    if name.startswith("in"):
        return KD * (IN_AT[int(name[2:]) + 1] - IN_AT[int(name[2:])])
    return (KFF % KF) * D if name == "fd5" else SLOT


def step_tag(step):
    return f"{step[0]}{step[1]}{step[2]}"


def keys_of(step):
    return SEQ if step[2] == 1 or step[0] == "x" else P


ROUND = float(1.5 * 2 ** 23)
TURN = (6.28125, float(np.float32(2 * np.pi - 6.28125) // 2 ** -21 * 2 ** -21))
TURN = (*TURN, float(np.float32(2 * np.pi - TURN[0] - TURN[1])))
PI_IN = 3.1415925

ARENA = 31100


PIECES = {"in0": 2 * KD, "in2": 2 * KD, "dtf": 2, "cmp": 2, **{f"gu{i}": 2 for i in range(KFF // 2)}}
PARTS = {"first": (1, FIRST_CHUNKS), "layer": (LAYERS, LAYER_CHUNKS + ["unused"])}
assert len(PARTS["layer"][1]) % SLOTS == 0


def place_chunks():
    place, at, landed = {}, 0, [0] * SLOTS
    for part, (rounds, names) in PARTS.items():
        per = [0] * SLOTS
        for j, name in enumerate(names):
            per[(at + j) % SLOTS] += 16 * PIECES.get(name, 1) * (name != "unused")
        seen = [0] * SLOTS
        for j, name in enumerate(names):
            s = (at + j) % SLOTS
            seen[s] += 16 * PIECES.get(name, 1) * (name != "unused")
            place[part, name] = (s, landed[s] + seen[s], per[s])
        landed = [a + rounds * b for a, b in zip(landed, per)]
        at += rounds * len(names)
    return place


PLACE = place_chunks()

LAYER_USES = {"G0": 34, "G1": 34, "S": 27, "P": 27, "O": 44, "X": 28}
LAYER_DVE_STEPS = 132


def two_blocks(nc, t, out):
    with ExitStack() as ctx, nc.allow_non_contiguous_dma(reason="small vectors turned onto partitions"):
        def sb(name, shape, dt=F32):
            return ctx.enter_context(nc.sbuf_tensor(name, shape, dt))

        def sem(name):
            return ctx.enter_context(nc.semaphore(name))

        ring_at = -(-nc.sbuf_base // 32) * 32
        ring = sb("ring", [P, SLOTS, SLOT])
        x_rows = sb("x_rows", [P, TB, D])
        h_rows_at = -(-nc.sbuf_base // 32) * 32
        h_rows = sb("h_rows", [P, TB, D])
        h_t_at = -(-nc.sbuf_base // 32) * 32
        h_t = sb("h_t", [P, KD, SEQ])
        ident = sb("ident", [P, P])
        tri = sb("tri", [P, SEQ])
        causal = sb("causal", [P, SEQ])
        windowed = sb("windowed", [P, SEQ])
        cmp_mask = sb("cmp_mask", [P, TB, CMP])
        head_of = sb("head_of", [P, HEADS])
        half_power = sb("half_power", [P, TB])
        inv_freq = sb("inv_freq", [P, HD // 2])
        pos_i = sb("pos_i", [P, TB], I32)
        pos_f = sb("pos_f", [P, TB])
        angle = sb("angle", [P, 4, TB, HD // 2])
        rope_c = sb("rope_c", [P, TB, HD])
        rope_s = sb("rope_s", [P, TB, HD])
        stage = sb("stage", [P, P])
        c_col = sb("c_col", [P, KD])
        c_act = sb("c_act", [P, KD])
        conv_col = sb("conv_col", [P, CONV_TILES * (CONV_K + 1) + KD])
        bias24 = sb("bias24", [P, SSD_HEADS + FOX_HEADS])
        a_log_b = sb("a_log_b", [P, SSD_HEADS])
        d_skip_b = sb("d_skip_b", [P, SSD_HEADS])
        sp = sb("sp", [P, 6, TB, SSD_HEADS + FOX_HEADS])
        dt_a = sb("dt_a", [P, 5, TB, SSD_HEADS])
        route_w = sb("route_w", [P, KD, N_GROUPS + N_EXPERTS])
        route_b = sb("route_b", [P, N_GROUPS + N_EXPERTS])
        rt = sb("rt", [P, TB, N_GROUPS + N_EXPERTS])
        rt_s = sb("rt_s", [P, 24, TB, PER_GROUP])
        rt_m = sb("rt_m", [P, TB, N_EXPERTS])
        back = sb("back", [P, PER_GROUP])
        gates = sb("gates", [P, TB, N_EXPERTS])
        rounds_f = sb("rounds_f", [P, 4])
        rounds_i = sb("rounds_i", [1, 2], I32)
        bn = sb("bn", [P, TB, 2, 6])
        mean_var = sb("mean_var", [P, TB, 2])
        square_sum = sb("square_sum", [P, TB])
        var_in = sb("var_in", [P, TB])
        rstd = sb("rstd", [P, TB])
        g_col = sb("g_col", [P, G_END])
        neg_max = sb("neg_max", [P, 2, HEADS])
        den = sb("den", [P, 4, HEADS])
        rden = sb("rden", [P, 2, HEADS])
        sink_neg = sb("sink_neg", [P, HEADS])
        sink_e = sb("sink_e", [P, 4, HEADS])
        branch_g = sb("branch_g", [P, TB, HEADS * 3])
        w2 = sb("w2", [HD, 2, HD])
        w2_k = sb("w2_k", [HD, 2, HD])
        w2_v = sb("w2_v", [HD, HD])
        cmp_h = sb("cmp_h", [HD, 4, 2, CMP])
        cmp_hv = sb("cmp_hv", [HD, 2, HEADS // 2, CMP])
        cmp_k = sb("cmp_k", [P, 2 * CMP])
        arena_at = -(-nc.sbuf_base // 32) * 32
        arena = sb("arena", [P, ARENA])
        ring_r = nc.alloc_sbuf_tensor_at("ring_r", [P, SLOTS, SLOT], F32R, offset=ring_at)
        first_low = nc.alloc_sbuf_tensor_at("first_low", [P, KD, SEQ], F32R, offset=h_rows_at)
        h_t_r = nc.alloc_sbuf_tensor_at("h_t_r", [P, KD, SEQ], F32R, offset=h_t_at)

        def view(at, *shape):
            n = int(np.prod(shape))
            assert at + n <= ARENA, (at, shape)
            v = arena[:, at:at + n]
            if len(shape) == 2:
                v = v.rearrange("p (a b) -> p a b", b=shape[1])
            elif len(shape) == 3:
                v = v.rearrange("p (a b c) -> p a b c", b=shape[1], c=shape[2])
            return v

        GATES_AT = 12 * D + CONV_TILES * (SEQ + CONV_K - 1) + TB * D
        at = 0
        mod = view(at, 6, D)
        xs = view(at, TB, SSD_HEADS, SSD_P)
        at += 6 * D
        b_mod = view(at, 1, 2 * D)
        conv = view(at, CONV_TILES, SEQ)
        ssd_y = view(at + CONV_TILES * SEQ, TB, D)
        pair_w = [ring[:, j, :] if j < SLOTS else arena[:, GATES_AT + (j - SLOTS) * SLOT:GATES_AT + (j - SLOTS + 1) * SLOT] for j in range(len(PAIR_CHUNKS))]
        pick = view(at, TB, P)
        pick_g = view(at + SEQ, TB, P)
        pick_t = view(at + 2 * SEQ, 1, SEQ)
        taken_t = view(at + D, KD, P)
        pair_y = view(at + 2 * D, 1, D)
        expert_t = view(at + 3 * D, 2, HALF)
        hid_t = view(at + 4 * D, KF, P)
        place = view(at + 4 * D + 512, TB, PICKS)
        gate_of = view(at + 4 * D + 768, TB, PICKS)
        slot_row = view(at + 5 * D, 1, SLOT_TOKENS)
        picked = view(at + 5 * D + 64, TB, N_EXPERTS)
        load_of = view(at + 5 * D + 128, 1, N_EXPERTS)
        at += 6 * D
        PAD = SEQ + CONV_K - 1
        BIAS_ROW = P - (len(MOD_CHUNKS) - len(MOD_FIRST)) * (HALF // P)
        xbc_pad = view(at, CONV_TILES, PAD)
        conv_tanh = view(at, CONV_TILES, SEQ)
        decay = view(at, TB * SSD_GROUPS, SSD_R, P)
        ln_rows = view(at, 4, D)
        at += CONV_TILES * PAD
        z_silu = view(at, TB, D)
        y_turned = view(at, KD, SEQ)
        resid = view(at, TB, D)
        at += TB * D
        assert at == GATES_AT
        gate_ssd = view(at, TB, D)
        at += TB * D
        gate_att = view(at, TB, D)
        at += TB * D
        q_t, k_t, v_rows = view(at, 4, SEQ), view(at + 1024, 4, SEQ), view(at + 2048, TB, HALF)
        x_end, cb, states = view(at, SSD_HEADS, SSD_P), view(at + 1024, TB * SSD_GROUPS, P), view(at + 2048, SSD_GROUPS, SSD_R * SSD_P)
        at += 3072
        fox_o, fox_ot = view(at, TB, HALF), view(at + 1024, KF, SEQ)
        b_rows = view(at + 1024, SSD_GROUPS, SSD_N)
        at += 2048
        S_AT = at
        scores = view(at, 2, 4, SEQ)
        probs_t = view(at + 2048, 4, 2, P)
        at += 3072
        assert at - GATES_AT >= (len(PAIR_CHUNKS) - SLOTS) * SLOT
        xdt = h_rows[:, :, :].rearrange("p t (h d) -> p t h d", d=SSD_P)

        PW = C_G
        at = 0
        proj = view(at, TB, PW)
        at += TB * PW
        gate_t = view(at, TB, 3 * D)
        ff_t = view(at, KFF, SEQ)
        at += TB * 3 * D
        rot = view(at, 1, 2816)
        swa_r = rot[:, 0, 0:1280].rearrange("p (t n) -> p t n", t=TB)
        nsa_q = rot[:, 0, 1280:2304].rearrange("p (t n) -> p t n", t=TB)
        nsa_k = rot[:, 0, 2304:2816].rearrange("p (t n) -> p t n", t=TB)
        mem_v = rot[:, 0, 0:1024].rearrange("p (t n) -> p t n", t=TB)
        x_gain = rot[:, 0, 0:D]
        at += 2816
        qt = view(at, 8, SEQ)
        merged = view(at, TB, D)
        at += 2048
        kt = view(at, 8, SEQ)
        kc_t = arena[:, at + 512:at + 512 + 4 * 272].rearrange("p (v g n) -> p v g n", v=2, g=2)
        at += 2048
        o_a, o_b, o_c = (view(at + 1024 * i, TB, HALF) for i in range(3))
        lat_t = view(at + 1024, 5, SEQ)
        at += 3072
        o_t = view(at, KF, SEQ)
        at += 1024
        lat = view(at, TB, MLA_Q + MLA_KV)
        at += TB * (MLA_Q + MLA_KV)
        mla_q = view(at, TB, HEADS * MLA_QK)
        at += TB * HEADS * MLA_QK
        mla_k = view(at, TB, HEADS * MLA_QK)
        at += TB * HEADS * MLA_QK
        cmp_v = view(at, HEADS, HD)
        at += HEADS * HD
        assert at <= S_AT, (at, S_AT)
        rope_tmp = view(S_AT, 1, 2048)
        kc_twice = view(S_AT + 2048, TB, HALF)
        cmp_blk = arena[:, S_AT:S_AT + 1024].rearrange("p (v j n) -> p v j n", v=2, j=16)
        ff_tmp = view(S_AT, 4, HALF)
        at = S_AT + 3072
        o_tmp = view(at, 4, HD)
        at += 256
        kv_rows = h_rows
        mem_rows = h_rows
        mem_t = view(S_AT, KD, SEQ)
        assert at <= ARENA, at
        QT_AT, LAT_AT = TB * PW + TB * 3 * D + 2816, TB * PW + TB * 3 * D + 2816 + 8192
        def view_r(name, at, *shape):
            return nc.alloc_sbuf_tensor_at(name, [P, *shape], F32R, offset=arena_at + at * 4)

        early_places = view_r("early_w0", QT_AT + SLOT, SLOT), view_r("early_w1", QT_AT, SLOT)
        late_places = view_r("late_w0", 0, SLOT), view_r("late_w1", LAT_AT, SLOT)
        high_w = {name: (early_places if name.startswith("in") else late_places)[i % 2] for i, name in enumerate(SPLIT)}
        first_places = view_r("first_w0", S_AT - 2048, SLOT), view_r("first_w1", 0, SLOT)
        high_w.update({name: first_places[i % 2] for i, name in enumerate(FIRST_SPLIT)})
        first_high = view_r("first_high", 6 * D + CONV_TILES * SEQ, KD, SEQ)
        mix_high, mix_low = view_r("mix_high", LAT_AT, KD, SEQ), view_r("mix_low", LAT_AT + KD * SEQ, KD, SEQ)
        ROT_AT, KT_AT = QT_AT - 2816, QT_AT + 2048
        o_low = {"a": view_r("oa_low", LAT_AT - 1024, KF, SEQ), "b": view_r("ob_low", SLOT, KF, SEQ), "c": view_r("oc_low", ROT_AT, KF, SEQ)}
        o_high = {"a": view_r("oa_high", ROT_AT + 1024, KF, SEQ), "b": view_r("ob_high", KT_AT, KF, SEQ), "c": view_r("oc_high", KT_AT + 1024, KF, SEQ)}
        o_low["x"], o_high["x"] = o_low["a"], o_high["a"]
        mg_high, mem_high, hf_high = (view_r(name, v, KD, SEQ) for name, v in (("mg_high", ROT_AT), ("mem_high", KT_AT + 3072), ("hf_high", QT_AT)))
        hx_high, mem_low, h_low = mem_high, view_r("mem_low", S_AT, KD, SEQ), h_t_r
        ff_high, ff_low = view_r("ff_high", KT_AT, KFF, SEQ), view_r("ff_low", TB * PW, KFF, SEQ)

        def bank(name, first, n):
            ap = ctx.enter_context(nc.psum_tensor(f"ps_{name}", [P, n * HALF], F32))
            return Bank(ap, sem(f"{name}_full"), sem(f"{name}_free"))

        G0, G1 = bank("g0", 0, 1), bank("g1", 1, 1)
        S, PT = bank("s", 2, 2), bank("p", 4, 2)
        O, X = bank("o", 6, 1), bank("x", 7, 1)
        G, BANKS = (G0, G1), {"G0": G0, "G1": G1, "S": S, "P": PT, "O": O, "X": X}
        ASIDE = ("bra1", "brb1", "brc1", "out1", "memv", "xo1")

        MOD_ORDER = range(len(MOD_FIRST))


        def mod_bank(i):
            if i in MOD_SUMMED:
                return (S, PT)[MOD_SUMMED.index(i) % 2]
            return G[i // 2 if i < len(MOD_FIRST) else i % 2]

        def mod_cols(i):
            return mod[:, i // 2, i % 2 * HALF:(i % 2 + 1) * HALF]

        def banks_of(part, tag):
            return (S, PT) if part == "layer" and tag in ASIDE else G

        M0, M1, MO, MX = (Bank(b.ap, sem(f"expert_{n}_full"), sem(f"expert_{n}_free"), given)
                          for n, b, given in (("g0", G0, 2), ("g1", G1, 2), ("o", O, 1), ("x", X, 1)))
        EXPERT_BANKS = (M0, M1, MO, MX)

        landed = [sem(f"landed{s}") for s in range(SLOTS)]
        in_x, in_small, in_ln, in_stage, in_route = (sem(n) for n in ("in_x", "in_small", "in_ln", "in_stage", "in_route"))
        in_c, in_vec = sem("in_c"), sem("in_vec")
        consts = sem("consts")
        stored = sem("stored")
        c_tanh, c_ready = sem("c_tanh"), sem("c_ready")
        sp_exp, sp_ln, sp_abs, sp_one = sem("sp_exp"), sem("sp_ln"), sem("sp_abs"), sem("sp_one")
        conv_done, conv_tanhed = sem("conv_done"), sem("conv_tanhed")
        angle_ready, sines_ready = sem("angle_ready"), sem("sines_ready")
        sums_exp, forget_ready = sem("sums_exp"), sem("forget_ready")
        seg_exp, seg_cut, decay_ready = sem("seg_exp"), sem("seg_cut"), sem("decay_ready")
        conv_ready, xdt_ready = sem("conv_ready"), sem("xdt_ready")
        route_in, route_out = sem("route_in"), sem("route_out")
        high_ready = Named(sem("high_ready"), first=(1, FIRST_SPLIT), layer=(LAYERS, SPLIT))
        low_ready = Named(sem("low_ready"), first=(1, FIRST_SPLIT), layer=(LAYERS, SPLIT))
        x_high = Named(sem("x_high"), layer=(LAYERS, SPLIT_X))
        first_low_ready = sem("first_low_ready")
        ff_high_ready, ff_low_ready = sem("ff_high_ready"), sem("ff_low_ready")
        gate_tanhed, ff_used = sem("gate_tanhed"), sem("ff_used")
        picked_ready, rounds_ready, sums_cleared = sem("picked_ready"), sem("rounds_ready"), sem("sums_cleared")
        expert_landed = [sem(f"expert_landed_{name}") for name in PAIR_CHUNKS]
        expert_used = sem("expert_used")
        pick_ready, pick_g_ready = sem("pick_ready"), sem("pick_g_ready")
        expert_tanhed = sem("expert_tanhed")
        z_tanhed = sem("z_tanhed")
        norms = ["mix", "qn", "kvn", "mem", "xattn", "ffn"]
        x_ready = Named(sem("x_ready"), mid=(1, ["x"]), layer=(LAYERS, ["ffn"]))
        squares = Named(sem("squares"), first=(1, ["gy"]), layer=(LAYERS, norms), last=(1, ["out"]))
        var_ready = Named(sem("var_ready"), first=(1, ["h", "gy", "ln1", "h2"]), mid=(1, ["ln2"]), layer=(LAYERS, norms), last=(1, ["out"]))
        rstd_ready = Named(sem("rstd_ready"), first=(1, ["h", "gy", "ln1", "h2"]), mid=(1, ["ln2"]), layer=(LAYERS, norms), last=(1, ["out"]))
        gy_ready = sem("gy_ready")
        rows = Named(sem("rows_ready"), first=(1, ["h_left", "h_right", "gy", "mg", "h2"]),
                     layer=(LAYERS, ["mix", "swa", "nsa", "twice", "lat", "mk", "blk", "hcv", "ob", "mem", "merged", "xattn", "ffn"]))
        masked = Named(sem("scores_masked"), first=(1, [step_tag(s) for s in FOX_STEPS]), layer=(LAYERS, [step_tag(s) for s in LAYER_STEPS]))
        probs = Named(sem("probs_ready"), first=(1, [step_tag(s) for s in FOX_STEPS]), layer=(LAYERS, [step_tag(s) for s in LAYER_STEPS]))
        in_layer, in_mem = sem("in_layer"), sem("in_mem")
        mod_parts = sem("mod_parts")
        g_col_ready, last_used = sem("g_col_ready"), sem("last_used")
        bg_tanhed, cmp_tanhed = sem("bg_tanhed"), sem("cmp_tanhed")
        cmp_exp = sem("cmp_exp")
        last_rows, out_ready = sem("last_rows"), sem("out_ready")
        dve_steps, act_steps, pool_steps = sem("vector_steps"), sem("scalar_steps"), sem("gpsimd_steps")

        used = {}

        def chunk(eng, part, name, rnd=0):
            slot, count, per = PLACE[part, name]
            eng.wait_ge(landed[slot], count + rnd * per)
            return ring[:, slot, :]

        def keys(w, k, n):
            return w[:, 0:k * n].rearrange("p (k n) -> p k n", n=n)

        block = ctx.enter_context(nc.Block())

        @block.tensor
        def _(pe):
            def claim(b, name, rnd=0):
                v = b.turn(name, rnd)
                if not (isinstance(v, int) and v == 0):
                    pe.wait_ge(b.free, v)

            def begin(part):
                per = LAYER_USES if part == "layer" else {}
                for n, b in BANKS.items():
                    b.begin(part, per.get(n, 0))

            def end(rounds=1):
                for n, b in BANKS.items():
                    b.end(rounds)

            def turned(part, tag, n, rnd=0):
                for r in range(max(0, n - 2), n):
                    b = (X, O)[r % 2]
                    pe.wait_ge(b.free, b.nth(part, f"{tag}{r}", rnd))

            def turn_rows(tag, pieces, rnd=0, size=P, ready={}):
                for r in range(0, len(pieces), 2):
                    if r // 2 in ready:
                        pe.wait_ge(*ready[r // 2])
                    b = (X, O)[r // 2 % 2]
                    claim(b, f"{tag}{r // 2}", rnd)
                    for i, piece in enumerate(pieces[r:r + 2]):
                        for tb in range(TB):
                            ins = pe.transpose(b.ap[0:size, i * SEQ + tb * P:i * SEQ + (tb + 1) * P], piece(tb), ident[:, :])
                    ins.then_inc(b.full, 1)

            def weights(part, name, k, n, rnd=0):
                if name in (SPLIT if part == "layer" else FIRST_SPLIT):
                    return split_chunk(name, k, n, rnd, part)
                return keys(chunk(pe, part, name, rnd), k, n)

            def split_chunk(name, k, n, rnd, part="layer"):
                pe.wait_ge(low_ready.sem, low_ready.at(part, name, rnd))
                return keys(high_w[name], k, n), keys(ring_r[:, PLACE[part, name][0], :], k, n)

            def passes(lhs, rhs):
                return [(lhs[0], rhs[0]), (lhs[0], rhs[1]), (lhs[1], rhs[0])] if isinstance(lhs, tuple) else [(lhs, rhs)]

            def product_rows(part, name, tag, lhs, w, nk, lo, n, rnd=0, last=True, blocks=range(TB)):
                for tb in blocks:
                    b = banks_of(part, tag)[tb]
                    claim(b, tag, rnd)
                    both = passes(lhs, w)
                    for k in range(nk):
                        for i, (x, a) in enumerate(both):
                            ins = pe.matmul(b.ap[:, 0:n], x[:, k, tb * P:(tb + 1) * P], a[:, k, lo:lo + n],
                                            start=k == 0 and i == 0, stop=k == nk - 1 and i == len(both) - 1)
                    ins.then_inc(b.full, 1)
                if last:
                    used[part, name] = (b, tag)

            def product_turned(part, name, tag, rhs, w, nk, rnd=0):
                for f in range(4):
                    b = G[f // 2]
                    if f % 2 == 0:
                        claim(b, tag, rnd)
                    for k in range(nk):
                        both = passes(w, rhs)
                        for i, (a, x) in enumerate(both):
                            ins = pe.matmul(b.ap[:, (f % 2) * SEQ:(f % 2 + 1) * SEQ], a[:, k, f * P:(f + 1) * P], x[:, k, :],
                                            start=k == 0 and i == 0, stop=k == nk - 1 and i == len(both) - 1)
                    if f % 2:
                        ins.then_inc(b.full, 1)
                used[part, name] = (G1, tag)

            def product_wide(part, name, lhs, rnd=0):
                w = weights(part, name, KF, D, rnd)
                for half in range(2):
                    product_rows(part, name, f"{name}{half}", lhs, w, KF, half * HALF, HALF, rnd, last=half == 1)

            def score_step(part, step, q, kk, rnd=0):
                kind, pp, qb = step
                nk = keys_of(step)
                claim(S, step_tag(step), rnd)
                s4 = S.ap[:, :].rearrange("p (i n) -> p i n", n=SEQ)
                for i in range(4):
                    half, pr = divmod(i, 2)
                    if kind in ("mla", "x"):
                        head, lo, n = 4 * pp + i, 0, MLA_QK if kind == "mla" else XD
                        ins = pe.matmul(s4[:, i, 0:nk], q[0:n, head, qb * P:(qb + 1) * P], kk[0:n, head, 0:nk], start=True, stop=True)
                        continue
                    lo, pair = HD * half, 2 * pp + pr
                    kpair = pair if kind == "fox" else 0
                    ins = pe.matmul(s4[:, i, 0:nk], q[lo:lo + HD, pair, qb * P:(qb + 1) * P], kk[lo:lo + HD, kpair, 0:nk],
                                    start=True, stop=kind != "fox")
                    if kind == "fox":
                        forget = lambda b: sp[:, 5, b, SSD_HEADS + 2 * pair + half:SSD_HEADS + 2 * pair + half + 1].broadcast_to([P, P])
                        ins = pe.matmul(s4[:, i, 0:nk], forget(0), tri[:, 0:nk], start=False, stop=qb == 0)
                        if qb == 1:
                            ins = pe.matmul(s4[:, i, P:SEQ], forget(1), tri[:, 0:P], start=False, stop=True)
                ins.then_inc(S.full, 1)

            def turn_probs(part, step, rnd=0):
                tag, kbs = step_tag(step), keys_of(step) // P
                p4 = PT.ap[:, :].rearrange("p (i b n) -> p i b n", i=4, b=2)
                pe.wait_ge(probs.sem, probs.at(part, tag, rnd))
                claim(PT, tag, rnd)
                n = masked.parts[part].index(tag)
                for i in range(4):
                    for b in range(kbs):
                        ins = pe.transpose(p4[:, i, b, :], scores[:, n % 2, i, b * P:(b + 1) * P], ident[:, :])
                ins.then_inc(PT.full, 1)

            def output_step(part, step, v, rnd=0, width=HD):
                tag, kbs = step_tag(step), keys_of(step) // P
                claim(O, tag, rnd)
                pe.wait_ge(PT.free, PT.nth(part, tag, rnd))
                for i in range(4):
                    for b in range(kbs):
                        ins = pe.matmul(O.ap[:, i * width:(i + 1) * width], probs_t[:, i, b, :], v(step, i, b),
                                        start=b == 0, stop=b == kbs - 1)
                ins.then_inc(O.full, 1)

            def attention(part, steps, q, kk, v, rnd=0, width=HD, filler=None):
                for step in steps[:2]:
                    score_step(part, step, q, kk(step), rnd)
                for n, step in enumerate(steps):
                    if filler and step in FILLERS:
                        filler(FILLERS[step])
                    turn_probs(part, step, rnd)
                    if n + 2 < len(steps):
                        score_step(part, steps[n + 2], q, kk(steps[n + 2]), rnd)
                    output_step(part, step, v, rnd, width)

            begin("first")
            pe.wait_ge(consts, 1)
            pe.wait_ge(c_ready, 1)
            def modulation(i):
                name, b = MOD_CHUNKS[i], mod_bank(i)
                if i in MOD_SUMMED:
                    pe.wait_ge(mod_parts, MOD_SUMMED.index(i) + 1)
                    claim(b, name)
                    pe.matmul(b.ap[:, 0:HALF], tri[:, P:SEQ], mod_cols(i), start=True, stop=False)
                    used["first", name] = (mod_parts, lambda rnd: MOD_SUMMED.index(i) + 1)
                else:
                    w = keys(chunk(pe, "first", name), KD, HALF)
                    claim(b, name)
                    for k in range(KD):
                        pe.matmul(b.ap[:, 0:HALF], c_act[:, k:k + 1].broadcast_to([P, P]), w[:, k, :], start=k == 0, stop=False)
                    used["first", name] = (b, name)
                if i == MOD_ORDER[0]:
                    pe.wait_ge(in_small, 16)
                    pe.wait_ge(in_stage, 16 * 4)
                if i < len(MOD_FIRST):
                    ins = pe.matmul(b.ap[:, 0:HALF], tri[0:1, P:SEQ], b_mod[0:1, 0, i * HALF:(i + 1) * HALF], start=False, stop=True)
                else:
                    for j in range(HALF // P):
                        row = BIAS_ROW + (i - len(MOD_FIRST)) * (HALF // P) + j
                        ins = pe.matmul(b.ap[:, j * P:(j + 1) * P], ident[BIAS_ROW:, row:row + 1].broadcast_to([P - BIAS_ROW, P]), stage[BIAS_ROW:, :],
                                        start=False, stop=j == HALF // P - 1)
                ins.then_inc(b.full, 1)

            for i in MOD_ORDER:
                modulation(i)

            claim(X, "conv_col")
            n = CONV_TILES * (CONV_K + 1) + KD
            pe.transpose(X.ap[:, 0:n], stage[0:n, :], ident[0:n, 0:n]).then_inc(X.full, 1)

            turn_rows("h", [lambda tb, k=k: h_rows[:, tb, k * P:(k + 1) * P] for k in range(KD)],
                      ready={0: (rows.sem, rows.at("first", "h_left")), 2: (rows.sem, rows.at("first", "h_right"))})
            turned("first", "h", 4)

            w = chunk(pe, "first", "dtf")[:, 0:KD * 24].rearrange("p (k n) -> p k n", n=24)
            product_rows("first", "dtf", "dtf", h_t, w, KD, 0, 24)
            pe.wait_ge(first_low_ready, 1)
            for name in FIRST_SPLIT:
                w, x = weights("first", name, KD, HALF), (first_high, first_low)
                if name in ("v", "z0", "z1", "ga0", "ga1"):
                    product_rows("first", name, name, x, w, KD, 0, HALF)
                else:
                    product_turned("first", name, name, x, w, KD)
            modulation(8)

            def gate_half(name, tb):
                product_rows("first", name, name, h_t, keys(chunk(pe, "first", name), KD, HALF), KD, 0, HALF, last=tb == 1, blocks=(tb,))

            for b in G:
                pe.wait_ge(b.free, b.nth("first", "v"))
            pe.wait_ge(forget_ready, 1)
            attention("first", FOX_STEPS, q_t, lambda s: k_t, lambda s, i, b: v_rows[
                :, b, (2 * (2 * s[1] + i % 2) + i // 2) * HD:(2 * (2 * s[1] + i % 2) + i // 2 + 1) * HD], filler=lambda half: gate_half(*half))
            pe.wait_ge(O.free, O.nth("first", step_tag(FOX_STEPS[-1])))
            turn_rows("fox", [lambda tb, k=k: fox_o[:, tb, k * P:(k + 1) * P] for k in range(KF)])
            turned("first", "fox", 2)
            product_wide("first", "att", fox_ot)

            claim(X, "sums")
            a_in = dt_a[:, 1, :, :].rearrange("p t h -> p (t h)")
            pe.matmul(X.ap[:, 0:32], tri[:, 0:P], a_in, start=True, stop=True)
            pe.matmul(X.ap[:, 32:64], tri[:, P:SEQ], a_in, start=True, stop=True).then_inc(X.full, 1)
            pe.wait_ge(conv_ready, 4)
            claim(O, "b_rows")
            for g in range(SSD_GROUPS):
                ins = pe.transpose(O.ap[:, g * P:(g + 1) * P], conv[:, 8 + g, 0:P], ident[:, :])
            ins.then_inc(O.full, 1)
            for r in range(4):
                tb, half = divmod(r, 2)
                b = (X, O)[r % 2]
                claim(b, f"xs{r}")
                for i in range(4):
                    ins = pe.transpose(b.ap[:, i * P:(i + 1) * P], conv[:, 4 * half + i, tb * P:(tb + 1) * P], ident[:, :])
                ins.then_inc(b.full, 1)
            claim(S, "cb")
            for c in range(TB):
                for g in range(SSD_GROUPS):
                    ins = pe.matmul(S.ap[:, (c * SSD_GROUPS + g) * P:(c * SSD_GROUPS + g + 1) * P], conv[:, 8 + g, c * P:(c + 1) * P],
                                    conv[:, 12 + g, c * P:(c + 1) * P], start=True, stop=True)
            ins.then_inc(S.full, 1)
            for c in range(TB):
                for g in range(SSD_GROUPS):
                    b = G[g % 2]
                    claim(b, f"seg{c}{g}")
                    for r in range(SSD_R):
                        h = g * SSD_R + r
                        ins = pe.matmul(b.ap[:, r * P:(r + 1) * P], dt_a[:, 1, c, h:h + 1].broadcast_to([P, P]), tri[:, 0:P],
                                        start=True, stop=True)
                    ins.then_inc(b.full, 1)
            gate_half("gs1", 0)
            pe.wait_ge(xdt_ready, 1)
            pe.wait_ge(O.free, O.nth("first", "b_rows"))
            claim(S, "states")
            for g in range(SSD_GROUPS):
                ins = pe.matmul(S.ap[:, g * SEQ:(g + 1) * SEQ], b_rows[:, g, :],
                                x_end[:, g * SSD_R:(g + 1) * SSD_R, :].rearrange("p h d -> p (h d)"), start=True, stop=True)
            ins.then_inc(S.full, 1)
            gate_half("gs1", 1)
            modulation(9)
            for c in range(TB):
                claim(PT, f"yd{c}")
                for g in range(SSD_GROUPS):
                    pe.wait_ge(decay_ready, c * SSD_GROUPS + g + 1)
                    for r in range(SSD_R):
                        h = g * SSD_R + r
                        ins = pe.matmul(PT.ap[:, h * SSD_P:(h + 1) * SSD_P], decay[:, c * SSD_GROUPS + g, r, :], xdt[:, c, h, :],
                                        start=True, stop=True)
                ins.then_inc(PT.full, 1)
            pe.wait_ge(S.free, S.nth("first", "states"))
            claim(S, "yo")
            for g in range(SSD_GROUPS):
                ins = pe.matmul(S.ap[:, g * SEQ:(g + 1) * SEQ], conv[:, 12 + g, P:SEQ], states[:, g, :], start=True, stop=True)
            ins.then_inc(S.full, 1)
            modulation(4)
            pe.wait_ge(rows.sem, rows.at("first", "gy"))
            turn_rows("gy", [lambda tb, k=k: ssd_y[:, tb, k * P:(k + 1) * P] for k in range(KD)])
            turned("first", "gy", 4)
            for name in ["so0", "so1"]:
                product_rows("first", name, name, y_turned, keys(chunk(pe, "first", name), KD, HALF), KD, 0, HALF)

            modulation(10)
            modulation(5)
            pe.wait_ge(rows.sem, rows.at("first", "mg"))
            turn_rows("mg", [lambda tb, k=k: gate_att[:, tb, k * P:(k + 1) * P] for k in range(KD)])
            turned("first", "mg", 4)
            for name in ["o0", "o1"]:
                product_rows("first", name, name, h_t, keys(chunk(pe, "first", name), KD, HALF), KD, 0, HALF)

            modulation(11)
            modulation(6)
            modulation(7)

            pe.wait_ge(rows.sem, rows.at("first", "h2"))
            turn_rows("h2", [lambda tb, k=k: h_rows[:, tb, k * P:(k + 1) * P] for k in range(KD)])
            turned("first", "h2", 4)
            pe.wait_ge(in_route, 32)
            product_rows("first", "route", "route", h_t, route_w, KD, 0, N_GROUPS + N_EXPERTS)

            pe.wait_ge(picked_ready, 1)
            claim(X, "places")
            upto, ones = tri[:, 0:P], tri[:, P:SEQ]
            pe.matmul(X.ap[:, 0:16], upto, picked[:, 0, :], start=True, stop=True)
            pe.matmul(X.ap[:, 16:32], ones, picked[:, 0, :], start=True, stop=False)
            pe.matmul(X.ap[:, 16:32], upto, picked[:, 1, :], start=False, stop=True)
            pe.matmul(X.ap[:, 32:48], ones, picked[:, 0, :], start=True, stop=False)
            pe.matmul(X.ap[:, 32:48], ones, picked[:, 1, :], start=False, stop=True)
            pe.matmul(X.ap[:, 48:48 + SLOT_TOKENS], ones, tri[:, 0:SLOT_TOKENS], start=True, stop=True).then_inc(X.full, 1)
            end()

            def gather(q, name="taken"):
                pe.wait_ge(pick_ready, q + 1)
                for j, b in enumerate((MO, MX)):
                    claim(b, name, q - 1)
                    for i in range(4):
                        k = 4 * j + i
                        for tb in range(TB):
                            ins = pe.matmul(b.ap[:, i * P:(i + 1) * P], h_rows[:, tb, k * P:(k + 1) * P], pick[:, tb, :],
                                            start=tb == 0, stop=tb == TB - 1)
                    ins.then_inc(b.full, 1)

            def scatter(start=False, stop=False):
                for tb, b in enumerate((S, PT)):
                    for half in range(2):
                        ins = pe.matmul(b.ap[:, half * HALF:(half + 1) * HALF], pick_t[:, 0, tb * P:(tb + 1) * P],
                                        pair_y[:, 0, half * HALF:(half + 1) * HALF], start=start, stop=stop)
                    if stop:
                        ins.then_inc(b.full, 1)

            begin("mid")
            pe.wait_ge(sums_cleared, 1)
            claim(S, "sums")
            claim(PT, "sums")
            scatter(start=True)
            for b in EXPERT_BANKS:
                b.begin("start", 0)
            pe.wait_ge(rounds_ready, 1)
            n_pairs = pe.value_load(rounds_i[0:1, 1:2], min_val=PAIRS, max_val=PAIRS * ROUNDS)
            gather(0, "taken")
            for b in EXPERT_BANKS:
                b.end(1)
            for b, n in ((M0, 2), (M1, 2), (MO, 2), (MX, 2)):
                b.begin("moe", n)
            for b in (MO, MX):
                pe.wait_ge(b.free, b.nth("start", "taken"))
            with pe.Fori(0, n_pairs) as q:
                def pair_weights(j):
                    pe.wait_ge(expert_landed[j], q * 16 + 16)
                    return pair_w[j]

                for b in (MO, MX):
                    pe.wait_ge(b.free, q * 2 + 1)
                claim(M0, "gate", q)
                claim(M1, "up", q)
                for e in range(2):
                    lanes = slice(e * SLOT_TOKENS, (e + 1) * SLOT_TOKENS)
                    for kind, b in enumerate((M0, M1)):
                        w = keys(pair_weights(2 * e + kind), KD, HALF)
                        for k in range(KD):
                            ins = pe.matmul(b.ap[lanes, :], taken_t[:, k, lanes], w[:, k, :], start=k == 0, stop=k == KD - 1)
                        ins.then_inc(expert_used if e == 0 else b.full, 1)
                for y in (MO, MX):
                    pe.wait_ge(y.free, q * 2 + 2)
                pe.wait_ge(M1.free, q * 2 + M1.given)
                scatter()
                pe.wait_ge(M1.free, M1.nth("moe", "up", q))
                claim(M0, "hid", q)
                for k in range(KF):
                    ins = pe.transpose(M0.ap[:, k * P:(k + 1) * P], expert_t[:, 0, k * P:(k + 1) * P], ident[:, :])
                ins.then_inc(M0.full, 1)
                claim(M1, "turned", q)
                pe.wait_ge(pick_g_ready, q + 1)
                for tb in range(TB):
                    ins = pe.transpose(M1.ap[:, tb * P:(tb + 1) * P], pick_g[:, tb, :], ident[:, :])
                ins.then_inc(M1.full, 1)
                gather(q + 1)
                pe.wait_ge(M0.free, M0.nth("moe", "hid", q))
                for e in range(2):
                    wd = keys(pair_weights(4 + e), KF, D)
                    lanes = slice(e * SLOT_TOKENS, (e + 1) * SLOT_TOKENS)
                    for half, y in enumerate((MO, MX)):
                        if e == 0:
                            claim(y, "out", q)
                        for k in range(KF):
                            ins = pe.matmul(y.ap[lanes, :], hid_t[:, k, lanes], wd[:, k, half * HALF:(half + 1) * HALF],
                                            start=k == 0, stop=k == KF - 1)
                        if e == 1:
                            ins.then_inc(y.full, 1)
                    if e == 0:
                        ins.then_inc(expert_used, 1)
            for y in (MO, MX):
                pe.wait_ge(y.free, n_pairs * 2 + 2)
            pe.wait_ge(M1.free, n_pairs * 2 + M1.given)
            scatter(stop=True)
            end()

            begin("layer")
            with pe.Fori(0, LAYERS) as l:
                claim(X, "g_col", l)
                pe.wait_ge(in_layer, 16 * 11 + l * (16 * 11))
                pe.transpose(X.ap[:, 0:G_END], stage[0:G_END, :], ident[0:G_END, 0:G_END]).then_inc(X.full, 1)
                pe.wait_ge(rows.sem, rows.at("layer", "mix", l))
                turn_rows("mix", [lambda tb, k=k: h_rows[:, tb, k * P:(k + 1) * P] for k in range(KD)], l)
                turned("layer", "mix", 4, l)
                for i in IN_ORDER:
                    n = IN_AT[i + 1] - IN_AT[i]
                    product_rows("layer", f"in{i}", f"in{i}", (mix_high, mix_low), split_chunk(f"in{i}", KD, n, l), KD, 0, n, l)

                def gate_product(name):
                    product_rows("layer", name, name, h_t, keys(chunk(pe, "layer", name, l), KD, HALF), KD, 0, HALF, l)

                gate_product("g0")

                pe.wait_ge(rows.sem, rows.at("layer", "lat", l))
                turn_rows("lat", [lambda tb, k=k: lat[:, tb, k * P:(k + 1) * P] for k in range(5)], l)
                turned("layer", "lat", 3, l)
                n = HEADS * MLA_QK
                w = chunk(pe, "layer", "qb", l)[:, 0:3 * n].rearrange("p (k n) -> p k n", n=n)
                product_rows("layer", "qb", "qb0", lat_t, w, 3, 0, HALF, l, last=False)
                product_rows("layer", "qb", "qb1", lat_t, w, 3, HALF, n - HALF, l)
                w = keys(chunk(pe, "layer", "kvb", l), 2, D)
                product_rows("layer", "kvb", "kvb0", lat_t[:, 3:5, :], w, 2, 0, HALF, l, last=False)
                product_rows("layer", "kvb", "kvb1", lat_t[:, 3:5, :], w, 2, HALF, HALF, l)

                def pair(src, lo, i):
                    return lambda tb: src[:, tb, lo + i * P:lo + (i + 1) * P]

                pe.wait_ge(rows.sem, rows.at("layer", "twice", l))
                turn_rows("nsc", [pair(kc_twice, 0, i) for i in range(4)], l)
                pe.wait_ge(rows.sem, rows.at("layer", "swa", l))
                turn_rows("swa", [pair(swa_r, 0, i) for i in range(4)] + [lambda tb: swa_r[:, tb, 512:640]], l)
                turned("layer", "swa", 3, l)
                attention("layer", SWA_STEPS, qt, lambda s: kt, lambda s, i, b: proj[:, b, C_AV + HD * (i // 2):C_AV + HD * (i // 2 + 1)], l,
                          filler=gate_product)

                pe.wait_ge(rows.sem, rows.at("layer", "nsa", l))
                turn_rows("nsr", [pair(proj, C_BQ, i) for i in range(4)], l)
                turn_rows("nsq", [pair(nsa_q, 0, i) for i in range(4)]
                          + [lambda tb: nsa_k[:, tb, 0:P], lambda tb: nsa_k[:, tb, P:2 * P]], l)
                gate_product("g2")
                w = ring[:, PLACE["layer", "cmp"][0], 0:2 * 16 * HD].rearrange("p (v j n) -> p v j n", v=2, j=16)
                chunk(pe, "layer", "cmp", l)
                pe.wait_ge(rows.sem, rows.at("layer", "blk", l))
                claim(X, "cmph", l)
                for v in range(2):
                    for j in range(16):
                        ins = pe.matmul(X.ap[0:HD, v * 2 * CMP:(v + 1) * 2 * CMP], w[:, v, j, :], cmp_blk[:, v, j, :], start=j == 0, stop=j == 15)
                ins.then_inc(X.full, 1)
                used["layer", "cmp"] = (X, "cmph")
                gate_product("g3")
                pe.wait_ge(rows.sem, rows.at("layer", "hcv", l))
                claim(O, "cmpkv", l)
                pe.matmul(O.ap[:, 0:2 * CMP], w2_k[:, :, :].rearrange("p a b -> p (a b)"),
                          cmp_h[:, 2, :, :].rearrange("p g n -> p (g n)"), start=True, stop=True)
                pe.matmul(O.ap[:, 64:64 + HD], cmp_hv[:, :, :, :].rearrange("p g h n -> p (g h n)"), w2_v[:, :], start=True, stop=True)\
                    .then_inc(O.full, 1)
                pe.wait_ge(O.free, O.nth("layer", "cmpkv", l))
                turned("layer", "nsr", 2, l)
                for qb in range(TB):
                    tag = f"cmp0{qb}"
                    claim(S, tag, l)
                    for h in range(HEADS):
                        f, pr = divmod(h, 4)
                        ins = pe.matmul(S.ap[:, f * HALF + pr * CMP:f * HALF + (pr + 1) * CMP], qt[f * HD:(f + 1) * HD, pr, qb * P:(qb + 1) * P],
                                        cmp_k[f * HD:(f + 1) * HD, f * CMP:(f + 1) * CMP], start=True, stop=True)
                    ins.then_inc(S.full, 1)
                gate_product("g4")
                for qb in range(TB):
                    tag = f"cmp0{qb}"
                    n = masked.parts["layer"].index(tag)
                    pe.wait_ge(probs.sem, probs.at("layer", tag, l))
                    claim(PT, tag, l)
                    pe.transpose(PT.ap[:, 0:P], scores[:, n % 2, 0, 0:P], ident[:, :]).then_inc(PT.full, 1)
                    claim(O, tag, l)
                    pe.wait_ge(PT.free, PT.nth("layer", tag, l))
                    pe.matmul(O.ap[:, :], probs_t[:, 0, 0, :], cmp_v[:, :, :].rearrange("p h d -> p (h d)"), start=True, stop=True)\
                        .then_inc(O.full, 1)
                turned("layer", "nsq", 3, l)
                place_of = {"sel": (0, C_VS), "win": (1, C_VW)}
                attention("layer", SEL_STEPS + WIN_STEPS, qt[:, 4:8, :], lambda s: kt[:, place_of[s[0]][0]:place_of[s[0]][0] + 1, :],
                          lambda s, i, b: proj[:, b, place_of[s[0]][1] + HD * (i // 2):place_of[s[0]][1] + HD * (i // 2 + 1)], l, filler=gate_product)

                pe.wait_ge(rows.sem, rows.at("layer", "mk", l))
                turn_rows("mq", [lambda tb, h=h: mla_q[:, tb, h * MLA_QK:(h + 1) * MLA_QK] for h in range(HEADS)], l, MLA_QK)
                turn_rows("mk", [lambda tb, h=h: mla_k[:, tb, h * MLA_QK:(h + 1) * MLA_QK] for h in range(HEADS)], l, MLA_QK)
                turned("layer", "mk", 4, l)
                attention("layer", MLA_STEPS, qt, lambda s: kt, lambda s, i, b: kv_rows[:, b, (4 * s[1] + i) * P + HD:(4 * s[1] + i + 1) * P], l)

                for name, src in (("a", o_a), ("b", o_b), ("c", o_c)):
                    if name == "b":
                        pe.wait_ge(rows.sem, rows.at("layer", "ob", l))
                    else:
                        pe.wait_ge(O.free, O.nth("layer", step_tag((SWA_STEPS if name == "a" else MLA_STEPS)[-1]), l))
                    turn_rows(f"o{name}", [lambda tb, k=k, s=src: s[:, tb, k * P:(k + 1) * P] for k in range(KF)], l)
                for name in "abc":
                    if name == "c":
                        pe.wait_ge(rows.sem, rows.at("layer", "mem", l))
                        turn_rows("mem", [lambda tb, k=k: mem_rows[:, tb, k * P:(k + 1) * P] for k in range(KD)], l)
                    turned("layer", f"o{name}", 2, l) if name != "c" else turned("layer", "mem", 4, l)
                    product_wide("layer", f"br{name}", (o_high[name], o_low[name]), l)
                product_turned("layer", "memk", "memk", (mem_high, mem_low), split_chunk("memk", KD, HALF, l), KD, l)
                pe.wait_ge(rows.sem, rows.at("layer", "merged", l))
                turn_rows("mg", [lambda tb, k=k: merged[:, tb, k * P:(k + 1) * P] for k in range(KD)], l)
                turned("layer", "mg", 4, l)
                for name in ["out0", "out1"]:
                    product_rows("layer", name, name, (mg_high, h_low), split_chunk(name, KD, HALF, l), KD, 0, HALF, l)

                product_rows("layer", "memv", "memv", (mem_high, mem_low), split_chunk("memv", KD, HALF, l), KD, 0, HALF, l)
                pe.wait_ge(rows.sem, rows.at("layer", "xattn", l))
                turn_rows("hx", [lambda tb, k=k: h_rows[:, tb, k * P:(k + 1) * P] for k in range(KD)], l)
                turned("layer", "hx", 4, l)
                product_turned("layer", "xq", "xq", (hx_high, h_low), split_chunk("xq", KD, HALF, l), KD, l)
                for b in G:
                    pe.wait_ge(b.free, b.nth("layer", "xq", l))
                attention("layer", X_STEPS, qt, lambda s: kt, lambda s, i, b: mem_v[:, b, i * XD:(i + 1) * XD], l, XD)
                pe.wait_ge(O.free, O.nth("layer", step_tag(X_STEPS[-1]), l))
                turn_rows("ox", [lambda tb, k=k: o_a[:, tb, k * P:(k + 1) * P] for k in range(KF)], l)
                turned("layer", "ox", 2, l)
                product_wide("layer", "xo", (o_high["x"], o_low["x"]), l)

                pe.wait_ge(rows.sem, rows.at("layer", "ffn", l))
                turn_rows("hf", [lambda tb, k=k: h_rows[:, tb, k * P:(k + 1) * P] for k in range(KD)], l)
                turned("layer", "hf", 4, l)
                for c in range(KFF // 2):
                    product_turned("layer", f"gu{c}", f"gu{c}", (hf_high, h_low), split_chunk(f"gu{c}", KD, HALF, l), KD, l)
                claim(S, "ffd", l)
                claim(PT, "ffd", l)
                for c in range(6):
                    w = split_chunk(f"fd{c}", KF if c < 5 else KFF - 20, D, l)
                    for k in range(4 * c, min(4 * c + 4, KFF)):
                        if k % 2 == 0:
                            pe.wait_ge(ff_low_ready, l * (KFF // 2) + k // 2 + 1)
                        for tb, b in enumerate((S, PT)):
                            for half in range(2):
                                for i, (a, x) in enumerate(passes((ff_high, ff_low), w)):
                                    ins = pe.matmul(b.ap[:, half * HALF:(half + 1) * HALF], a[:, k, tb * P:(tb + 1) * P],
                                                    x[:, k - 4 * c, half * HALF:(half + 1) * HALF],
                                                    start=k == 0 and i == 0, stop=k == KFF - 1 and i == 2)
                            if k == KFF - 1:
                                ins.then_inc(b.full, 1)
                    if c < 5:
                        ins.then_inc(ff_used, 1)
                        used["layer", f"fd{c}"] = (ff_used, lambda rnd, c=c: 5 * rnd + c + 1)
                used["layer", "fd5"] = (PT, "ffd")
            end(LAYERS)

        @block.sync
        def _(sync):
            last = [None] * SLOTS

            def sources(part, name, rnd):
                def cols(w, lo, n):
                    return w.rearrange("(k p) n -> p k n", p=P)[:, :, lo:lo + n]
                if part == "first":
                    if name.startswith("mod"):
                        return [t["w_mod"][0].rearrange("(p k) n -> p k n", p=P)[:, :, int(name[3:]) * HALF:(int(name[3:]) + 1) * HALF]]
                    if name == "dtf":
                        return [cols(t["w_in"][0], OFF_DT, SSD_HEADS), cols(t["w_in"][0], OFF_F, FOX_HEADS)]
                    if name == "att":
                        return [cols(t["w_att_o"][0], 0, D)]
                    i = int(name[-1]) if name[-1].isdigit() else 0
                    w, off = {"xbc": ("w_in", OFF_XBC), "q": ("w_in", OFF_Q), "k": ("w_in", OFF_K), "v": ("w_in", OFF_V), "z": ("w_in", OFF_Z),
                              "ga": ("w_in", OFF_GA), "gs": ("w_in", OFF_GS), "so": ("w_ssd_o", 0), "o": ("w_o", 0)}[name.rstrip("0123456789")]
                    return [cols(t[w][0], off + i * HALF, HALF)]
                i = int(name[-1]) if name[-1].isdigit() else 0
                if name.startswith("in"):
                    return [cols(t["w_in_2"][rnd], IN_AT[i], IN_AT[i + 1] - IN_AT[i])]
                if name.startswith("gu"):
                    i = int(name[2:])
                    return [cols(t["w_gate_up_2"][rnd], i * SEQ, SEQ), cols(t["w_gate_up_2"][rnd], D_FF + i * SEQ, SEQ)]
                if name.startswith("g"):
                    return [cols(t["w_in_2"][rnd], C_G + i * HALF, HALF)]
                if name == "cmp":
                    return [t[w][rnd].rearrange("(j p) n -> p j n", p=P) for w in ("nsa_wk1_2", "nsa_wv1_2")]
                if name.startswith("fd"):
                    return [cols(t["w_down_2"][rnd][i * HALF:min((i + 1) * HALF, D_FF), :], 0, D)]
                w, lo, n = {"qb": ("mla_w_q_b_2", 0, HEADS * MLA_QK), "kvb": ("mla_w_kv_b_2", 0, D), "bra": ("w_br_a_2", 0, D),
                            "brb": ("w_br_b_2", 0, D), "brc": ("w_br_c_2", 0, D), "out": ("w_out_2", i * HALF, HALF),
                            "memk": ("w_xkv_2", 0, HALF), "memv": ("w_xkv_2", HALF, HALF), "xq": ("w_xq_2", 0, HALF),
                            "xo": ("w_xo_2", 0, D)}[name.rstrip("0123456789")]
                return [cols(t[w][rnd], lo, n)]

            PAIRED = ("in0", "in2")

            def load(part, name, rnd=0):
                slot, before = PLACE[part, name][0], last[PLACE[part, name][0]]
                if before:
                    where, use = used[before[0], before[1]]
                    if isinstance(where, Bank):
                        sync.wait_ge(where.full, where.nth(before[0], use, before[2]))
                    else:
                        sync.wait_ge(where, use(before[2]))
                pieces = sources(part, name, rnd)
                if name == "cmp":
                    dst = ring[:, slot, 0:2 * 16 * HD].rearrange("p (v j n) -> p v j n", v=2, j=16)
                    dsts = [dst[:, 0], dst[:, 1]]
                elif part == "layer" and name in PAIRED:
                    dst = ring[:, slot, :].rearrange("p (k r f d) -> p k f r d", k=KD, f=2, d=HD)
                    src = pieces[0].rearrange("p k (f r d) -> p k f r d", f=2, d=HD)
                    dsts, pieces = ([v[:, k, f] for k in range(KD) for f in range(2)] for v in (dst, src))
                else:
                    n = sum(s.shape[2] for s in pieces)
                    dst = ring[:, slot, 0:pieces[0].shape[1] * n].rearrange("p (k n) -> p k n", n=n)
                    at_n = np.cumsum([0] + [s.shape[2] for s in pieces])
                    dsts = [dst[:, :, int(at_n[j]):int(at_n[j + 1])] for j in range(len(pieces))]
                for d, s in zip(dsts, pieces):
                    sync.dma_start(d, s).then_inc(landed[slot], 16)
                last[slot] = (part, name, rnd)

            sync.dma_start(c_col[:, :], t["c"].rearrange("a (p k) -> p (a k)", p=P)).then_inc(in_c, 16)
            for name in FIRST_CHUNKS:
                load("first", name)
            for name, use, rnd in last:
                where, what = used[name, use]
                if isinstance(where, Bank):
                    sync.wait_ge(where.full, where.nth(name, what, rnd))
                else:
                    sync.wait_ge(where, what(rnd))

            done_with = {"gate0": (expert_used, lambda q: q * 3 + 5), "up0": (expert_used, lambda q: q * 3 + 6),
                         "gate1": (M0.full, lambda q: M0.nth("moe", "gate", q)), "up1": (M1.full, lambda q: M1.nth("moe", "up", q)),
                         "down0": (expert_used, lambda q: q * 3 + 7), "down1": (MX.full, lambda q: MX.nth("moe", "out", q))}

            def load_pair(p, q):
                for j, name in enumerate(PAIR_CHUNKS):
                    where, count = done_with[name]
                    sync.wait_ge(where, count(q - 1))
                    w = t[f"w_{name[:-1]}"][0, p * 2 + int(name[-1])].rearrange("(k p) n -> p k n", p=P)
                    sync.dma_start(keys(pair_w[j], w.shape[1], w.shape[2]), w).then_inc(expert_landed[j], 16)

            with sync.Fori(0, PAIRS) as p:
                load_pair(p, p)
            sync.wait_ge(rounds_ready, 1)
            n_rounds = sync.value_load(rounds_i[0:1, 0:1], min_val=1, max_val=ROUNDS)
            with sync.If(n_rounds > 1):
                with sync.Fori(1, n_rounds) as again:
                    with sync.Fori(0, PAIRS) as p:
                        load_pair(p, again * PAIRS + p)
            for s in range(SLOTS):
                where, count = done_with[PAIR_CHUNKS[s]]
                used["moe", f"slot{s}"] = (where, lambda rnd, count=count: count(n_rounds * PAIRS - 1))
                last[s] = ("moe", f"slot{s}", 0)
            for rnd in range(LAYERS):
                for name in LAYER_CHUNKS:
                    load("layer", name, rnd)
            sync.wait_ge(out_ready, 1)
            sync.dma_start(out[0].rearrange("(b p) n -> p b n", p=P), h_rows[:, :, :]).then_inc(stored, 16)
            sync.wait_ge(stored, 16)

        @block.gpsimd
        def _(pool):
            st = Steps(pool, pool_steps)
            st.done(pool.memset(ident[:, :], 0.0))
            st.done(pool.memset(tri[:, :], 1.0))
            st.done(pool.memset(causal[:, :], 0.0))
            st.done(pool.memset(cmp_mask[:, :, :], 0.0))
            st.done(pool.memset(head_of[:, :], 1.0))
            st.done(pool.memset(half_power[:, :], -0.5))
            st.done(pool.memset(xbc_pad[:, :, 0:CONV_K - 1], 0.0))
            st.settle()
            for i in range(HD // 2):
                st.done(pool.memset(inv_freq[:, i:i + 1], float(np.float32(10000.0) ** np.float32(-i / (HD // 2)))))
            for i in range(PER_GROUP):
                st.done(pool.memset(back[:, i:i + 1], float(PER_GROUP - i)))
            st.done(pool.affine_select(out=ident[:, :], in_=ident[:, :], compare_op=ALU.not_equal, fill=1.0, base=0,
                                       pattern=[[-1, P]], channel_multiplier=1))
            st.done(pool.affine_select(out=tri[:, :], in_=tri[:, :], compare_op=ALU.is_ge, fill=0.0, base=0,
                                       pattern=[[1, SEQ]], channel_multiplier=-1))
            st.done(pool.affine_select(out=causal[:, :], in_=causal[:, :], compare_op=ALU.is_ge, fill=MASKED, base=P,
                                       pattern=[[-1, SEQ]], channel_multiplier=1))
            st.done(pool.affine_select(out=cmp_mask[:, :, :], in_=cmp_mask[:, :, :], compare_op=ALU.is_ge, fill=MASKED,
                                       base=1 - CMP_BLOCK, pattern=[[P, TB], [-CMP_STRIDE, CMP]], channel_multiplier=1))
            st.done(pool.affine_select(out=head_of[:, :], in_=head_of[:, :], compare_op=ALU.is_ge, fill=0.0, base=0,
                                       pattern=[[-CMP, HEADS]], channel_multiplier=1))
            st.settle()
            st.done(pool.affine_select(out=windowed[:, :], in_=causal[:, :], compare_op=ALU.is_ge, fill=MASKED, base=-1,
                                       pattern=[[1, SEQ]], channel_multiplier=-1))
            st.done(pool.affine_select(out=head_of[:, :], in_=head_of[:, :], compare_op=ALU.is_ge, fill=0.0, base=CMP - 1,
                                       pattern=[[CMP, HEADS]], channel_multiplier=-1))
            st.settle()
            pool.sem_inc(consts, 1)

            def root(part, name, rnd=0):
                pool.wait_ge(var_ready.sem, var_ready.at(part, name, rnd))
                pool.tensor_tensor(rstd[:, :], var_in[:, :], half_power[:, :], ALU.pow).then_inc(rstd_ready.sem, 1)

            root("first", "h")
            for i in range(TB * SSD_GROUPS):
                b = G[i % SSD_GROUPS % 2]
                pool.wait_ge(b.free, b.nth("first", f"seg{i // SSD_GROUPS}{i % SSD_GROUPS}"))
                pool.affine_select(out=decay[:, i], in_=decay[:, i], compare_op=ALU.is_ge, fill=-MASKED, base=0,
                                   pattern=[[0, SSD_R], [1, P]], channel_multiplier=-1).then_inc(seg_cut, 1)
            for name in ["gy", "ln1", "h2"]:
                root("first", name)
            root("mid", "ln2")
            with pool.Fori(0, LAYERS) as l:
                for name in var_ready.parts["layer"]:
                    root("layer", name, l)
            root("last", "out")

        @block.scalar
        def _(act):
            st = Steps(act, act_steps)
            act.wait_ge(in_c, 16)
            act.activation(c_act[:, :], c_col[:, :], ACT.Tanh, scale=0.5).then_inc(c_tanh, 1)
            act.dma_start(stage[0:64, :], t["conv_w"][0].rearrange("j (t p) -> (j t) p", p=P)).then_inc(in_stage, 16)
            act.dma_start(stage[64:80, :], t["conv_b"][0].rearrange("(t p) -> t p", p=P)).then_inc(in_stage, 16)
            act.dma_start(stage[80:88, :], t["ssd_norm_w"][0].rearrange("(t p) -> t p", p=P)).then_inc(in_stage, 16)
            act.dma_start(stage[BIAS_ROW:, :], t["b_mod"][0, 2 * D:].rearrange("(t p) -> t p", p=P)).then_inc(in_stage, 16)
            act.dma_start(b_mod[0:1, :, :].rearrange("p a n -> p (a n)"), t["b_mod"][:, 0:2 * D]).then_inc(in_small, 16)
            act.dma_start(x_rows[:, :, :], t["x"][0].rearrange("(b p) n -> p b n", p=P)).then_inc(in_x, 16)
            for dst, src in ((bias24[:, 0:SSD_HEADS], "dt_bias"), (bias24[:, SSD_HEADS:], "forget_b"), (a_log_b[:, :], "a_log"),
                             (d_skip_b[:, :], "d_skip"), (route_b[:, 0:N_GROUPS], "b_router_group"), (route_b[:, N_GROUPS:], "b_router_expert")):
                act.dma_start(dst, t[src].broadcast_to([P, dst.shape[1]])).then_inc(in_vec, 16)
            act.dma_start(pos_i[:, :], t["positions_2"].rearrange("a (b p) -> p (a b)", p=P)).then_inc(in_vec, 16)
            act.dma_start(route_w[:, :, 0:N_GROUPS], t["w_router_group"][0].rearrange("(k p) n -> p k n", p=P)).then_inc(in_route, 16)
            act.dma_start(route_w[:, :, N_GROUPS:], t["w_router_expert"][0].rearrange("(k p) n -> p k n", p=P)).then_inc(in_route, 16)

            def copy_turned(part, tag, n, dst, rnd=0, size=P):
                for r in range(n):
                    b = (X, O)[r % 2]
                    d = dst(r)
                    act.wait_ge(b.full, b.nth(part, f"{tag}{r}", rnd))
                    act.activation(d, b.ap[0:size, 0:d.shape[1] * SEQ].rearrange("p (k n) -> p k n", n=SEQ), ACT.Copy).then_inc(b.free, 1)

            def take(part, name, dst, func=ACT.Copy, scale=1.0, rnd=0):
                for i, b in enumerate(banks_of(part, name)):
                    d = dst(i)
                    act.wait_ge(b.full, b.nth(part, name, rnd))
                    src = b.ap[:, 0:d.free_size()]
                    if len(d.shape) == 3:
                        src = src.rearrange("p (a n) -> p a n", n=d.shape[2])
                    act.activation(d, src, func, scale=scale).then_inc(b.free, 1)

            def square_rows(part, name, src, junk, rnd=0):
                act.activation(junk(0), src(0), ACT.Square, accum_out=square_sum[:, 0:1])
                act.activation(junk(1), src(1), ACT.Square, accum_out=square_sum[:, 1:2]).then_inc(squares.sem, 1)

            def make_high(name, rnd, *free, part="layer"):
                slot, count, per = PLACE[part, name]
                act.wait_ge(landed[slot], count + rnd * per)
                for where, value in free:
                    act.wait_ge(where, value)
                n = chunk_size(name)
                act.activation(high_w[name][:, 0:n], ring[:, slot, 0:n], ACT.Copy).then_inc(high_ready.sem, 1)

            def turned_high(tag, tiles, dst, rnd, gains=None):
                for k in range(tiles):
                    b, i = (X, O)[k // 2 % 2], k % 2
                    if i == 0:
                        act.wait_ge(b.full, b.nth("layer", f"{tag}{k // 2}", rnd))
                    if gains is not None:
                        ins = act.activation(dst[:, k, :], b.ap[:, i * SEQ:(i + 1) * SEQ], ACT.Copy, scale=gains[:, k:k + 1])
                    elif i == 1:
                        ins = act.activation(dst[:, k - 1:k + 1, :], b.ap[:, :].rearrange("p (k n) -> p k n", n=SEQ), ACT.Copy)
                    if i == 1:
                        ins.then_inc(x_high.sem, 1)

            def exp_step(part, step, rnd=0):
                tag, nk = step_tag(step), keys_of(step)
                n = masked.parts[part].index(tag)
                act.wait_ge(masked.sem, masked.at(part, tag, rnd))
                if step[0] == "swa":
                    act.activation(sink_e[:, n % 4, 4:8], sink_e[:, n % 4, 0:4], ACT.Exp)
                for i in range(4):
                    s = scores[:, n % 2, i, 0:nk]
                    ins = act.activation(s, s, ACT.Exp, bias=neg_max[:, n % 2, i:i + 1], scale=-1.0, accum_out=den[:, n % 4, i:i + 1])
                ins.then_inc(probs.sem, 1)

            def attention(part, steps, rnd=0, filler=None, between={}):
                exp_step(part, steps[0], rnd)
                for n, step in enumerate(steps):
                    if n + 1 < len(steps):
                        exp_step(part, steps[n + 1], rnd)
                    if filler and step in FILLERS:
                        filler(FILLERS[step])
                    kb = keys_of(step) // P
                    act.wait_ge(PT.full, PT.nth(part, step_tag(step), rnd))
                    act.activation(probs_t[:, :, 0:kb, :], PT.ap[:, :].rearrange("p (i b n) -> p i b n", i=4, b=2)[:, :, 0:kb, :], ACT.Copy)\
                        .then_inc(PT.free, 1)
                    if n in between:
                        between[n]()

            make_high("xbc0", 0, part="first")
            for r in range(4):
                b = (X, O)[r % 2]
                act.wait_ge(b.full, b.nth("first", f"h{r}"))
                for dst in (h_t, first_high):
                    ins = act.activation(dst[:, 2 * r:2 * r + 2, :], b.ap[:, :].rearrange("p (k n) -> p k n", n=SEQ), ACT.Copy)
                ins.then_inc(b.free, 1)
            make_high("xbc1", 0, (rows.sem, rows.at("first", "h_right")), part="first")

            def conv_gate(c):
                act.wait_ge(conv_done, c + 1)
                act.activation(conv_tanh[:, 4 * c:4 * c + 4, :], conv[:, 4 * c:4 * c + 4, :], ACT.Tanh).then_inc(conv_tanhed, 1)

            act.wait_ge(sp_abs, 1)
            act.activation(a_log_b[:, :], a_log_b[:, :], ACT.Exp)
            act.activation(sp[:, 1], sp[:, 1], ACT.Exp, scale=-1.0).then_inc(sp_exp, 1)
            act.wait_ge(sp_one, 1)
            act.activation(sp[:, 3], sp[:, 2], ACT.Ln).then_inc(sp_ln, 1)

            def take_first(name, *how):
                take("first", name, *how)
                if FIRST_SPLIT.index(name) + 2 < len(FIRST_SPLIT):
                    make_high(FIRST_SPLIT[FIRST_SPLIT.index(name) + 2], 0, part="first")

            for i in range(4):
                take_first(f"xbc{i}", lambda j, i=i: xbc_pad[:, 4 * i + 2 * j:4 * i + 2 * j + 2, CONV_K - 1:])
                if i:
                    conv_gate(i - 1)
            take_first("q", lambda j: q_t[:, 2 * j:2 * j + 2, :])
            take_first("k", lambda j: k_t[:, 2 * j:2 * j + 2, :])
            conv_gate(3)
            take_first("v", lambda j: v_rows[:, j, :])
            for i in range(2):
                for tb, b in enumerate(G):
                    act.wait_ge(b.full, b.nth("first", f"z{i}"))
                    act.activation(z_silu[:, tb, i * HALF:(i + 1) * HALF], b.ap[:, :], ACT.Tanh, scale=0.5).then_inc(z_tanhed, 1)
                make_high(f"ga{i}", 0, part="first")
            for i in range(2):
                take("first", f"ga{i}", lambda tb, i=i: gate_att[:, tb, i * HALF:(i + 1) * HALF], ACT.Tanh, 0.5)
            act.wait_ge(angle_ready, 1)
            act.activation(angle[:, 0:2], angle[:, 0:2], ACT.Sin).then_inc(sines_ready, 1)

            def take_gate_half(name, tb):
                b, i = G[tb], int(name[2:])
                act.wait_ge(b.full, b.nth("first", name))
                act.activation(gate_ssd[:, tb, i * HALF:(i + 1) * HALF], b.ap[:, :], ACT.Tanh, scale=0.5).then_inc(b.free, 1)

            attention("first", FOX_STEPS, filler=lambda half: take_gate_half(*half))
            copy_turned("first", "fox", 2, lambda r: fox_ot[:, 2 * r:2 * r + 2, :])
            act.wait_ge(X.free, X.nth("first", "sums"))
            act.activation(dt_a[:, 3], dt_a[:, 2], ACT.Exp)
            act.activation(dt_a[:, 4], dt_a[:, 4], ACT.Exp).then_inc(sums_exp, 1)
            act.wait_ge(O.full, O.nth("first", "b_rows"))
            act.activation(b_rows[:, :, :], O.ap[:, :].rearrange("p (g n) -> p g n", n=SSD_N), ACT.Copy).then_inc(O.free, 1)
            for i in range(TB * SSD_GROUPS):
                act.wait_ge(seg_cut, i + 1)
                act.activation(decay[:, i], decay[:, i], ACT.Exp).then_inc(seg_exp, 1)
            take_gate_half("gs1", 0)
            act.wait_ge(S.full, S.nth("first", "states"))
            act.activation(states[:, :, :], S.ap[:, :].rearrange("p (g n) -> p g n", n=SSD_R * SSD_P), ACT.Copy).then_inc(S.free, 1)
            take_gate_half("gs1", 1)
            act.wait_ge(gy_ready, 1)
            square_rows("first", "gy", lambda tb: ssd_y[:, tb, :], lambda tb: z_silu[:, tb, :])
            copy_turned("first", "mg", 4, lambda r: h_t[:, 2 * r:2 * r + 2, :])
            for i, name in enumerate(["ln1_g", "ln1_b", "ln2_g", "ln2_b"]):
                act.dma_start(ln_rows[:, i, :], t[name].broadcast_to([P, D])).then_inc(in_ln, 16)
            for i in (6, 7):
                b = mod_bank(i)
                act.wait_ge(b.full, b.nth("first", MOD_CHUNKS[i]))
                act.activation(mod_cols(i), b.ap[:, :], ACT.Copy).then_inc(b.free, 1)
            copy_turned("first", "h2", 4, lambda r: h_t[:, 2 * r:2 * r + 2, :])
            act.wait_ge(route_in, 1)
            act.activation(rt_s[:, 1], rt_s[:, 0], ACT.Exp).then_inc(route_out, 1)
            act.wait_ge(route_in, 2)
            act.activation(rt_s[:, 12, :, 1:2], rt_s[:, 12, :, 0:1], ACT.Exp).then_inc(route_out, 1)

            def take_tokens(at_q):
                for j, b in enumerate((MO, MX)):
                    act.wait_ge(b.full, at_q)
                    act.activation(taken_t[:, 4 * j:4 * j + 4, :], b.ap[:, :].rearrange("p (k n) -> p k n", n=P), ACT.Copy).then_inc(b.free, 1)

            act.wait_ge(rounds_ready, 1)
            n_pairs = act.value_load(rounds_i[0:1, 1:2], min_val=PAIRS, max_val=PAIRS * ROUNDS)
            take_tokens(MO.nth("start", "taken"))
            with act.Fori(0, n_pairs) as q:
                act.wait_ge(M0.full, M0.nth("moe", "gate", q))
                act.activation(expert_t[:, 0, :], M0.ap[:, :], ACT.Tanh, scale=0.5).then_inc(expert_tanhed, 1)
                act.wait_ge(M1.full, M1.nth("moe", "turned", q))
                act.activation(pick_t[:, 0, :], M1.ap[:, 0:SEQ], ACT.Copy).then_inc(M1.free, 1)
                take_tokens(MO.nth("moe", "taken", q))
                for half, b in enumerate((MO, MX)):
                    act.wait_ge(b.full, b.nth("moe", "out", q))
                    act.activation(pair_y[:, 0, half * HALF:(half + 1) * HALF], b.ap[:, :], ACT.Copy).then_inc(b.free, 1)

            with act.Fori(0, LAYERS) as l:
                for lo, name, n in ((G_MIX, "norm_mix_2", KD), (G_XATTN, "norm_xattn_2", KD), (G_MEM, "norm_mem_2", KD), (G_FFN, "norm_ffn_2", KD),
                                    (G_QN, "mla_q_norm_2", 3), (G_KVN, "mla_kv_norm_2", 2)):
                    act.dma_start(stage[lo:lo + n, :], t[name][l].rearrange("(t p) -> t p", p=P)).then_inc(in_layer, 16)
                for lo, name in ((G_PEK, "nsa_pe_k_2"), (G_PEV, "nsa_pe_v_2")):
                    act.dma_start(stage[lo:lo + 16, :], t[name][l].rearrange("(j a) d -> j (a d)", a=2)).then_inc(in_layer, 16)
                act.dma_start(sink_neg[:, :], t["swa_sinks_2"][l].rearrange("(a n) -> a n", a=1).broadcast_to([P, HEADS])).then_inc(in_layer, 16)
                act.dma_start(w2[:, 0, :], t["nsa_wk2_2"][l]).then_inc(in_layer, 16)
                act.dma_start(w2[:, 1, :], t["nsa_wv2_2"][l]).then_inc(in_layer, 16)
                def done(tag):
                    b = banks_of("layer", tag)[1]
                    return b.full, b.nth("layer", tag, l)

                make_high("in1", l, (last_used, l + 1))
                act.wait_ge(x_ready.sem, x_ready.start["layer"] + l)
                square_rows("layer", "mix", lambda tb: x_rows[:, tb, :], lambda tb: h_rows[:, tb, :], l)
                make_high("in0", l)
                act.wait_ge(g_col_ready, l + 1)
                turned_high("mix", KD, mix_high, l, g_col[:, G_MIX:])
                for at_i, i in enumerate(IN_ORDER):
                    take("layer", f"in{i}", lambda tb, a=IN_AT[i], b=IN_AT[i + 1]: proj[:, tb, a:b], rnd=l)
                    if at_i < 4:
                        make_high(f"in{IN_ORDER[at_i + 2]}", l, done(f"in{i}"))
                for b in G:
                    act.wait_ge(b.free, b.nth("layer", "in5", l))
                square_rows("layer", "qn", lambda tb: proj[:, tb, C_QA:C_KV], lambda tb: lat[:, tb, 0:MLA_Q], l)
                act.wait_ge(var_ready.sem, var_ready.at("layer", "qn", l))
                square_rows("layer", "kvn", lambda tb: proj[:, tb, C_KV:C_KR], lambda tb: lat[:, tb, MLA_Q:], l)
                act.activation(branch_g[:, :, :], proj[:, :, C_BG:C_QA], ACT.Tanh, scale=0.5).then_inc(bg_tanhed, 1)

                def take_gate(name):
                    i = int(name[1:])
                    take("layer", name, lambda tb: gate_t[:, tb, i * HALF:(i + 1) * HALF], ACT.Tanh, 0.5, l)

                take_gate("g0")
                take("layer", "qb0", lambda tb: mla_q[:, tb, 0:HALF], rnd=l)
                take("layer", "qb1", lambda tb: mla_q[:, tb, HALF:], rnd=l)
                take("layer", "kvb0", lambda tb: kv_rows[:, tb, 0:HALF], rnd=l)
                take("layer", "kvb1", lambda tb: kv_rows[:, tb, HALF:], rnd=l)

                copy_turned("layer", "nsc", 2, lambda r: kc_t[:, r, :, 0:SEQ], l)
                copy_turned("layer", "swa", 3, lambda r: qt[:, 2 * r:2 * r + 2, :] if r < 2 else kt[:, 0:1, :], l)
                attention("layer", SWA_STEPS, l, take_gate)
                copy_turned("layer", "nsr", 2, lambda r: qt[:, 2 * r:2 * r + 2, :], l)
                copy_turned("layer", "nsq", 3, lambda r: qt[:, 4 + 2 * r:6 + 2 * r, :] if r < 2 else kt[:, 0:2, :], l)
                take_gate("g2")
                act.wait_ge(X.full, X.nth("layer", "cmph", l))
                act.activation(cmp_h[:, 0:2].rearrange("p v g n -> p (v g n)"), X.ap[0:HD, 0:4 * CMP], ACT.Tanh, scale=0.5).then_inc(cmp_tanhed, 1)
                take_gate("g3")
                for qb in range(TB):
                    tag = f"cmp0{qb}"
                    n = masked.parts["layer"].index(tag)
                    act.wait_ge(masked.sem, masked.at("layer", tag, l))
                    act.activation(scores[:, n % 2, 0, 0:P], scores[:, n % 2, 0, 0:P], ACT.Exp, scale=-1.0).then_inc(cmp_exp, 1)
                take_gate("g4")
                for qb in range(TB):
                    act.wait_ge(PT.full, PT.nth("layer", f"cmp0{qb}", l))
                    act.activation(probs_t[:, 0, 0, :], PT.ap[:, 0:P], ACT.Copy).then_inc(PT.free, 1)
                attention("layer", SEL_STEPS + WIN_STEPS, l, take_gate)
                copy_turned("layer", "mq", 4, lambda r: qt[0:MLA_QK, 2 * r:2 * r + 2, :], l, MLA_QK)
                copy_turned("layer", "mk", 4, lambda r: kt[0:MLA_QK, 2 * r:2 * r + 2, :], l, MLA_QK)

                attention("layer", MLA_STEPS, l, between={0: lambda: make_high("bra", l), 2: lambda: make_high("brb", l)})
                act.wait_ge(O.full, O.nth("layer", step_tag(MLA_STEPS[-1]), l))
                act.dma_start(mem_rows[:, :, :], t["mem_2"][0].rearrange("(b p) n -> p b n", p=P)).then_inc(in_mem, 16)
                for name in "abc":
                    turned_high(f"o{name}", KF, o_high[name], l)
                make_high("brc", l, done("bra1"))
                act.wait_ge(in_mem, 16 + l * 16)
                square_rows("layer", "mem", lambda tb: mem_rows[:, tb, :], lambda tb: mem_t[:, :, :].rearrange("p k n -> p (k n)")[:, tb * D:(tb + 1) * D], l)
                turned_high("mem", KD, mem_high, l, g_col[:, G_MEM:])
                make_high("memk", l, done("brb1"))
                make_high("out0", l, done("brc1"))
                take("layer", "memk", lambda j: kt[:, 2 * j:2 * j + 2, :], rnd=l)
                turned_high("mg", KD, mg_high, l)
                make_high("out1", l, done("memk"))
                make_high("memv", l, done("out0"))
                for b in banks_of("layer", "out1"):
                    act.wait_ge(b.free, b.nth("layer", "out1", l))
                square_rows("layer", "xattn", lambda tb: x_rows[:, tb, :], lambda tb: h_rows[:, tb, :], l)
                make_high("xq", l, done("out1"))
                take("layer", "memv", lambda tb: mem_v[:, tb, :], rnd=l)
                turned_high("hx", KD, hx_high, l, g_col[:, G_XATTN:])
                make_high("xo", l, done("memv"))
                take("layer", "xq", lambda j: qt[:, 2 * j:2 * j + 2, :], rnd=l)
                attention("layer", X_STEPS, l)
                make_high("gu0", l, done("xq"))
                turned_high("ox", KF, o_high["x"], l)
                for b in banks_of("layer", "xo1"):
                    act.wait_ge(b.free, b.nth("layer", "xo1", l))
                square_rows("layer", "ffn", lambda tb: x_rows[:, tb, :], lambda tb: h_rows[:, tb, :], l)
                make_high("gu1", l, done("xo1"))
                turned_high("hf", KD, hf_high, l, g_col[:, G_FFN:])

                def hidden_high(c):
                    act.wait_ge(G1.free, G1.nth("layer", f"gu{c}", l))
                    act.activation(ff_high[:, 2 * c:2 * c + 2, :], ff_t[:, 2 * c:2 * c + 2, :], ACT.Copy).then_inc(ff_high_ready, 1)

                for c in range(KFF // 2):
                    act.wait_ge(G0.full, G0.nth("layer", f"gu{c}", l))
                    act.activation(ff_tmp[:, c % 2, :], G0.ap[:, :], ACT.Tanh, scale=0.5).then_inc(gate_tanhed, 1)
                    make_high(SPLIT[SPLIT.index(f"gu{c}") + 2], l, done(f"gu{c}"))
                    if c:
                        hidden_high(c - 1)
                hidden_high(KFF // 2 - 1)
                for c in range(4):
                    make_high(f"fd{c + 2}", l, (ff_used, l * 5 + c + 1))
            act.wait_ge(x_ready.sem, x_ready.total)
            square_rows("last", "out", lambda tb: x_rows[:, tb, :], lambda tb: h_rows[:, tb, :])
            act.dma_start(x_gain[:, :], t["norm_final_2"].rearrange("(a n) -> a n", a=1).broadcast_to([P, D])).then_inc(in_ln, 16)

        @block.vector
        def _(dve):
            st = Steps(dve, dve_steps)

            def over(v, n):
                return v.unsqueeze(2).broadcast_to([v.shape[0], v.shape[1], n])

            def across(v, n):
                return v.unsqueeze(1).broadcast_to([v.shape[0], n, v.shape[1]])

            def gain_turned(part, tag, tiles, dst, gains, rnd=0):
                for r in range((tiles + 1) // 2):
                    b, n = (X, O)[r % 2], min(2, tiles - 2 * r)
                    dve.wait_ge(b.full, b.nth(part, f"{tag}{r}", rnd))
                    dve.tensor_tensor(dst[:, 2 * r:2 * r + n, :], b.ap[:, 0:n * SEQ].rearrange("p (k n) -> p k n", n=SEQ),
                                      over(gains[:, 2 * r:2 * r + n], SEQ), ALU.mult).then_inc(b.free, 1)

            def turned_low(tag, tiles, dst, high, rnd, gains=None, whole=None):
                for k in range(tiles):
                    b, i = (X, O)[k // 2 % 2], k % 2
                    if i == 0:
                        dve.wait_ge(x_high.sem, x_high.at("layer", f"{tag}{k // 2}", rnd))
                        if whole is not None:
                            dve.tensor_tensor(whole[:, k:k + 2, :], b.ap[:, :].rearrange("p (k n) -> p k n", n=SEQ), over(gains[:, k:k + 2], SEQ), ALU.mult)
                    if gains is not None:
                        ins = dve.scalar_tensor_tensor(dst[:, k, :], b.ap[:, i * SEQ:(i + 1) * SEQ], gains[:, k:k + 1],
                                                       high[:, k, :].bitcast(F32), ALU.mult, ALU.subtract)
                    elif i == 1:
                        ins = dve.tensor_tensor(dst[:, k - 1:k + 1, :], b.ap[:, :].rearrange("p (k n) -> p k n", n=SEQ),
                                                high[:, k - 1:k + 1, :].bitcast(F32), ALU.subtract)
                    if i == 1:
                        ins.then_inc(b.free, 1)

            def make_low(name, part="layer", rnd=0):
                n, slot = chunk_size(name), PLACE[part, name][0]
                dve.wait_ge(high_ready.sem, high_ready.at(part, name, rnd))
                dve.tensor_tensor(ring_r[:, slot, 0:n], ring[:, slot, 0:n], high_w[name][:, 0:n].bitcast(F32), ALU.subtract).then_inc(low_ready.sem, 1)

            def rms_rows(part, name, n, eps, src, dst, rnd=0):
                dve.wait_ge(squares.sem, squares.at(part, name, rnd))
                dve.tensor_scalar(var_in[:, :], square_sum[:, :], 1.0 / n, eps, ALU.mult, ALU.add).then_inc(var_ready.sem, 1)
                dve.wait_ge(rstd_ready.sem, rstd_ready.at(part, name, rnd))
                for tb in range(TB):
                    ins = dve.tensor_scalar(dst(tb), src(tb), rstd[:, tb:tb + 1], None, ALU.mult)
                return ins

            def layer_norm(part, name, src, dst):
                for tb in range(TB):
                    for half in range(2):
                        st.done(dve.bn_stats(bn[:, tb, half, :], src[:, tb, half * HALF:(half + 1) * HALF]))
                st.settle()
                for tb in range(TB):
                    st.done(dve.bn_aggr(mean_var[:, tb, :], bn[:, tb, :, :].rearrange("p a b -> p (a b)")))
                st.settle()
                dve.tensor_scalar(var_in[:, :], mean_var[:, :, 1], LN_EPS, None, ALU.add).then_inc(var_ready.sem, 1)

            def layer_norm_end(part, name, src, dst):
                dve.wait_ge(rstd_ready.sem, rstd_ready.at(part, name))
                for tb in range(TB):
                    st.done(dve.tensor_scalar(dst[:, tb, :], src[:, tb, :], mean_var[:, tb, 0:1], rstd[:, tb:tb + 1], ALU.subtract, ALU.mult))
                st.settle()

            def scale_shift(v, scale, shift):
                st.done(dve.tensor_tensor(v, v, across(scale, TB), ALU.mult))
                st.settle()
                return dve.tensor_tensor(v, v, across(shift, TB), ALU.add)

            def mask_step(part, step, rnd=0):
                kind, pp, qb = step
                tag, nk = step_tag(step), keys_of(step)
                n = masked.parts[part].index(tag)
                scale = {"mla": MLA_QK, "x": XD}.get(kind, HD) ** -0.5
                s4 = S.ap[:, :].rearrange("p (i n) -> p i n", n=SEQ)[:, :, 0:nk]
                dst = scores[:, n % 2, :, 0:nk]
                low = neg_max[:, n % 2, 0:4]
                dve.wait_ge(S.full, S.nth(part, tag, rnd))
                if kind == "x":
                    ins = dve.tensor_scalar(dst, s4, -scale, None, ALU.mult)
                else:
                    m = causal[:, P:SEQ] if qb == 0 else windowed[:, :] if kind == "swa" else causal[:, :]
                    ins = dve.scalar_tensor_tensor(dst, s4, -scale, across(m, 4), ALU.mult, ALU.add)
                ins.then_inc(S.free, 1)
                dve.wait_ge(S.free, S.nth(part, tag, rnd))
                ins = dve.tensor_reduce(low, dst, AX_X, ALU.min)
                if kind == "swa":
                    st.done(ins)
                    st.settle()
                    sink = sink_neg[:, :].rearrange("p (f a r) -> p f a r", f=2, a=2)[:, :, pp, :]
                    low4 = low.rearrange("p (f r) -> p f r", f=2)
                    st.done(dve.tensor_tensor(low4, low4, sink, ALU.min))
                    st.settle()
                    ins = dve.tensor_tensor(sink_e[:, n % 4, 0:4].rearrange("p (f r) -> p f r", f=2), low4, sink, ALU.subtract)
                ins.then_inc(masked.sem, 1)

            def finish_step(part, step, dst, rnd=0, gate=None, width=HD):
                tag = step_tag(step)
                n = masked.parts[part].index(tag)
                total, inv = den[:, n % 4, 0:4], rden[:, n % 2, 0:4]
                dve.wait_ge(probs.sem, probs.at(part, tag, rnd))
                if step[0] == "swa":
                    st.done(dve.tensor_tensor(total, total, sink_e[:, n % 4, 4:8], ALU.add))
                    st.settle()
                st.done(dve.reciprocal(inv, total))
                st.settle()
                if gate is not None:
                    inv4 = inv.rearrange("p (f r) -> p f r", f=2)
                    st.done(dve.tensor_tensor(inv4, inv4, gate, ALU.mult))
                    st.settle()
                dve.wait_ge(O.full, O.nth(part, tag, rnd))
                o4 = O.ap[:, 0:4 * width].rearrange("p (i d) -> p i d", d=width)
                if gate is None:
                    if len(dst.shape) == 4:
                        o4 = o4.rearrange("p (f r) d -> p f r d", f=2)
                        w = over(inv, width).rearrange("p (f r) d -> p f r d", f=2)
                    else:
                        w = over(inv, width)
                    dve.tensor_tensor(dst, o4, w, ALU.mult).then_inc(O.free, 1)
                    return None
                dve.tensor_tensor(o_tmp[:, :, :], o4, over(inv, width), ALU.mult).then_inc(O.free, 1)
                dve.wait_ge(O.free, O.nth(part, tag, rnd))
                return dve.tensor_tensor(dst, dst, o_tmp[:, :, :].rearrange("p (f r) d -> p f r d", f=2), ALU.add)

            def attention(part, steps, dst, rnd=0, gate=None, width=HD, end=None, between={}):
                for step in steps[:2]:
                    mask_step(part, step, rnd)
                for n, step in enumerate(steps):
                    if n + 2 < len(steps):
                        mask_step(part, steps[n + 2], rnd)
                    ins = finish_step(part, step, dst(step), rnd, gate(step) if gate else None, width)
                    if ins is not None:
                        if end and n == len(steps) - 1:
                            ins.then_inc(end, 1)
                        else:
                            st.done(ins)
                            st.settle()
                    if n in between:
                        between[n]()

            def crossed(o):
                return lambda s: o[:, s[2], :].rearrange("p (f a r d) -> p f a r d", f=2, a=2, d=HD)[:, :, s[1], :, :]

            dve.wait_ge(c_tanh, 1)
            st.done(dve.scalar_tensor_tensor(c_act[:, :], c_act[:, :], 1.0, c_col[:, :], ALU.add, ALU.mult))
            st.settle()
            dve.tensor_scalar(c_act[:, :], c_act[:, :], 0.5, None, ALU.mult).then_inc(c_ready, 1)

            def add_modulation(i):
                slot, count, _ = PLACE["first", MOD_CHUNKS[i]]
                w, total = keys(ring[:, slot, :], KD, HALF), mod_cols(i)
                dve.wait_ge(landed[slot], count)
                for k in range(KD):
                    if k == 0:
                        ins = dve.tensor_scalar(total, w[:, k, :], c_act[:, k:k + 1], None, ALU.mult)
                    else:
                        ins = dve.scalar_tensor_tensor(total, w[:, k, :], c_act[:, k:k + 1], total, ALU.mult, ALU.add)
                    if k < KD - 1:
                        st.done(ins)
                        st.settle()
                ins.then_inc(mod_parts, 1)

            def take_modulation(i):
                b = mod_bank(i)
                dve.wait_ge(b.full, b.nth("first", MOD_CHUNKS[i]))
                plus = 0.0 if i // 2 in (0, 3) else 1.0
                dve.tensor_scalar(mod_cols(i), b.ap[:, 0:HALF], plus, None, ALU.add).then_inc(b.free, 1)

            dve.wait_ge(c_ready, 1)
            for i in MOD_SUMMED[:2]:
                add_modulation(i)
            dve.wait_ge(in_x, 16)
            layer_norm("first", "h", x_rows, h_rows)
            layer_norm_end("first", "h", x_rows, h_rows)
            for half, name in enumerate(("h_left", "h_right")):
                cols = slice(half * HALF, (half + 1) * HALF)
                for i in (half, 2 + half):
                    take_modulation(i)
                for i in (half, 2 + half):
                    dve.wait_ge(mod_bank(i).free, mod_bank(i).nth("first", MOD_CHUNKS[i]))
                scale_shift(h_rows[:, :, cols], mod[:, 1, cols], mod[:, 0, cols]).then_inc(rows.sem, 1)

            dve.wait_ge(X.full, X.nth("first", "conv_col"))
            nc_ = CONV_TILES * (CONV_K + 1)
            st.done(dve.tensor_scalar(conv_col[:, 0:nc_], X.ap[:, 0:nc_], 0.5, None, ALU.mult))
            dve.tensor_copy(conv_col[:, nc_:], X.ap[:, nc_:nc_ + KD]).then_inc(X.free, 1)

            make_low("xbc0", "first")
            for b, r in ((X, 2), (O, 3)):
                dve.wait_ge(b.free, b.nth("first", f"h{r}"))
            dve.tensor_tensor(first_low[:, :, :], h_t[:, :, :], first_high[:, :, :].bitcast(F32), ALU.subtract).then_inc(first_low_ready, 1)

            dve.wait_ge(in_vec, 16 * 7)
            for tb, b in enumerate(G):
                dve.wait_ge(b.full, b.nth("first", "dtf"))
                dve.tensor_tensor(sp[:, 0, tb, :], b.ap[:, 0:24], bias24[:, :], ALU.add).then_inc(b.free, 1)
            for b in G:
                dve.wait_ge(b.free, b.nth("first", "dtf"))
            st.done(dve.tensor_scalar(sp[:, 0, :, SSD_HEADS:], sp[:, 0, :, SSD_HEADS:], -1.0, None, ALU.mult))
            st.settle()
            dve.scalar_tensor_tensor(sp[:, 1], sp[:, 0], -1.0, sp[:, 0], ALU.mult, ALU.max).then_inc(sp_abs, 1)
            dve.wait_ge(sp_exp, 1)
            dve.tensor_scalar(sp[:, 2], sp[:, 1], 1.0, None, ALU.add).then_inc(sp_one, 1)
            dve.wait_ge(sp_one, 1)
            st.done(dve.tensor_scalar(sp[:, 4], sp[:, 2], -1.0, None, ALU.add))
            st.settle()
            st.done(dve.tensor_scalar(sp[:, 5], sp[:, 4], 0.0, None, ALU.is_equal))
            st.settle()
            st.done(dve.tensor_tensor(sp[:, 4], sp[:, 4], sp[:, 5], ALU.add))
            st.settle()
            st.done(dve.reciprocal(sp[:, 4], sp[:, 4]))
            st.done(dve.tensor_tensor(sp[:, 5], sp[:, 5], sp[:, 1], ALU.mult))
            st.settle()
            st.done(dve.tensor_tensor(sp[:, 4], sp[:, 4], sp[:, 1], ALU.mult))
            st.settle()
            dve.wait_ge(sp_ln, 1)
            st.done(dve.tensor_tensor(sp[:, 3], sp[:, 3], sp[:, 4], ALU.mult))
            st.settle()
            st.done(dve.tensor_tensor(sp[:, 3], sp[:, 3], sp[:, 5], ALU.add))
            st.settle()
            st.done(dve.scalar_tensor_tensor(sp[:, 5], sp[:, 0], 0.0, sp[:, 3], ALU.max, ALU.add))
            st.settle()
            st.done(dve.tensor_copy(dt_a[:, 0], sp[:, 5, :, 0:SSD_HEADS]))
            st.done(dve.tensor_scalar(sp[:, 5, :, SSD_HEADS:], sp[:, 5, :, SSD_HEADS:], HD ** 0.5, None, ALU.mult))
            st.settle()
            dve.scalar_tensor_tensor(dt_a[:, 1], dt_a[:, 0], -1.0, across(a_log_b[:, :], TB), ALU.mult, ALU.mult).then_inc(forget_ready, 1)

            make_low("xbc1", "first")

            def convolve(c):
                for b in G:
                    dve.wait_ge(b.free, b.nth("first", f"xbc{c}"))
                for j in range(CONV_K):
                    for tile in range(4 * c, 4 * c + 4):
                        tap = xbc_pad[:, tile, j:j + SEQ]
                        w = conv_col[:, j * CONV_TILES + tile:j * CONV_TILES + tile + 1]
                        if j == 0:
                            bias = conv_col[:, CONV_K * CONV_TILES + tile:CONV_K * CONV_TILES + tile + 1]
                            ins = dve.tensor_scalar(conv[:, tile, :], tap, w, bias, ALU.mult, ALU.add)
                        else:
                            ins = dve.scalar_tensor_tensor(conv[:, tile, :], tap, w, conv[:, tile, :], ALU.mult, ALU.add)
                        if j < CONV_K - 1 or tile < 4 * c + 3:
                            st.done(ins)
                    if j < CONV_K - 1:
                        st.settle()
                ins.then_inc(conv_done, 1)

            def conv_gate(c):
                dve.wait_ge(conv_tanhed, c + 1)
                u = conv[:, 4 * c:4 * c + 4, :]
                dve.scalar_tensor_tensor(u, conv_tanh[:, 4 * c:4 * c + 4, :], 1.0, u, ALU.add, ALU.mult).then_inc(conv_ready, 1)

            make_low("xbc2", "first")
            convolve(0)
            make_low("xbc3", "first")
            convolve(1)
            make_low("q", "first")
            convolve(2)
            make_low("k", "first")
            make_low("v", "first")
            convolve(3)
            make_low("z0", "first")
            conv_gate(0)
            conv_gate(1)
            make_low("z1", "first")
            conv_gate(2)
            conv_gate(3)
            for i in range(2):
                for tb, b in enumerate(G):
                    z = z_silu[:, tb, i * HALF:(i + 1) * HALF]
                    dve.wait_ge(z_tanhed, 2 * i + tb + 1)
                    dve.scalar_tensor_tensor(z, z, 1.0, b.ap[:, :], ALU.add, ALU.mult).then_inc(b.free, 1)
                make_low(f"ga{i}", "first")
            dve.wait_ge(consts, 1)
            st.done(dve.tensor_copy(pos_f[:, :], pos_i[:, :]))
            st.settle()
            for tb in range(TB):
                st.done(dve.tensor_scalar(angle[:, 2, tb, :], inv_freq[:, :], pos_f[:, tb:tb + 1], None, ALU.mult))
            st.settle()
            for f, (shift, add) in enumerate(((0.0, 0.0), (0.25, float(np.pi / 2)))):
                turns, ang, r = angle[:, 3], angle[:, 2], angle[:, f]
                st.done(dve.tensor_scalar(turns, ang, float(1 / (2 * np.pi)), shift, ALU.mult, ALU.add))
                st.settle()
                st.done(dve.tensor_scalar(turns, turns, ROUND, None, ALU.add))
                st.settle()
                st.done(dve.tensor_scalar(turns, turns, -ROUND, None, ALU.add))
                st.settle()
                for j, part in enumerate(TURN):
                    st.done(dve.scalar_tensor_tensor(r, turns, -part, ang if j == 0 else r, ALU.mult, ALU.add))
                    st.settle()
                st.done(dve.tensor_scalar(r, r, add, None, ALU.add))
                st.settle()
                ins = dve.tensor_scalar(r, r, -PI_IN, PI_IN, ALU.max, ALU.min)
                if f == 0:
                    st.done(ins)
                else:
                    ins.then_inc(angle_ready, 1)
            add_modulation(8)
            take_modulation(8)
            dve.wait_ge(sines_ready, 1)
            hh = HD // 2
            st.done(dve.tensor_copy(rope_c[:, :, 0:hh], angle[:, 1]))
            st.done(dve.tensor_copy(rope_c[:, :, hh:], angle[:, 1]))
            st.done(dve.tensor_scalar(rope_s[:, :, 0:hh], angle[:, 0], -1.0, None, ALU.mult))
            st.done(dve.tensor_copy(rope_s[:, :, hh:], angle[:, 0]))


            attention("first", FOX_STEPS, lambda s: fox_o[:, s[2], s[1] * SEQ:(s[1] + 1) * SEQ].rearrange("p (r f d) -> p f r d", f=2, d=HD))
            add_modulation(9)
            for half in range(2):
                for tb, b in enumerate(G):
                    d = gate_att[:, tb, half * HALF:(half + 1) * HALF]
                    dve.wait_ge(b.full, b.nth("first", f"att{half}"))
                    dve.scalar_tensor_tensor(d, d, 1.0, b.ap[:, :], ALU.add, ALU.mult).then_inc(b.free, 1)

            dve.wait_ge(X.full, X.nth("first", "sums"))
            st.done(dve.tensor_copy(dt_a[:, 2], X.ap[:, 0:32].rearrange("p (t h) -> p t h", t=TB)))
            st.settle()
            dve.tensor_tensor(dt_a[:, 4], X.ap[:, 32:64].rearrange("p (t h) -> p t h", t=TB), dt_a[:, 2], ALU.subtract).then_inc(X.free, 1)
            for r in range(4):
                tb, half = divmod(r, 2)
                b = (X, O)[r % 2]
                hs = slice(8 * half, 8 * half + 8)
                src = b.ap[:, :].rearrange("p (h d) -> p h d", d=SSD_P)
                dve.wait_ge(b.full, b.nth("first", f"xs{r}"))
                st.done(dve.tensor_copy(xs[:, tb, hs, :], src))
                dve.tensor_tensor(xdt[:, tb, hs, :], src, over(dt_a[:, 0, tb, hs], SSD_P), ALU.mult).then_inc(b.free, 1)
            dve.wait_ge(sums_exp, 1)
            for b, r in ((X, 2), (O, 3)):
                dve.wait_ge(b.free, b.nth("first", f"xs{r}"))
            dve.tensor_tensor(x_end[:, :, :], xdt[:, 0], over(dt_a[:, 4, 0, :], SSD_P), ALU.mult).then_inc(xdt_ready, 1)
            dve.wait_ge(S.full, S.nth("first", "cb"))
            dve.tensor_copy(cb[:, :, :], S.ap[:, :].rearrange("p (c n) -> p c n", n=P)).then_inc(S.free, 1)
            for i in range(TB * SSD_GROUPS):
                c, g = divmod(i, SSD_GROUPS)
                b = G[g % 2]
                dve.wait_ge(b.full, b.nth("first", f"seg{c}{g}"))
                dve.tensor_tensor(decay[:, i], b.ap[:, :].rearrange("p (r n) -> p r n", n=P),
                                  over(dt_a[:, 2, c, g * SSD_R:(g + 1) * SSD_R], P), ALU.subtract).then_inc(b.free, 1)
            for tb in range(TB):
                st.done(dve.tensor_tensor(ssd_y[:, tb, :].rearrange("p (h d) -> p h d", d=SSD_P), xs[:, tb], over(d_skip_b[:, :], SSD_P), ALU.mult))
            dve.wait_ge(S.free, S.nth("first", "cb"))
            for i in range(TB * SSD_GROUPS):
                dve.wait_ge(seg_exp, i + 1)
                dve.tensor_tensor(decay[:, i], decay[:, i], across(cb[:, i, :], SSD_R), ALU.mult).then_inc(decay_ready, 1)
            st.settle()
            take_modulation(9)
            for c in range(TB):
                dve.wait_ge(PT.full, PT.nth("first", f"yd{c}"))
                dve.tensor_tensor(ssd_y[:, c, :], PT.ap[:, :], ssd_y[:, c, :], ALU.add).then_inc(PT.free, 1)
            dve.wait_ge(S.full, S.nth("first", "yo"))
            dve.tensor_tensor(xs[:, 0], S.ap[:, :].rearrange("p (h d) -> p h d", d=SSD_P), over(dt_a[:, 3, 1, :], SSD_P), ALU.mult).then_inc(S.free, 1)
            dve.wait_ge(S.free, S.nth("first", "yo"))
            dve.wait_ge(PT.free, PT.nth("first", "yd1"))
            st.done(dve.tensor_tensor(ssd_y[:, 1, :], ssd_y[:, 1, :], xs[:, 0].rearrange("p h d -> p (h d)"), ALU.add))
            st.settle()
            dve.scalar_tensor_tensor(ssd_y[:, :, :], ssd_y[:, :, :], 0.5, z_silu[:, :, :], ALU.mult, ALU.mult).then_inc(gy_ready, 1)
            rms_rows("first", "gy", D, LN_EPS, lambda tb: ssd_y[:, tb, :], lambda tb: ssd_y[:, tb, :]).then_inc(rows.sem, 1)
            take_modulation(4)
            gain_turned("first", "gy", KD, y_turned, conv_col[:, nc_:])
            add_modulation(10)
            for i in range(2):
                for tb, b in enumerate(G):
                    cols = slice(i * HALF, (i + 1) * HALF)
                    dve.wait_ge(b.full, b.nth("first", f"so{i}"))
                    dve.scalar_tensor_tensor(gate_ssd[:, tb, cols], gate_ssd[:, tb, cols], 1.0, b.ap[:, :], ALU.add, ALU.mult).then_inc(b.free, 1)
            for b in G:
                dve.wait_ge(b.free, b.nth("first", "so1"))
            dve.tensor_tensor(gate_att[:, :, :], gate_att[:, :, :], gate_ssd[:, :, :], ALU.add).then_inc(rows.sem, 1)

            take_modulation(10)
            take_modulation(5)
            add_modulation(11)

            def residual_norm(part, name, gain, shift):
                st.done(dve.scalar_tensor_tensor(resid[:, :, :], x_rows[:, :, :], ALPHA, resid[:, :, :], ALU.mult, ALU.add))
                st.settle()
                layer_norm(part, name, resid, x_rows)
                layer_norm_end(part, name, resid, x_rows)
                return scale_shift(x_rows[:, :, :], gain, shift)

            for i in range(2):
                for tb, b in enumerate(G):
                    cols = slice(i * HALF, (i + 1) * HALF)
                    dve.wait_ge(b.full, b.nth("first", f"o{i}"))
                    dve.scalar_tensor_tensor(resid[:, tb, cols], b.ap[:, :], 0.5, mod[:, 2, cols], ALU.mult, ALU.mult).then_inc(b.free, 1)
            for b in G:
                dve.wait_ge(b.free, b.nth("first", "o1"))
            for b in EXPERT_BANKS:
                dve.sem_inc(b.full, b.given)
                dve.sem_inc(b.free, b.given)
            dve.sem_inc(expert_used, 4)
            dve.wait_ge(in_ln, 16 * 4)
            st.done(residual_norm("first", "ln1", ln_rows[:, 0, :], ln_rows[:, 1, :]))
            st.settle()
            layer_norm("first", "h2", x_rows, h_rows)
            layer_norm_end("first", "h2", x_rows, h_rows)
            for i in (6, 7):
                dve.wait_ge(mod_bank(i).free, mod_bank(i).nth("first", MOD_CHUNKS[i]))
            scale_shift(h_rows[:, :, :], mod[:, 4, :], mod[:, 3, :]).then_inc(rows.sem, 1)
            take_modulation(11)

            for tb, b in enumerate(G):
                dve.wait_ge(b.full, b.nth("first", "route"))
                dve.tensor_tensor(rt[:, tb, :], b.ap[:, 0:N_GROUPS + N_EXPERTS], route_b[:, :], ALU.add).then_inc(b.free, 1)
            for b in G:
                dve.wait_ge(b.free, b.nth("first", "route"))

            def small(i):
                return rt_s[:, i]

            def one(i):
                return rt_s[:, i, :, 0]

            def do(ins):
                st.done(ins)
                st.settle()

            def first_best(v, top, hot):
                do(dve.tensor_reduce(one(top), v, AX_X, ALU.max))
                do(dve.tensor_tensor(small(5), v, over(one(top), PER_GROUP), ALU.is_equal))
                do(dve.tensor_tensor(small(5), small(5), across(back[:, :], TB), ALU.mult))
                do(dve.tensor_reduce(one(6), small(5), AX_X, ALU.max))
                do(dve.tensor_tensor(small(hot), small(5), over(one(6), PER_GROUP), ALU.is_equal))

            first_best(rt[:, :, 0:N_GROUPS], 2, 8)
            dve.tensor_tensor(small(0), rt[:, :, 0:N_GROUPS], over(one(2), N_GROUPS), ALU.subtract).then_inc(route_in, 1)
            for tb in range(TB):
                st.done(dve.tensor_tensor(rt_m[:, tb, :].rearrange("p (g e) -> p g e", g=N_GROUPS),
                                          rt[:, tb, N_GROUPS:].rearrange("p (g e) -> p g e", g=N_GROUPS), over(rt_s[:, 8, tb, :], PER_GROUP), ALU.mult))
            st.settle()
            for tb in range(TB):
                st.done(dve.tensor_reduce(rt_s[:, 9, tb, :], rt_m[:, tb, :].rearrange("p (g e) -> p e g", g=N_GROUPS), AX_X, ALU.add))
            st.settle()
            first_best(small(9), 10, 13)
            do(dve.scalar_tensor_tensor(small(14), small(13), -MASKED, small(9), ALU.mult, ALU.add))
            first_best(small(14), 11, 15)
            dve.tensor_tensor(one(12), one(11), one(10), ALU.subtract).then_inc(route_in, 1)
            do(dve.tensor_tensor(small(20), small(13), small(15), ALU.add))
            for tb in range(TB):
                st.done(dve.tensor_tensor(picked[:, tb, :].rearrange("p (g e) -> p g e", g=N_GROUPS), over(rt_s[:, 8, tb, :], PER_GROUP),
                                          across(rt_s[:, 20, tb, :], N_GROUPS), ALU.mult))
            st.settle()
            dve.sem_inc(picked_ready, 1)
            dve.wait_ge(route_out, 2)
            do(dve.tensor_reduce(one(3), small(1), AX_X, ALU.add))
            do(dve.tensor_scalar(one(16), rt_s[:, 12, :, 1], 1.0, None, ALU.add))
            do(dve.tensor_tensor(one(16), one(16), one(3), ALU.mult))
            do(dve.reciprocal(one(16), one(16)))
            do(dve.tensor_scalar(one(16), one(16), 0.5, None, ALU.mult))
            do(dve.tensor_tensor(one(17), one(16), rt_s[:, 12, :, 1], ALU.mult))
            do(dve.tensor_tensor(small(18), small(13), over(one(16), PER_GROUP), ALU.mult))
            do(dve.tensor_tensor(small(19), small(15), over(one(17), PER_GROUP), ALU.mult))
            do(dve.tensor_tensor(small(18), small(18), small(19), ALU.add))
            for tb in range(TB):
                st.done(dve.tensor_tensor(gates[:, tb, :].rearrange("p (g e) -> p g e", g=N_GROUPS), over(rt_s[:, 8, tb, :], PER_GROUP),
                                          across(rt_s[:, 18, tb, :], N_GROUPS), ALU.mult))
            st.done(dve.memset(pick_t[:, 0, :], 0.0))
            st.done(dve.memset(pair_y[:, 0, :], 0.0))
            st.done(dve.memset(place[:, :, PICKS - 2:], 0.0))
            st.done(dve.memset(gate_of[:, :, PICKS - 2:], 0.0))
            st.settle()
            for i in range(ROUNDS):
                st.done(dve.tensor_copy(gate_of[:, :, i * N_EXPERTS:(i + 1) * N_EXPERTS], gates[:, :, :]))
            st.settle()
            dve.sem_inc(sums_cleared, 1)

            dve.wait_ge(X.full, X.nth("first", "places"))
            st.done(dve.tensor_copy(load_of[:, 0, :], X.ap[:, 32:48]))
            st.done(dve.tensor_copy(slot_row[:, 0, :], X.ap[:, 48:48 + SLOT_TOKENS]))
            do(dve.tensor_tensor(place[:, :, 0:N_EXPERTS], X.ap[:, 0:32].rearrange("p (t e) -> p t e", t=TB), picked[:, :, :], ALU.mult))
            dve.sem_inc(X.free, 1)
            for i in range(1, ROUNDS):
                st.done(dve.tensor_scalar(place[:, :, i * N_EXPERTS:(i + 1) * N_EXPERTS], place[:, :, 0:N_EXPERTS],
                                          -float(i * SLOT_TOKENS), None, ALU.add))
            do(dve.tensor_reduce(rounds_f[:, 0:1], load_of[:, 0, :], AX_X, ALU.max))
            do(dve.tensor_scalar(rounds_f[:, 1:2], rounds_f[:, 0:1], float(SLOT_TOKENS) + 0.5, 1.0, ALU.is_ge, ALU.add))
            for i in range(2, ROUNDS):
                do(dve.scalar_tensor_tensor(rounds_f[:, 1:2], rounds_f[:, 0:1], float(i * SLOT_TOKENS) + 0.5, rounds_f[:, 1:2], ALU.is_ge, ALU.add))
            do(dve.tensor_scalar(rounds_f[:, 2:3], rounds_f[:, 1:2], float(PAIRS), None, ALU.mult))
            do(dve.tensor_copy(rounds_i[:, :], rounds_f[0:1, 1:3]))
            dve.sem_inc(rounds_ready, 1)

            def pick_slots(q, dst, gate):
                for j in range(2):
                    for tb in range(TB):
                        c = bass.ds(q * 2 + j, 1)
                        d = dst[:, tb, j * SLOT_TOKENS:(j + 1) * SLOT_TOKENS]
                        if gate:
                            ins = dve.tensor_scalar(d, slot_row[:, 0, :], place[:, tb, c], gate_of[:, tb, c], ALU.is_equal, ALU.mult)
                        else:
                            ins = dve.tensor_scalar(d, slot_row[:, 0, :], place[:, tb, c], None, ALU.is_equal)
                return ins

            n_pairs = dve.value_load(rounds_i[0:1, 1:2], min_val=PAIRS, max_val=PAIRS * ROUNDS)
            pick_slots(0, pick, False).then_inc(pick_ready, 1)
            pick_slots(0, pick_g, True).then_inc(pick_g_ready, 1)
            dve.wait_ge(MX.full, MX.nth("start", "taken"))
            with dve.Fori(0, n_pairs) as q:
                dve.wait_ge(MX.full, q * 2 + 1)
                pick_slots(q + 1, pick, False).then_inc(pick_ready, 1)
                dve.wait_ge(expert_tanhed, q + 1)
                dve.scalar_tensor_tensor(expert_t[:, 1, :], expert_t[:, 0, :], 1.0, M0.ap[:, :], ALU.add, ALU.mult).then_inc(M0.free, 1)
                dve.wait_ge(M0.free, M0.nth("moe", "gate", q))
                dve.wait_ge(M1.full, M1.nth("moe", "up", q))
                dve.tensor_tensor(expert_t[:, 0, :], expert_t[:, 1, :], M1.ap[:, :], ALU.mult).then_inc(M1.free, 1)
                dve.wait_ge(M0.full, M0.nth("moe", "hid", q))
                dve.tensor_copy(hid_t[:, :, :], M0.ap[:, :].rearrange("p (k n) -> p k n", n=P)).then_inc(M0.free, 1)
                dve.wait_ge(M1.full, M1.nth("moe", "turned", q))
                pick_slots(q + 1, pick_g, True).then_inc(pick_g_ready, 1)

            for tb, b in enumerate((S, PT)):
                dve.wait_ge(b.full, b.nth("mid", "sums"))
                dve.tensor_tensor(resid[:, tb, :], b.ap[:, :], mod[:, 5, :], ALU.mult).then_inc(b.free, 1)
            dve.sem_inc(last_used, 1)
            for b in (S, PT):
                dve.wait_ge(b.free, b.nth("mid", "sums"))
            residual_norm("mid", "ln2", ln_rows[:, 2, :], ln_rows[:, 3, :]).then_inc(x_ready.sem, 1)
            dve.wait_ge(x_ready.sem, 1)
            st.end()

            with dve.Fori(0, LAYERS) as l:
                st.begin(l, LAYER_DVE_STEPS)
                dve.wait_ge(in_layer, 16 * 11 + l * (16 * 11))
                st.done(dve.tensor_scalar(sink_neg[:, :], sink_neg[:, :], -1.0, None, ALU.mult))
                for i in range(2):
                    st.done(dve.tensor_scalar(w2_k[:, i, :], w2[:, 0, :], 0.5, None, ALU.mult))
                st.done(dve.tensor_scalar(w2_v[:, :], w2[:, 1, :], 0.5, None, ALU.mult))
                dve.wait_ge(X.full, X.nth("layer", "g_col", l))
                dve.tensor_copy(g_col[:, :], X.ap[:, 0:G_END]).then_inc(X.free, 1)
                rms_rows("layer", "mix", D, RMS_EPS, lambda tb: x_rows[:, tb, :], lambda tb: h_rows[:, tb, :], l).then_inc(rows.sem, 1)
                dve.wait_ge(X.free, X.nth("layer", "g_col", l))
                dve.sem_inc(g_col_ready, 1)
                make_low("in1", rnd=l)
                turned_low("mix", KD, mix_low, mix_high, l, g_col[:, G_MIX:], h_t)
                make_low("in0", rnd=l)
                make_low("in2", rnd=l)
                make_low("in3", rnd=l)

                def rope(pieces, half, cos, sin):
                    at_t, made = 0, []
                    for dst, src, tb in pieces:
                        nh = src.shape[1]
                        tmp = rope_tmp[:, 0, at_t:at_t + nh * 2 * half].rearrange("p (h d) -> p h d", h=nh)
                        at_t += nh * 2 * half
                        st.done(dve.tensor_tensor(tmp[:, :, 0:half], src[:, :, half:], across(sin(tb, 0), nh), ALU.mult))
                        st.done(dve.tensor_tensor(tmp[:, :, half:], src[:, :, 0:half], across(sin(tb, 1), nh), ALU.mult))
                        made.append(tmp)
                    st.settle()
                    for dst, src, tb in pieces:
                        for i in range(2):
                            part = slice(i * half, (i + 1) * half)
                            st.done(dve.tensor_tensor(dst[:, :, part], src[:, :, part], across(cos(tb), src.shape[1]), ALU.mult))
                    st.settle()
                    for (dst, src, tb), tmp in zip(pieces, made):
                        ins = dve.tensor_tensor(dst, dst, tmp, ALU.add)
                    return ins

                cos64, sin64 = (lambda tb: rope_c[:, tb, 0:hh]), (lambda tb, i: rope_s[:, tb, i * hh:(i + 1) * hh])
                by_head = lambda v: v.rearrange("p (h d) -> p h d", d=HD)
                for b in G:
                    dve.wait_ge(b.free, b.nth("layer", "in0", l))
                rope([(by_head(swa_r[:, tb, :]), by_head(proj[:, tb, 0:C_AV]), tb) for tb in range(TB)], hh, cos64, sin64).then_inc(rows.sem, 1)
                make_low("in4", rnd=l)
                make_low("in5", rnd=l)
                for b in G:
                    dve.wait_ge(b.free, b.nth("layer", "in4", l))
                dve.wait_ge(rows.sem, rows.at("layer", "swa", l))
                rope([(by_head(nsa_q[:, tb, :]), by_head(proj[:, tb, C_BQ:C_KC]), tb) for tb in range(TB)]
                     + [(by_head(nsa_k[:, tb, 0:P]), by_head(proj[:, tb, C_KS:C_VS]), tb) for tb in range(TB)]
                     + [(by_head(nsa_k[:, tb, P:]), by_head(proj[:, tb, C_KW:C_VW]), tb) for tb in range(TB)], hh, cos64, sin64).then_inc(rows.sem, 1)

                for tb in range(TB):
                    ins = dve.tensor_copy(kc_twice[:, tb, :].rearrange("p (v a d) -> p v a d", a=2, d=HD),
                                          by_head(proj[:, tb, C_KC:C_KS]).unsqueeze(2).broadcast_to([P, 4, 2, HD]))
                ins.then_inc(rows.sem, 1)

                st.done(rms_rows("layer", "qn", MLA_Q, RMS_EPS, lambda tb: proj[:, tb, C_QA:C_KV], lambda tb: lat[:, tb, 0:MLA_Q], l))
                rms_rows("layer", "kvn", MLA_KV, RMS_EPS, lambda tb: proj[:, tb, C_KV:C_KR], lambda tb: lat[:, tb, MLA_Q:], l).then_inc(rows.sem, 1)
                dve.wait_ge(bg_tanhed, l + 1)
                st.done(dve.tensor_scalar(branch_g[:, :, :], branch_g[:, :, :], 1.0, 0.5, ALU.add, ALU.mult))
                gain_turned("layer", "lat", 5, lat_t, g_col[:, G_QN:G_PEK], l)
                for v in range(2):
                    st.done(dve.memset(kc_t[:, v, :, SEQ:], 0.0))

                for b in G:
                    dve.wait_ge(b.free, b.nth("layer", "kvb1", l))
                dve.wait_ge(rows.sem, rows.at("layer", "nsa", l))
                hr = MLA_ROPE // 2
                cos32, sin32 = (lambda tb: rope_c[:, tb, 0:hh:2]), (lambda tb, i: rope_s[:, tb, i * hh:(i + 1) * hh:2])
                heads96 = lambda v: v.rearrange("p (h d) -> p h d", d=MLA_QK)
                q_pe = lambda tb: heads96(mla_q[:, tb, :])[:, :, HD:]
                k_pe = lambda tb: proj[:, tb, C_KR:C_G].unsqueeze(1)
                st.done(rope([(q_pe(tb), q_pe(tb), tb) for tb in range(TB)] + [(k_pe(tb), k_pe(tb), tb) for tb in range(TB)], hr, cos32, sin32))
                st.settle()
                for tb in range(TB):
                    k = heads96(mla_k[:, tb, :])
                    st.done(dve.tensor_copy(k[:, :, 0:HD], kv_rows[:, tb, :].rearrange("p (h d) -> p h d", d=P)[:, :, 0:HD]))
                    ins = dve.tensor_copy(k[:, :, HD:], across(proj[:, tb, C_KR:C_G], HEADS))
                    if tb == 0:
                        st.done(ins)
                ins.then_inc(rows.sem, 1)

                attention("layer", SWA_STEPS, crossed(o_a), l)

                for b, r in ((X, 0), (O, 1)):
                    dve.wait_ge(b.free, b.nth("layer", f"nsc{r}", l))
                st.settle()
                for v in range(2):
                    for half in range(2):
                        lanes = slice(HD * half, HD * half + HD)
                        for hi in range(2):
                            src = kc_t[lanes, v, :, 16 * hi:16 * hi + SEQ].rearrange("p g (n j a) -> p j g n a", j=8, a=2)[:, :, :, :, half]
                            pos = g_col[lanes, G_PEK + 16 * v + 8 * hi:G_PEK + 16 * v + 8 * hi + 8]
                            ins = dve.tensor_tensor(cmp_blk[lanes, v, 8 * hi:8 * hi + 8, :].rearrange("p j (g n) -> p j g n", g=2), src,
                                                    pos.unsqueeze(2).unsqueeze(3).broadcast_to([HD, 8, 2, CMP]), ALU.add)
                            if (v, half, hi) != (1, 1, 1):
                                st.done(ins)
                ins.then_inc(rows.sem, 1)
                dve.wait_ge(cmp_tanhed, l + 1)
                dve.scalar_tensor_tensor(cmp_h[:, 2:4].rearrange("p v g n -> p (v g n)"), cmp_h[:, 0:2].rearrange("p v g n -> p (v g n)"), 1.0,
                                         X.ap[0:HD, 0:4 * CMP], ALU.add, ALU.mult).then_inc(X.free, 1)
                dve.wait_ge(X.free, X.nth("layer", "cmph", l))
                dve.tensor_copy(cmp_hv[:, :, :, :], cmp_h[:, 3].unsqueeze(2).broadcast_to([HD, 2, HEADS // 2, CMP])).then_inc(rows.sem, 1)
                dve.wait_ge(O.full, O.nth("layer", "cmpkv", l))
                st.done(dve.tensor_copy(cmp_k[:, :], O.ap[:, 0:2 * CMP]))
                dve.tensor_tensor(cmp_v[:, :, :], across(O.ap[:, 64:64 + HD], HEADS), over(head_of[:, :], HD), ALU.mult).then_inc(O.free, 1)

                for qb in range(TB):
                    tag = f"cmp0{qb}"
                    n = masked.parts["layer"].index(tag)
                    s8 = scores[:, n % 2, 0, 0:P].rearrange("p (h n) -> p h n", n=CMP)
                    dve.wait_ge(S.full, S.nth("layer", tag, l))
                    for f in range(2):
                        ins = dve.scalar_tensor_tensor(s8[:, 4 * f:4 * f + 4, :], S.ap[:, f * HALF:f * HALF + 4 * CMP].rearrange("p (h n) -> p h n", n=CMP),
                                                       -HD ** -0.5, across(cmp_mask[:, qb, :], 4), ALU.mult, ALU.add)
                        if f == 0:
                            st.done(ins)
                    ins.then_inc(S.free, 1)
                    st.settle()
                    dve.wait_ge(S.free, S.nth("layer", tag, l))
                    st.done(dve.tensor_reduce(neg_max[:, n % 2, :], s8, AX_X, ALU.min))
                    st.settle()
                    st.done(dve.tensor_scalar(neg_max[:, n % 2, :], neg_max[:, n % 2, :], MASKED / 10, None, ALU.min))
                    st.settle()
                    dve.tensor_tensor(s8, s8, over(neg_max[:, n % 2, :], CMP), ALU.subtract).then_inc(masked.sem, 1)
                for qb in range(TB):
                    n = masked.parts["layer"].index(f"cmp0{qb}")
                    s8 = scores[:, n % 2, 0, 0:P].rearrange("p (h n) -> p h n", n=CMP)
                    dve.wait_ge(cmp_exp, TB * l + qb + 1)
                    st.done(dve.tensor_reduce(den[:, n % 4, :], s8, AX_X, ALU.add))
                    st.settle()
                    st.done(dve.tensor_scalar(den[:, n % 4, :], den[:, n % 4, :], 0.5, None, ALU.max))
                    st.settle()
                    st.done(dve.reciprocal(rden[:, n % 2, :], den[:, n % 4, :]))
                    st.settle()
                    dve.tensor_tensor(s8, s8, over(rden[:, n % 2, :], CMP), ALU.mult).then_inc(probs.sem, 1)
                for qb in range(TB):
                    dve.wait_ge(O.full, O.nth("layer", f"cmp0{qb}", l))
                    g0 = branch_g[:, qb, :].rearrange("p (h b) -> p h b", b=3)[:, :, 0]
                    dve.tensor_tensor(o_b[:, qb, :].rearrange("p (h d) -> p h d", d=HD), O.ap[:, :].rearrange("p (h d) -> p h d", d=HD),
                                      over(g0, HD), ALU.mult).then_inc(O.free, 1)
                dve.wait_ge(O.free, O.nth("layer", "cmp01", l))

                def branch(i):
                    return lambda s: branch_g[:, s[2], :].rearrange("p (f a r b) -> p f a r b", f=2, a=2, b=3)[:, :, s[1], :, i]

                attention("layer", SEL_STEPS + WIN_STEPS, crossed(o_b), l, lambda s: branch(1 if s[0] == "sel" else 2)(s), end=rows.sem)
                attention("layer", MLA_STEPS, lambda s: o_c[:, s[2], s[1] * SEQ:(s[1] + 1) * SEQ].rearrange("p (i d) -> p i d", d=HD), l,
                          between={1: lambda: make_low("bra", rnd=l)})
                for name in "abc":
                    turned_low(f"o{name}", KF, o_low[name], o_high[name], l)
                make_low("brb", rnd=l)

                for j, name in enumerate("abc"):
                    for half in range(2):
                        for tb, b in enumerate(banks_of("layer", f"br{name}{half}")):
                            m = merged[:, tb, half * HALF:(half + 1) * HALF]
                            g = gate_t[:, tb, j * D + half * HALF:j * D + (half + 1) * HALF]
                            dve.wait_ge(b.full, b.nth("layer", f"br{name}{half}", l))
                            dve.scalar_tensor_tensor(m if j == 0 else g, g, 1.0, b.ap[:, 0:HALF], ALU.add, ALU.mult).then_inc(b.free, 1)
                            if j:
                                dve.wait_ge(b.free, b.nth("layer", f"br{name}{half}", l))
                                ins = dve.tensor_tensor(m, m, g, ALU.add)
                                if (j, half, tb) != (2, 1, 1):
                                    st.done(ins)
                    if j == 1:
                        st.settle()
                    if j == 0:
                        make_low("brc", rnd=l)
                        rms_rows("layer", "mem", D, RMS_EPS, lambda tb: mem_rows[:, tb, :], lambda tb: mem_rows[:, tb, :], l).then_inc(rows.sem, 1)
                    if j == 1:
                        turned_low("mem", KD, mem_low, mem_high, l, g_col[:, G_MEM:])
                        make_low("memk", rnd=l)
                ins.then_inc(rows.sem, 1)
                make_low("out0", rnd=l)
                turned_low("mg", KD, h_low, mg_high, l)
                make_low("out1", rnd=l)

                for i in range(2):
                    for tb, b in enumerate(banks_of("layer", f"out{i}")):
                        x = x_rows[:, tb, i * HALF:(i + 1) * HALF]
                        dve.wait_ge(b.full, b.nth("layer", f"out{i}", l))
                        dve.scalar_tensor_tensor(x, b.ap[:, 0:HALF], 0.5, x, ALU.mult, ALU.add).then_inc(b.free, 1)
                    if i == 0:
                        make_low("memv", rnd=l)
                rms_rows("layer", "xattn", D, RMS_EPS, lambda tb: x_rows[:, tb, :], lambda tb: h_rows[:, tb, :], l).then_inc(rows.sem, 1)
                make_low("xq", rnd=l)
                turned_low("hx", KD, h_low, hx_high, l, g_col[:, G_XATTN:])
                make_low("xo", rnd=l)
                attention("layer", X_STEPS, lambda s: o_a[:, s[2], :].rearrange("p (i d) -> p i d", d=XD), l, None, XD)
                make_low("gu0", rnd=l)
                turned_low("ox", KF, o_low["x"], o_high["x"], l)
                for half in range(2):
                    for tb, b in enumerate(banks_of("layer", f"xo{half}")):
                        x = x_rows[:, tb, half * HALF:(half + 1) * HALF]
                        dve.wait_ge(b.full, b.nth("layer", f"xo{half}", l))
                        dve.tensor_tensor(x, b.ap[:, 0:HALF], x, ALU.add).then_inc(b.free, 1)

                rms_rows("layer", "ffn", D, RMS_EPS, lambda tb: x_rows[:, tb, :], lambda tb: h_rows[:, tb, :], l).then_inc(rows.sem, 1)
                make_low("gu1", rnd=l)
                turned_low("hf", KD, h_low, hf_high, l, g_col[:, G_FFN:])

                def hidden_low(c):
                    v = ff_t[:, 2 * c:2 * c + 2, :]
                    dve.wait_ge(ff_high_ready, l * (KFF // 2) + c + 1)
                    dve.tensor_tensor(ff_low[:, 2 * c:2 * c + 2, :], v, ff_high[:, 2 * c:2 * c + 2, :].bitcast(F32), ALU.subtract).then_inc(ff_low_ready, 1)

                for c in range(KFF // 2):
                    dve.wait_ge(gate_tanhed, l * (KFF // 2) + c + 1)
                    dve.scalar_tensor_tensor(ff_tmp[:, 2 + c % 2, :], ff_tmp[:, c % 2, :], 1.0, G0.ap[:, :], ALU.add, ALU.mult).then_inc(G0.free, 1)
                    dve.wait_ge(G1.full, G1.nth("layer", f"gu{c}", l))
                    dve.wait_ge(G0.free, G0.nth("layer", f"gu{c}", l))
                    dve.tensor_tensor(ff_t[:, 2 * c:2 * c + 2, :].rearrange("p k n -> p (k n)"), ff_tmp[:, 2 + c % 2, :], G1.ap[:, :], ALU.mult)\
                        .then_inc(G1.free, 1)
                    make_low(SPLIT[SPLIT.index(f"gu{c}") + 2], rnd=l)
                    if c:
                        hidden_low(c - 1)
                hidden_low(KFF // 2 - 1)
                for c in range(2, 6):
                    make_low(f"fd{c}", rnd=l)
                for tb, b in enumerate((S, PT)):
                    x = x_rows[:, tb, :]
                    dve.wait_ge(b.full, b.nth("layer", "ffd", l))
                    dve.scalar_tensor_tensor(x, b.ap[:, :], 0.5, x, ALU.mult, ALU.add).then_inc(b.free, 1)
                dve.sem_inc(last_used, 1)
                for b in (S, PT):
                    dve.wait_ge(b.free, b.nth("layer", "ffd", l))
                dve.sem_inc(x_ready.sem, 1)
                st.settle()
            st.end(LAYERS)

            rms_rows("last", "out", D, RMS_EPS, lambda tb: x_rows[:, tb, :], lambda tb: h_rows[:, tb, :]).then_inc(last_rows, 1)
            dve.wait_ge(last_rows, 1)
            dve.wait_ge(in_ln, 16 * 5)
            dve.tensor_tensor(h_rows[:, :, :], h_rows[:, :, :], across(x_gain, TB), ALU.mult).then_inc(out_ready, 1)


_INS = [
    "x", "c", "w_mod", "b_mod", "w_in", "conv_w", "conv_b", "dt_bias", "a_log", "d_skip", "ssd_norm_w", "forget_b",
    "w_ssd_o", "w_att_o", "w_o", "ln1_g", "ln1_b", "w_router_group", "b_router_group", "w_router_expert",
    "b_router_expert", "w_gate", "w_up", "w_down", "ln2_g", "ln2_b", "mem_2", "positions_2", "norm_mix_2", "w_in_2",
    "swa_sinks_2", "nsa_pe_k_2", "nsa_pe_v_2", "nsa_wk1_2", "nsa_wk2_2", "nsa_wv1_2", "nsa_wv2_2",
    "mla_q_norm_2", "mla_w_q_b_2", "mla_kv_norm_2", "mla_w_kv_b_2", "w_br_a_2", "w_br_b_2", "w_br_c_2",
    "w_out_2", "norm_xattn_2", "norm_mem_2", "w_xq_2", "w_xkv_2", "w_xo_2", "norm_ffn_2", "w_gate_up_2",
    "w_down_2", "norm_final_2",
]


def kernel(**inputs):
    import numpy as _np
    import concourse.bacc as _bacc
    from concourse import mybir as _mybir
    from concourse.bass_utils import run_bass_kernel_spmd as _run

    nc = _bacc.Bacc("TRN2", target_bir_lowering=False, num_devices=1)
    arrays, views = {}, {}
    for name in _INS:
        a = _np.ascontiguousarray(inputs[name])
        arrays[f"in_{name}_dram"] = a
        views[name] = nc.dram_tensor(f"in_{name}_dram", a.shape, _mybir.dt.from_np(a.dtype), kind="ExternalInput").ap()
    out = nc.dram_tensor("out_0_dram", (1, SEQ, D), F32, kind="ExternalOutput").ap()
    two_blocks(nc, views, out)
    r = _run(nc, [arrays], core_ids=[0])
    return r.results[0]["out_0_dram"]
```
